# Optimizing a Trainium2 kernel written in Bass

```python
import math
import jax, jax.numpy as jnp
from jax import lax
import numpy as np

D_MODEL = 1024
BATCH = 1
SEQ = 1024
DEPTH = 2
DEC_BATCH = 8
DEC_SEQ = 8
PAST_LEN = 8192
PAGE_SIZE = 128

N_MIXERS = 2
N_MLSTM = (DEPTH + 1) // 2
N_CONV = DEPTH // 2
MLSTM_HEADS = 4
MLSTM_DK = D_MODEL // MLSTM_HEADS
MLSTM_DV = D_MODEL // MLSTM_HEADS
MLSTM_QK = MLSTM_HEADS * MLSTM_DK
MLSTM_V = MLSTM_HEADS * MLSTM_DV
MLSTM_CHUNK = 128
CONV_W = 3
D_FF = -(-8 * D_MODEL // (3 * 256)) * 256
EPS = 1e-6

kernel_name = "mlstm_shortconv_hybrid_step"

def rmsnorm(x, g):
    x32 = x.astype(jnp.float32)
    y = x32 * lax.rsqrt(jnp.mean(x32 * x32, axis=-1, keepdims=True) + EPS) * g.astype(jnp.float32)
    return y.astype(x.dtype)

def swiglu(xn, w_gu, w_down):
    gu = jnp.einsum('bsd,df->bsf', xn, w_gu)
    g, u = jnp.split(gu, 2, axis=-1)
    return jnp.einsum('bsf,fd->bsd', jax.nn.silu(g) * u, w_down)

def mlstm_scan(q, k, v, li, lf, C0, n0, m0):
    B, S, H, DK = q.shape
    DV = v.shape[-1]
    L = math.gcd(S, MLSTM_CHUNK)
    NC = S // L

    def blocks(a):
        a = a.reshape((B, NC, L) + a.shape[2:])
        return jnp.swapaxes(jnp.moveaxis(a, 1, 0), 2, 3)

    causal = jnp.tril(jnp.ones((L, L), dtype=bool))

    def step(carry, xs):
        C, n, m = carry
        qc, kc, vc, lic, lfc = xs
        b = jnp.cumsum(lfc, axis=-1)
        Dm = jnp.where(causal, b[..., :, None] - b[..., None, :] + lic[..., None, :], -jnp.inf)
        inter = b + m[..., None]
        m_eff = jnp.maximum(inter, jnp.max(Dm, axis=-1))
        w_inter = jnp.exp(inter - m_eff)
        s = jnp.einsum('bhld,bhsd->bhls', qc, kc) * jnp.exp(Dm - m_eff[..., None])
        num = w_inter[..., None] * jnp.einsum('bhvd,bhld->bhlv', C, qc) + jnp.einsum('bhls,bhsv->bhlv', s, vc)
        den = w_inter * jnp.einsum('bhd,bhld->bhl', n, qc) + jnp.sum(s, axis=-1)
        h = num / jnp.maximum(jnp.abs(den), jnp.exp(-m_eff))[..., None]
        bL = b[..., -1]
        g = bL[..., None] - b + lic
        m_new = jnp.maximum(bL + m, jnp.max(g, axis=-1))
        a = jnp.exp(bL + m - m_new)
        wg = jnp.exp(g - m_new[..., None])
        C_new = a[..., None, None] * C + jnp.einsum('bhl,bhlv,bhld->bhvd', wg, vc, kc)
        n_new = a[..., None] * n + jnp.einsum('bhl,bhld->bhd', wg, kc)
        return (C_new, n_new, m_new), h

    (C, n, m), h = lax.scan(step, (C0, n0, m0), (blocks(q), blocks(k), blocks(v), blocks(li), blocks(lf)))
    h = jnp.moveaxis(jnp.swapaxes(h, 2, 3), 0, 1).reshape(B, S, H, DV)
    return h, C, n, m

def mlstm_mixer(xn, w_in, b_gate, g_head, w_out, C0, n0, m0):
    B, S, _ = xn.shape
    f32 = jnp.float32
    proj = jnp.einsum('bsd,de->bse', xn, w_in).astype(f32)
    q = proj[..., :MLSTM_QK].reshape(B, S, MLSTM_HEADS, MLSTM_DK) * (MLSTM_DK ** -0.5)
    k = proj[..., MLSTM_QK:2 * MLSTM_QK].reshape(B, S, MLSTM_HEADS, MLSTM_DK)
    v = proj[..., 2 * MLSTM_QK:2 * MLSTM_QK + MLSTM_V].reshape(B, S, MLSTM_HEADS, MLSTM_DV)
    o = proj[..., 2 * MLSTM_QK + MLSTM_V:2 * MLSTM_QK + 2 * MLSTM_V]
    gates = proj[..., 2 * MLSTM_QK + 2 * MLSTM_V:] + b_gate.astype(f32)
    li = gates[..., :MLSTM_HEADS]
    lf = jax.nn.log_sigmoid(gates[..., MLSTM_HEADS:])
    h, C, n, m = mlstm_scan(q, k, v, li, lf, C0.astype(f32), n0.astype(f32), m0.astype(f32))
    h = h * lax.rsqrt(jnp.mean(h * h, axis=-1, keepdims=True) + EPS)
    h = h.reshape(B, S, MLSTM_V) * g_head.astype(f32) * jax.nn.sigmoid(o)
    y = jnp.einsum('bse,ed->bsd', h.astype(xn.dtype), w_out)
    return y, C, n, m

def conv_mixer(xn, w_in, w_taps, w_out, buf):
    S = xn.shape[1]
    proj = jnp.einsum('bsd,de->bse', xn, w_in)
    bg, cg, u = jnp.split(proj, 3, axis=-1)
    u = cg * u
    u_pad = jnp.concatenate([buf.astype(u.dtype), u], axis=1)
    conv = w_taps[0] * u_pad[:, 0:S]
    for j in range(1, CONV_W):
        conv = conv + w_taps[j] * u_pad[:, j:j + S]
    y = jnp.einsum('bsd,de->bse', bg * conv, w_out)
    return y, u_pad[:, -(CONV_W - 1):]

def trunk(x, st_C, st_n, st_m, st_conv, norm_mix, norm_ffn, norm_final, w_mlstm_in, b_mlstm_gate,
          mlstm_head_norm, w_mlstm_out, w_conv_in, w_conv_taps, w_conv_out, w_ffn_gate_up, w_ffn_down):
    Cs, ns, ms, bufs = [], [], [], []
    for layer in range(DEPTH):
        j = layer // N_MIXERS
        xn = rmsnorm(x, norm_mix[layer])
        if layer % N_MIXERS == 0:
            y, C, n, m = mlstm_mixer(xn, w_mlstm_in[j], b_mlstm_gate[j], mlstm_head_norm[j], w_mlstm_out[j],
                                     st_C[j], st_n[j], st_m[j])
            Cs.append(C); ns.append(n); ms.append(m)
        else:
            y, b = conv_mixer(xn, w_conv_in[j], w_conv_taps[j], w_conv_out[j], st_conv[j])
            bufs.append(b)
        x = x + y
        x = x + swiglu(rmsnorm(x, norm_ffn[layer]), w_ffn_gate_up[layer], w_ffn_down[layer])
    return rmsnorm(x, norm_final), jnp.stack(Cs), jnp.stack(ns), jnp.stack(ms), jnp.stack(bufs)

def setup_inputs(seed: int = 0) -> dict:
    key = jax.random.key(seed)
    ks = jax.random.split(key, 20)
    nrm = jax.random.normal
    H = MLSTM_HEADS
    d_in = 2 * MLSTM_QK + 2 * MLSTM_V + 2 * H
    b_gate = jnp.concatenate([
        -1.0 + 0.1 * nrm(ks[10], (N_MLSTM, H)),
        3.0 + 3.0 * jax.random.uniform(ks[11], (N_MLSTM, H))], axis=-1)
    return {
        "x_prompt": nrm(ks[0], (BATCH, SEQ, D_MODEL)),
        "x_sample": nrm(ks[1], (DEC_BATCH, DEC_SEQ, D_MODEL)),
        "state_mlstm_C": 0.1 * nrm(ks[2], (N_MLSTM, DEC_BATCH, H, MLSTM_DV, MLSTM_DK)),
        "state_mlstm_n": nrm(ks[3], (N_MLSTM, DEC_BATCH, H, MLSTM_DK)),
        "state_mlstm_m": nrm(ks[4], (N_MLSTM, DEC_BATCH, H)),
        "state_conv": nrm(ks[5], (N_CONV, DEC_BATCH, CONV_W - 1, D_MODEL)),
        "norm_mix": 1.0 + 0.05 * nrm(ks[6], (DEPTH, D_MODEL)),
        "norm_ffn": 1.0 + 0.05 * nrm(ks[7], (DEPTH, D_MODEL)),
        "norm_final": 1.0 + 0.05 * nrm(ks[8], (D_MODEL,)),
        "w_mlstm_in": nrm(ks[9], (N_MLSTM, D_MODEL, d_in)) * D_MODEL ** -0.5,
        "b_mlstm_gate": b_gate,
        "mlstm_head_norm": 1.0 + 0.05 * nrm(ks[12], (N_MLSTM, MLSTM_V)),
        "w_mlstm_out": nrm(ks[13], (N_MLSTM, MLSTM_V, D_MODEL)) * MLSTM_V ** -0.5,
        "w_conv_in": nrm(ks[14], (N_CONV, D_MODEL, 3 * D_MODEL)) * D_MODEL ** -0.5,
        "w_conv_taps": nrm(ks[15], (N_CONV, CONV_W, D_MODEL)) * CONV_W ** -0.5,
        "w_conv_out": nrm(ks[16], (N_CONV, D_MODEL, D_MODEL)) * D_MODEL ** -0.5,
        "w_ffn_gate_up": nrm(ks[17], (DEPTH, D_MODEL, 2 * D_FF)) * D_MODEL ** -0.5,
        "w_ffn_down": nrm(ks[18], (DEPTH, D_FF, D_MODEL)) * D_FF ** -0.5,
    }

def reference(x_prompt, x_sample, state_mlstm_C, state_mlstm_n, state_mlstm_m, state_conv,
              norm_mix, norm_ffn, norm_final, w_mlstm_in, b_mlstm_gate, mlstm_head_norm, w_mlstm_out,
              w_conv_in, w_conv_taps, w_conv_out, w_ffn_gate_up, w_ffn_down):
    Bp = x_prompt.shape[0]
    f32 = jnp.float32
    zC = jnp.zeros((N_MLSTM, Bp, MLSTM_HEADS, MLSTM_DV, MLSTM_DK), f32)
    zn = jnp.zeros((N_MLSTM, Bp, MLSTM_HEADS, MLSTM_DK), f32)
    zm = jnp.zeros((N_MLSTM, Bp, MLSTM_HEADS), f32)
    zconv = jnp.zeros((N_CONV, Bp, CONV_W - 1, D_MODEL), x_prompt.dtype)
    y_prompt, C_p, n_p, m_p, conv_p = trunk(
        x_prompt, zC, zn, zm, zconv, norm_mix, norm_ffn, norm_final, w_mlstm_in, b_mlstm_gate,
        mlstm_head_norm, w_mlstm_out, w_conv_in, w_conv_taps, w_conv_out, w_ffn_gate_up, w_ffn_down)
    y_sample, C_s, n_s, m_s, conv_s = trunk(
        x_sample, state_mlstm_C, state_mlstm_n, state_mlstm_m, state_conv, norm_mix, norm_ffn, norm_final,
        w_mlstm_in, b_mlstm_gate, mlstm_head_norm, w_mlstm_out, w_conv_in, w_conv_taps, w_conv_out,
        w_ffn_gate_up, w_ffn_down)
    return (y_prompt, y_sample, C_p, n_p, m_p, conv_p, C_s, n_s, m_s, conv_s)


_drawn_inputs = setup_inputs


def setup_inputs(seed=0):
    import zlib

    import numpy as np

    out = dict(_drawn_inputs(seed))
    spreads = {}
    factors = {}
    for name, (base, spread) in spreads.items():
        noise = np.random.default_rng([zlib.crc32(name.encode()), seed]).standard_normal(out[name].shape)
        drawn = base * np.exp(spread * noise) if base else spread * noise
        out[name] = __import__('jax').numpy.asarray(drawn.astype(out[name].dtype))
    for name, factor in factors.items():
        out[name] = (out[name] * factor).astype(out[name].dtype)
    return out
```

```python
from contextlib import ExitStack

import concourse.bass as bass
from concourse import mybir

F32 = mybir.dt.float32
F32R = mybir.dt.float32r
BF16 = mybir.dt.bfloat16
ALU = mybir.AluOpType
ACT = mybir.ActivationFunctionType
AX = mybir.AxisListType

P = 128
EPS = 1e-6
BIG = 3.0e38
NEG = -1.0e30


class At:

    def __init__(self, u, t, i=0, du=0, dt=0):
        self.u, self.t, self.i, self.du, self.dt = u, t, i, du, dt

    def after(self, units, tiles):
        return At(self.u + units, self.t + tiles, self.i, self.du, self.dt)

    def slot(self):
        return self.u % 2

    def units(self, more):
        return self.i * self.du + (self.u + more)

    def loads(self):
        return self.i * (8 * self.du) + 16 * ((self.u + 1) // 2)

    def slices(self, more):
        return self.i * (3 * self.dt) + (3 * self.t + more)


class Semaphores:

    def __init__(self, sem):
        self.mask_ready = sem("mask_ready")
        self.const_ready = sem("const_ready")
        self.vec_ld = sem("vec_ld")
        self.vecT_full = sem("vecT_full")
        self.vec_ready = sem("vec_ready")
        self.x_ld = sem("x_ld")
        self.xt_full = sem("xt_full")
        self.xt_free = sem("xt_free")
        self.gate_zero = sem("gate_zero")
        self.gate_ld = sem("gate_ld")
        self.w_hi = sem("w_hi")
        self.w_lo = sem("w_lo")
        self.acc_full = sem("acc_full")
        self.acc_free = sem("acc_free")
        self.xh_ready = sem("xh_ready")
        self.x_ready = sem("x_ready")
        self.sq_ready = sem("sq_ready")
        self.ssq_ready = sem("ssq_ready")
        self.st_full = sem("st_full")
        self.v9_ready = sem("v9_ready")
        self.rcol_ready = sem("rcol_ready")
        self.rb_full = sem("rb_full")
        self.rb_free = sem("rb_free")
        self.row_link = sem("row_link")
        self.row_full = sem("row_full")
        self.row_act = sem("row_act")
        self.row_ready = sem("row_ready")
        self.rowT_full = sem("rowT_full")
        self.cols_ready = sem("cols_ready")
        self.so_ready = sem("so_ready")
        self.cur_ready = sem("cur_ready")
        self.db_full = sem("db_full")
        self.dx_ready = sem("dx_ready")
        self.qk_full = sem("qk_full")
        self.sd_ready = sem("sd_ready")
        self.kvp_full = sem("kvp_full")
        self.kv_ready = sem("kv_ready")
        self.wgv_ready = sem("wgv_ready")
        self.in_full = sem("in_full")
        self.t1_ready = sem("t1_ready")
        self.ia_full = sem("ia_full")
        self.num_ready = sem("num_ready")
        self.up_full = sem("up_full")
        self.ct_ready = sem("ct_ready")
        self.wgm_ready = sem("wgm_ready")
        self.wgvb_ready = sem("wgvb_ready")
        self.tr_full = sem("tr_full")
        self.ct0_ready = sem("ct0_ready")
        self.iv_full = sem("iv_full")
        self.iv_free = sem("iv_free")
        self.upb_full = sem("upb_full")
        self.cb_ready = sem("cb_ready")
        self.ss_ready = sem("ss_ready")
        self.ms_ready = sem("ms_ready")
        self.rs0_ready = sem("rs0_ready")
        self.rs_ready = sem("rs_ready")
        self.hn_ready = sem("hn_ready")
        self.ht_full = sem("ht_full")
        self.ho_ready = sem("ho_ready")
        self.hg_ready = sem("hg_ready")
        self.hhm_ready = sem("hhm_ready")
        self.hlm_ready = sem("hlm_ready")
        self.den_link = sem("den_link")
        self.smp_link = sem("smp_link")
        self.ot_full = sem("ot_full")
        self.cp_ready = sem("cp_ready")
        self.cp_st = sem("cp_st")
        self.sg_ready = sem("sg_ready")
        self.g2_ready = sem("g2_ready")
        self.g3_ready = sem("g3_ready")
        self.hh_ready = sem("hh_ready")
        self.hl_ready = sem("hl_ready")
        self.chh_ready = sem("chh_ready")
        self.chl_ready = sem("chl_ready")
        self.cv_link = sem("cv_link")
        self.m_ld = sem("m_ld")
        self.m_st = sem("m_st")
        self.fin_full = sem("fin_full")
        self.ya_ready = sem("ya_ready")
        self.yd_ready = sem("yd_ready")
        self.y_st = sem("y_st")
        self.so_full = sem("so_full")
        self.so_evict = sem("so_evict")
        self.so_st = sem("so_st")
        self.cs_ld = sem("cs_ld")
        self.cs_full = sem("cs_full")
        self.cs_ready = sem("cs_ready")


def build(nc, x_prompt, x_sample, state_C, state_n, state_m, state_conv, norm_mix, norm_ffn, norm_final,
          w_mlstm_in, b_gate, head_norm, w_mlstm_out, w_conv_in, w_conv_taps, w_conv_out, w_gate_up, w_down,
          y_prompt, y_sample, C_prompt, n_prompt, m_prompt, conv_prompt, C_sample, n_sample, m_sample, conv_sample):
    D = x_prompt.shape[2]
    SEQ = x_prompt.shape[1]
    DB, DS = x_sample.shape[0], x_sample.shape[1]
    H = state_C.shape[2]
    DK = state_C.shape[4]
    F = w_down.shape[1]
    KD = D // P
    TS = DB * DS
    T = SEQ + TS
    NC = SEQ // P
    NT = NC + 1
    SL = [(0, 384), (384, 384), (768, T - 768)]
    FB = F // 256
    CB = D // 256
    assert D == 1024 and SEQ == 1024 and TS == 64 and H == 4 and DK == 256 and KD == 8 and F % 256 == 0

    def tok(c):
        return slice(c * P, min((c + 1) * P, T))

    def ntok(c):
        return min(P, T - c * P)

    G_AT = At(0, 0)
    M_AT = G_AT.after(1, 1)
    F0_AT = M_AT.after(H * 10, H * 16)
    C_AT = F0_AT.after(FB * 6, FB * 12)
    F1_AT = C_AT.after(CB * 8, CB * 14)
    UNITS = F1_AT.u + FB * 6

    ctx = ExitStack()
    with ctx:
        def sb(name, shape, dt=F32, c=ctx):
            return c.enter_context(nc.sbuf_tensor(name, shape, dt))

        def sem(name):
            return ctx.enter_context(nc.semaphore(name))

        xT = sb("xT", [P, KD, T])
        xh = sb("xh", [P, KD, T], F32R)
        xl = sb("xl", [P, KD, T], F32R)
        stage = sb("stage", [P, 2, 1024])
        wh = sb("wh", [P, 2, 1024], F32R)
        wl = sb("wl", [P, 2, 1024], F32R)
        rb = sb("rb", [P, T])
        work = sb("work", [P, 8, T])
        workf = work[:, :, :].rearrange("p a t -> p (a t)")
        ssq, sqt = work[:, 6, :], work[:, 7, :]
        ident = sb("ident", [P, P])
        identb = sb("identb", [P, P], BF16)
        causal = sb("causal", [P, P], BF16)
        blockneg = sb("blockneg", [TS, TS], BF16)
        blocksel = sb("blocksel", [TS, DB])
        ones = sb("ones", [P, 1])
        halfneg = sb("halfneg", [P, NT])
        rcol = sb("rcol", [P, NT])
        v9 = sb("v9", [P, NT])
        NV = 9
        vecs = sb("vecs", [P, NV * KD])
        nT_all = sb("nT_all", [P, DB, H, 2])
        cols = sb("cols", [P, H, NT, 5])
        abc = sb("abc", [P, H, 2 * NC])
        ncol = sb("ncol", [P, H, 2])
        U_, W_, T_, G_, M_ = range(5)

        def gain(v, k):
            return vecs[:, v * KD + k:v * KD + k + 1]

        LAYER_GAIN = [0, 2, 1, 3, 4]

        with ExitStack() as c1:
            rows = sb("rows", [P, 8, T], F32, c1)
            sm = sb("sm", [4, 8, 2 * NC], F32, c1)
            bcol = sb("bcol", [P, 1], F32, c1)
        hh0 = sb("hh0", [P, 2, T], F32R)
        hl0 = sb("hl0", [P, 2, T], F32R)
        with ExitStack() as c2:
            CT = sb("CT", [P, 2, DK + 1], F32, c2)
            cring = sb("cring", [P, 2, 2, DK], F32, c2)
            ct0 = sb("ct0", [P, 2, DK], F32, c2)
            kvc = sb("kvc", [P, 2 * DK + 1], F32, c2)
            kvs = sb("kvs", [TS, 2 * DK + 1], F32, c2)
            wgv = sb("wgv", [P, DK + 1], F32, c2)
            wgvb = sb("wgvb", [TS, DK], F32, c2)
            dx = sb("dx", [P, P], F32, c2)
            t1 = sb("t1", [P, DK + 1], F32, c2)
            num = sb("num", [P, DK + 1], F32, c2)
            ivs = sb("ivs", [P, 2, TS], F32, c2)
            cc = sb("cc", [P, NT, 5], F32, c2)
            ca = sb("ca", [P, 2 * NC], F32, c2)
            cn = sb("cn", [P, 2, DB], F32, c2)
            cg = sb("cg", [P, 2], F32, c2)
            nn = sb("nn", [P, 2, DB], F32, c2)
            wgm = sb("wgm", [TS, DB], F32, c2)
            qd = sb("qd", [TS, DB], F32, c2)
            sc = sb("sc", [P, 8], F32, c2)
        with ExitStack() as c3:
            hh1 = sb("hh1", [P, 2, T], F32R, c3)
            hl1 = sb("hl1", [P, 2, T], F32R, c3)
        HH, HL = [hh0, hh1], [hl0, hl1]
        ub = workf[:, 3 * T:3 * T + SEQ + 2]
        us = workf[:, 4 * T:4 * T + DB * (DS + 2)].rearrange("p (b s) -> p b s", b=DB)
        cstT = workf[:, 4 * T + 128:4 * T + 256].rearrange("p (b r k) -> p b r k", b=DB, r=2)
        cso = workf[:, 4 * T + 256:4 * T + 384].rearrange("p (b r k) -> p b r k", b=DB, r=2)
        cpo = workf[:, 4 * T + 384:4 * T + 400].rearrange("p (r k) -> p r k", r=2)
        outv = workf[:, 4 * T + 512:4 * T + 512 + 4 * P].rearrange("p (a n) -> p a n", a=4)

        acc = ctx.enter_context(nc.psum_tensor("acc", [P, 6, 512], F32))
        pA = ctx.enter_context(nc.psum_tensor("pA", [P, 512], F32))
        pB = ctx.enter_context(nc.psum_tensor("pB", [P, 512], F32))

        s = Semaphores(sem)
        w_ld = [sem("w_ld0"), sem("w_ld1")]
        c_ld = [sem("c_ld0"), sem("c_ld1")]
        c_st = [sem("c_st0"), sem("c_st1")]


        w_in_v = w_mlstm_in[0].rearrange("(k p) n -> p k n", p=P)
        w_conv_v = w_conv_in[0].rearrange("(k p) n -> p k n", p=P)
        w_gu_v = [w_gate_up[l].rearrange("(k p) n -> p k n", p=P) for l in range(2)]
        stage_col = [stage[:, j, :].rearrange("p (k n) -> p k n", k=KD) for j in range(2)]
        stage_row = [stage[:, j, :].rearrange("p (k n) -> p k n", k=2) for j in range(2)]
        gate0 = 4 * D

        ffn_turns = FB - 1
        assert ffn_turns % 2 == 0
        FFN_DU, FFN_DT = 12, 24
        HEAD_DU, HEAD_DT = 10, 16

        def filler(at, before, c, p):
            if c < 4:
                if not before:
                    return None
                i = 12 * (c // 2) + 6 * (c % 2) + p
                return at.after(c // 2, i // 3), i // 3, i % 3, None
            if p % 2 == 0:
                return None
            i = 3 * (c % 2) + p // 2
            gate = at.after(2, 8) if before else at
            return gate.after((c - 4) // 2, (c - 4) // 2), None, i // 2, i % 2

        def filler_unit(at, before, c):
            f = None if c % 2 else filler(at, before, c, 1)
            return f and (f[0] if f[1] is None else at.after(c // 2, 2 * c))

        block = ctx.enter_context(nc.Block())

        @block.sync
        def _(sp):
            def load(at, src, row):
                if at.u >= 2:
                    sp.wait_ge(s.w_lo, at.units(-1))
                j = at.slot()
                sp.dma_start((stage_row if row else stage_col)[j], src).then_inc(w_ld[j], 16)

            def load_up(at, w, col):
                load(at, w[:, :, bass.ds(col, P)] if not isinstance(col, int) else w[:, :, col:col + P], False)

            def load_down(at, w, i):
                v = w.rearrange("(i k p) n -> p i k n", k=2, p=P)
                for half in range(2):
                    cs = slice(half * 512, (half + 1) * 512)
                    src = v[:, i, :, cs] if isinstance(i, int) else \
                        v[:, bass.ds(i, 1), :, cs].rearrange("p a k n -> p (a k) n")
                    load(at.after(half, 0), src, True)

            def load_up_head(at, h, first, last, hooks={}):
                for j in range(first, last):
                    if j in hooks:
                        hooks[j]()
                    load_up(at.after(j - first, 0), w_in_v, h * 256 + ((j // 2) * D + (j % 2) * P))

            def load_up_ffn(at, l, i):
                for j in range(4):
                    load_up(at.after(j, 0), w_gu_v[l], i * 256 + ((j % 2) * F + (j // 2) * P))

            def load_up_conv(at, i):
                for j in range(6):
                    which = [1, 2, 0][j % 3]
                    load_up(at.after(j, 0), w_conv_v, i * 256 + which * D + (j // 3) * P)

            def store_head(h):
                sp.wait_ge(s.cp_ready, h + 1)
                dst = C_prompt[0, 0].rearrange("h (t p) k -> p h t k", p=P)
                dst = dst[:, h] if isinstance(h, int) else dst[:, bass.ds(h, 1)].rearrange("p a t k -> p (a t) k")
                sp.dma_start(dst, ct0[:]).then_inc(s.cp_st, 16)

            for c in range(NC):
                sp.dma_start(workf[:, c * D:(c + 1) * D], x_prompt[0, c * P:(c + 1) * P, :]).then_inc(s.x_ld, 16)
            sp.dma_start(rb[0:TS, 0:D], x_sample.rearrange("b s d -> (b s) d")).then_inc(s.x_ld, 16)
            sp.wait_ge(s.gate_zero, 1)
            with nc.allow_non_contiguous_dma(reason="eight columns"):
                sp.dma_start(stage_col[0][:, :, 0:H], w_in_v[:, :, gate0:gate0 + H]).then_inc(s.gate_ld, 16)
                sp.dma_start(stage_col[0][:, :, 32:32 + H], w_in_v[:, :, gate0 + H:gate0 + 2 * H]).then_inc(s.gate_ld, 16)
            load_up_head(M_AT, 0, 0, 8)
            with sp.Fori(0, H - 1) as h:
                at = At(M_AT.u + 8, 0, h, HEAD_DU, HEAD_DT)
                load_up_head(at, h + 1, 0, 6, {4: lambda: store_head(h)})
                load_down(at.after(6, 0), w_mlstm_out[0], h)
                load_up_head(at.after(8, 0), h + 1, 6, 8)
            load_down(At(M_AT.u + 38, 0), w_mlstm_out[0], H - 1)
            store_head(H - 1)

            def load_ffn(base, l):
                load_up_ffn(base, l, 0)
                with sp.Fori(0, ffn_turns // 2) as i:
                    at = At(base.u + 4, 0, i, FFN_DU, FFN_DT)
                    for e in range(2):
                        load_up_ffn(at.after(6 * e, 0), l, i * 2 + (1 + e))
                        load_down(at.after(6 * e + 4, 0), w_down[l], i * 2 + e)
                load_down(base.after(6 * FB - 2, 0), w_down[l], FB - 1)

            load_ffn(F0_AT, 0)
            load_up_conv(C_AT, 0)
            for i in range(CB):
                if i + 1 < CB:
                    load_up_conv(C_AT.after(6 + 8 * i, 0), i + 1)
                load_down(C_AT.after(8 * i + 12 if i + 1 < CB else 8 * CB - 2, 0), w_conv_out[0], i)
            load_ffn(F1_AT, 1)

            for c in range(NT):
                sp.wait_ge(s.yd_ready if c % 2 else s.ya_ready, c // 2 + 1)
                if c < NC:
                    sp.dma_start(y_prompt[0, c * P:(c + 1) * P, :], workf[:, c * D:(c + 1) * D]).then_inc(s.y_st, 16)
                else:
                    sp.dma_start(y_sample.rearrange("b s d -> (b s) d"), rb[0:TS, 0:D]).then_inc(s.y_st, 16)
            sp.wait_ge(s.y_st, 16 * NT)
            sp.wait_ge(s.cp_st, 16 * H)

        @block.gpsimd
        def _(pool):
            g = nc.gpsimd
            g.memset(ident[:], 0.0).then_inc(s.mask_ready, 1)
            g.memset(identb[:], 0.0).then_inc(s.mask_ready, 1)
            g.memset(causal[:], 0.0).then_inc(s.mask_ready, 1)
            g.memset(blockneg[:], 0.0).then_inc(s.mask_ready, 1)
            g.memset(blocksel[:], 1.0).then_inc(s.mask_ready, 1)
            g.memset(ones[:], 1.0).then_inc(s.mask_ready, 1)
            g.memset(halfneg[:], -0.5).then_inc(s.mask_ready, 1)
            pool.wait_ge(s.mask_ready, 7)
            for m in (ident, identb):
                g.affine_select(out=m[:], in_=m[:], compare_op=ALU.not_equal, fill=1.0, base=0,
                                pattern=[[-1, P]], channel_multiplier=1).then_inc(s.mask_ready, 1)
            g.affine_select(out=causal[:], in_=causal[:], compare_op=ALU.is_ge, fill=NEG, base=0,
                            pattern=[[1, P]], channel_multiplier=-1).then_inc(s.mask_ready, 1)
            g.affine_select(out=blockneg[:], in_=blockneg[:], compare_op=ALU.is_ge, fill=NEG, base=0,
                            pattern=[[1, TS]], channel_multiplier=-1).then_inc(s.mask_ready, 1)
            bn = blockneg[:, :].rearrange("p (b s) -> p b s", b=DB)
            pool.wait_ge(s.mask_ready, 11)
            g.affine_select(out=bn, in_=bn, compare_op=ALU.is_ge, fill=NEG, base=0,
                            pattern=[[-DS, DB], [0, DS]], channel_multiplier=1).then_inc(s.mask_ready, 1)
            g.affine_select(out=blocksel[:], in_=blocksel[:], compare_op=ALU.is_ge, fill=0.0, base=0,
                            pattern=[[-DS, DB]], channel_multiplier=1).then_inc(s.mask_ready, 1)
            pool.wait_ge(s.mask_ready, 13)
            g.affine_select(out=bn, in_=bn, compare_op=ALU.is_ge, fill=NEG, base=DS - 1,
                            pattern=[[DS, DB], [0, DS]], channel_multiplier=-1).then_inc(s.mask_ready, 1)
            g.affine_select(out=blocksel[:], in_=blocksel[:], compare_op=ALU.is_ge, fill=0.0, base=DS - 1,
                            pattern=[[DS, DB]], channel_multiplier=-1).then_inc(s.mask_ready, 1)
            pool.wait_ge(s.mask_ready, 15)
            g.memset(v9[:], 1.0).then_inc(s.const_ready, 1)

            def rstd(L):
                pool.wait_ge(s.v9_ready, 2 * (L + 1))
                g.tensor_tensor(rcol[:], v9[:], halfneg[:], ALU.pow).then_inc(s.rcol_ready, 1)

            def head(v, h):
                return v[:, h] if isinstance(h, int) else v[:, bass.ds(h, 1)].rearrange("p a t k -> p (a t) k")

            def c_load(h, b):
                pool.dma_start(cring[:, b % 2], head(state_C[0, b].rearrange("h (t p) k -> p h t k", p=P), h)).then_inc(c_ld[b % 2], 16)

            def c_store(h, b):
                pool.dma_start(head(C_sample[0, b].rearrange("h (t p) k -> p h t k", p=P), h), cring[:, b % 2]).then_inc(c_st[b % 2], 16)

            def mix(h, last):
                for c in range(NT):
                    n = ntok(c)
                    pool.wait_ge(s.ms_ready, h * NT + (c + 1))
                    if c < NC:
                        pool.wait_ge(s.cb_ready, h * NC + (c + 1))
                    if 1 <= c < NC - 1:
                        pool.wait_ge(c_st[(c + 1) % 2], h * 64 + 16 * ((c + 1) // 2))
                    if c == NC and not last:
                        for b in range(2):
                            pool.wait_ge(c_st[b], h * 64 + 64)
                    g.tensor_tensor(sc[0:n, 4:5], sc[0:n, 3:4], halfneg[0:n, 0:1], ALU.pow).then_inc(s.rs0_ready, 1)
                    if c < NC:
                        c_store(h, c)
                    if 1 <= c < NC - 1:
                        c_load(h, c + 1)
                    if c == NC and not last:
                        for b in range(2):
                            c_load(h + 1, b)

            rstd(0)
            pool.wait_ge(s.cols_ready, 3)
            pool.wait_ge(s.m_st, 32)
            c_load(0, 0)
            c_load(0, 1)
            with pool.Fori(0, H - 1) as h:
                mix(h, False)
            mix(H - 1, True)
            for L in range(1, 4):
                rstd(L)
            for j in range(2):
                pool.wait_ge(c_st[j], 64 * H)
            pool.wait_ge(s.so_evict, 1)
            pool.dma_start(n_sample[0].rearrange("b h (t p) -> (b h t) p", p=P), outv[0:64, 0, :]).then_inc(s.so_st, 16)
            pool.wait_ge(s.so_evict, 2)
            pool.dma_start(n_prompt[0, 0].rearrange("h (t p) -> (h t) p", p=P), outv[0:8, 1, :]).then_inc(s.so_st, 16)
            pool.wait_ge(s.so_evict, 3)
            pool.dma_start(conv_sample[0].rearrange("b r (k p) -> (b r k) p", p=P), outv[:, 2, :]).then_inc(s.so_st, 16)
            pool.wait_ge(s.so_evict, 4)
            pool.dma_start(conv_prompt[0, 0].rearrange("r (k p) -> (r k) p", p=P), outv[0:16, 3, :]).then_inc(s.so_st, 16)
            rstd(4)
            pool.wait_ge(s.so_st, 64)

        @block.scalar
        def _(act):
            a = nc.scalar

            def convert(at):
                nx = at.after(1, 0)
                if nx.u >= UNITS:
                    return
                act.wait_ge(w_ld[nx.slot()], nx.loads())
                if nx.u >= 2:
                    act.wait_ge(s.acc_full, at.slices(0))
                a.activation(wh[:, nx.slot(), :], stage[:, nx.slot(), :], ACT.Copy).then_inc(s.w_hi, 1)

            def refresh(L, j):
                if 8 * L + j > 0:
                    act.wait_ge(s.ssq_ready, 8 * L + j)
                a.activation(sqt, xT[:, j, :], ACT.Square).then_inc(s.sq_ready, 1)
                if L < 4:
                    a.activation(xh[:, j, :], xT[:, j, :], ACT.Copy, scale=gain(LAYER_GAIN[L], j)).then_inc(s.xh_ready, 1)
                else:
                    act.wait_ge(s.sq_ready, 8 * L + j + 1)
                    a.activation(xT[:, j, :], xT[:, j, :], ACT.Copy, scale=gain(4, j)).then_inc(s.xh_ready, 1)

            def down(at, L=None):
                for half in range(2):
                    u = at.after(half, 4 * half)
                    convert(u)
                    if L is not None:
                        for j in range(4):
                            act.wait_ge(s.acc_free, u.slices(3 * (j + 1)))
                            refresh(L, 4 * half + j)

            for n, v in enumerate((norm_mix[0:1, :], norm_mix[1:2, :], norm_ffn[0:1, :], norm_ffn[1:2, :],
                                   norm_final.rearrange("(a d) -> a d", a=1), head_norm,
                                   w_conv_taps[0, 0:1, :], w_conv_taps[0, 1:2, :], w_conv_taps[0, 2:3, :])):
                act.dma_start(rows[n * KD:(n + 1) * KD, 7, 0:P], v.rearrange("a (k p) -> (a k) p", p=P)).then_inc(s.vec_ld, 16)
            act.dma_start(rows[0:64, 7, P:2 * P], state_n[0].rearrange("b h (t p) -> (b h t) p", p=P)).then_inc(s.vec_ld, 16)
            with nc.allow_non_contiguous_dma(reason="a few words"):
                act.dma_start(sm[0:H, 0, NC:2 * NC], state_m[0].rearrange("b h -> h b")).then_inc(s.m_ld, 16)
                act.dma_start(bcol[0:H, :], b_gate[0, 0:H].rearrange("(h a) -> h a", a=1)).then_inc(s.m_ld, 16)
                act.dma_start(bcol[32:32 + H, :], b_gate[0, H:2 * H].rearrange("(h a) -> h a", a=1)).then_inc(s.m_ld, 16)

            act.wait_ge(s.gate_ld, 32)
            a.activation(wh[:, 0, :], stage[:, 0, :], ACT.Copy).then_inc(s.w_hi, 1)
            act.wait_ge(s.vec_ready, 1)
            act.wait_ge(s.xt_free, NT)
            for j in range(KD):
                refresh(0, j)
            convert(G_AT)
            R = lambda k, p=0, n=H: rows[p:p + n, k, :]
            act.wait_ge(s.row_full, 1)
            a.activation(R(3), R(3), ACT.Exp, scale=-1.0).then_inc(s.row_act, 1)
            act.wait_ge(s.row_act, 1)
            a.activation(R(3), R(3), ACT.Ln, bias=1.0).then_inc(s.row_act, 1)

            def row_exps():
                act.wait_ge(s.row_full, 2)
                a.activation(R(7, 32), R(3), ACT.Exp).then_inc(s.row_act, 1)
                act.wait_ge(s.row_full, 3)
                a.activation(R(7, 64), R(0), ACT.Exp, scale=-1.0).then_inc(s.row_act, 1)
                act.wait_ge(s.row_full, 4)
                a.activation(R(7, 96), R(5), ACT.Exp).then_inc(s.row_act, 1)
                a.activation(sm[:, 6, :], sm[:, 5, :], ACT.Exp).then_inc(s.row_act, 1)
                act.wait_ge(s.row_ready, 1)
                with nc.allow_non_contiguous_dma(reason="a few words"):
                    act.dma_start(m_prompt[0].rearrange("b h -> h b"), sm[:, 7, NC - 1:NC]).then_inc(s.m_st, 16)
                    act.dma_start(m_sample[0].rearrange("b h -> h b"), sm[:, 7, NC:2 * NC]).then_inc(s.m_st, 16)
                act.wait_ge(s.m_st, 32)

            def up_head(at, hooks):
                for j in range(6):
                    convert(at.after(j, j))
                    if j in hooks:
                        hooks[j]()

            def mix(at, h, before):
                st = h * NT
                act.wait_ge(s.cur_ready, h + 1)

                def kv(c):
                    act.wait_ge(s.kvp_full, st + (c + 2))
                    if c >= 1:
                        act.wait_ge(s.up_full, h * NC + c)
                    if c < 0:
                        a.activation(kvs[:, 0:2 * DK], acc[0:TS, 4, :], ACT.Copy).then_inc(s.kv_ready, 1)
                    else:
                        a.activation(kvc[:, 0:2 * DK], acc[:, 4, :], ACT.Copy).then_inc(s.kv_ready, 1)

                def decay(c):
                    n = ntok(c)
                    act.wait_ge(s.db_full, st + (c + 1))
                    if c >= 1:
                        act.wait_ge(s.ia_full, st + c)
                    a.activation(dx[0:n, 0:n], acc[0:n, 3, 0:n], ACT.Exp, bias=cc[0:n, c, U_:U_ + 1]).then_inc(s.dx_ready, 1)

                kv(-1)
                decay(0)
                kv(0)
                for c in range(NT):
                    n = ntok(c)
                    act.wait_ge(s.in_full, st + (c + 1))
                    if c >= 1:
                        act.wait_ge(s.ss_ready, st + c)
                    w = DK + 1 if c < NC else DK
                    a.activation(t1[0:n, 0:w], acc[0:n, 0, 0:w], ACT.Copy, scale=cc[0:n, c, W_:W_ + 1]).then_inc(s.t1_ready, 1)
                    if c < NC:
                        act.wait_ge(s.wgm_ready, h + 1)
                        if c >= 1:
                            act.wait_ge(s.upb_full, h * NC + c)
                        a.activation(wgvb[:], kvs[:, DK:2 * DK], ACT.Copy, scale=wgm[:, c:c + 1]).then_inc(s.wgvb_ready, 1)
                        if filler_unit(at, before, c):
                            convert(filler_unit(at, before, c))
                        act.wait_ge(s.tr_full, h * NC + (c + 1))
                        if c >= 1:
                            act.wait_ge(s.iv_full, h * NC + c)
                        a.activation(ct0[:], pA[:, :].rearrange("p (a v) -> p a v", a=2), ACT.Copy).then_inc(s.ct0_ready, 1)
                        decay(c + 1)
                        if c + 1 < NC:
                            kv(c + 1)
                    act.wait_ge(s.num_ready, st + (c + 1))
                    a.activation(t1[0:n, 0:DK], num[0:n, 0:DK], ACT.Square, accum_out=sc[0:n, 0:1]).then_inc(s.ss_ready, 1)
                    act.wait_ge(s.rs_ready, st + (c + 1))
                    a.activation(num[0:n, 0:DK], num[0:n, 0:DK], ACT.Copy, scale=sc[0:n, 5:6]).then_inc(s.hn_ready, 1)

            def gate(at, h):
                act.wait_ge(s.acc_free, at.slices(0))
                for o, n in SL:
                    a.activation(work[:, 6:8, o:o + n], work[:, 6:8, o:o + n], ACT.Sigmoid).then_inc(s.so_ready, 1)
                for k, (o, n) in enumerate(SL):
                    act.wait_ge(s.hg_ready, h * 3 + (k + 1))
                    a.activation(hh0[:, :, o:o + n], work[:, 0:2, o:o + n], ACT.Copy).then_inc(s.hhm_ready, 1)

            def stored(h):
                act.wait_ge(s.cp_st, h * 16 + 16)

            up_head(M_AT, {4: row_exps})
            mix(M_AT.after(6, 6), 0, False)
            with act.Fori(0, H - 1) as h:
                at = At(M_AT.u + 8, M_AT.t + 8, h, HEAD_DU, HEAD_DT)
                up_head(at, {0: lambda: gate(at, h), 5: lambda: stored(h)})
                mix(at.after(6, 6), h + 1, True)
            gate(M_AT.after(38, 56), H - 1)
            down(M_AT.after(38, 56), 1)

            act.dma_start(workf[:, 5 * T:5 * T + P], state_conv[0].rearrange("b r (k p) -> (b r k) p", p=P)).then_inc(s.cs_ld, 16)

            def up_ffn(at, i, q):
                for t in range(2):
                    u = at.after(2 * t, 2 * t)
                    convert(u)
                    for k, (o, n) in enumerate(SL):
                        act.wait_ge(s.acc_free, u.slices(k + 1))
                        a.activation(work[:, 1, o:o + n], work[:, 0, o:o + n], ACT.Sigmoid).then_inc(s.sg_ready, 1)
                    u = at.after(2 * t + 1, 2 * t + 1)
                    convert(u)
                    for k, (o, n) in enumerate(SL):
                        act.wait_ge(s.acc_free, u.slices(k + 1))
                        a.activation(HH[i % 2][:, t, o:o + n], work[:, 3, o:o + n], ACT.Copy).then_inc(s.hh_ready, 1)

            def ffn(base, l, L):
                q = 6 * FB * l
                up_ffn(base, 0, q)
                with act.Fori(0, ffn_turns // 2) as i:
                    at = At(base.u + 4, base.t + 4, i, FFN_DU, FFN_DT)
                    for e in range(2):
                        up_ffn(at.after(6 * e, 12 * e), 1 + e, i * 12 + (q + 6 + 6 * e))
                        down(at.after(6 * e + 4, 12 * e + 4))
                down(base.after(6 * FB - 2, 12 * FB - 8), L)

            def up_conv(at, i):
                for t in range(2):
                    for j in range(3):
                        convert(at.after(3 * t + j, 3 * t + j))
                    u = at.after(3 * t + 2, 3 * t + 2)
                    for k, (o, n) in enumerate(SL):
                        act.wait_ge(s.acc_free, u.slices(k + 1))
                        a.activation(HH[i % 2][:, t, o:o + n], work[:, 2, o:o + n], ACT.Copy).then_inc(s.chh_ready, 1)

            for j in range(2):
                act.wait_ge(c_st[j], 64 * H)
            act.wait_ge(s.cp_st, 16 * H)
            ffn(F0_AT, 0, 2)
            up_conv(C_AT, 0)
            for i in range(CB):
                if i + 1 < CB:
                    up_conv(C_AT.after(6 + 8 * i, 6 + 14 * i), i + 1)
                    down(C_AT.after(12 + 8 * i, 12 + 14 * i))
                else:
                    down(C_AT.after(8 * CB - 2, 14 * CB - 8), 3)
            ffn(F1_AT, 1, 4)

            act.wait_ge(s.rcol_ready, 5)
            act.wait_ge(s.so_st, 64)
            for c in range(0, NT, 2):
                n = ntok(c)
                act.wait_ge(s.fin_full, c + 1)
                b = 2 * (c % 3)
                dst = workf[:, c * D:(c + 1) * D] if c < NC else rb[:, 0:D]
                a.activation(dst[0:n, :].rearrange("p (a n) -> p a n", a=2), acc[0:n, b:b + 2, :], ACT.Copy,
                             scale=rcol[0:n, c:c + 1]).then_inc(s.ya_ready, 1)

        @block.vector
        def _(dve):
            v = nc.vector

            def convert(at):
                nx = at.after(1, 0)
                if nx.u >= UNITS:
                    return
                dve.wait_ge(s.w_hi, nx.units(1))
                j = nx.slot()
                v.tensor_tensor(wl[:, j, :], stage[:, j, :], wh[:, j, :].bitcast(F32), ALU.subtract).then_inc(s.w_lo, 1)

            def refresh(L, j):
                dve.wait_ge(s.sq_ready, 8 * L + j + 1)
                if j == 0:
                    v.tensor_copy(ssq, sqt).then_inc(s.ssq_ready, 1)
                else:
                    dve.wait_ge(s.ssq_ready, 8 * L + j)
                    v.tensor_tensor(ssq, ssq, sqt, ALU.add).then_inc(s.ssq_ready, 1)
                if L < 4:
                    dve.wait_ge(s.xh_ready, 8 * L + j + 1)
                    v.scalar_tensor_tensor(out=xl[:, j, :], in0=xT[:, j, :], scalar=gain(LAYER_GAIN[L], j),
                                           in1=xh[:, j, :].bitcast(F32), op0=ALU.mult, op1=ALU.subtract).then_inc(s.x_ready, 1)

            def mean_square(L):
                dve.wait_ge(s.st_full, L + 1)
                v.tensor_scalar(v9[:, 0:NC], pA[:, 0:NC], 1.0 / D, EPS, ALU.mult, ALU.add).then_inc(s.v9_ready, 1)
                v.tensor_scalar(v9[0:TS, NC:NT], pA[0:TS, NC:NT], 1.0 / D, EPS, ALU.mult, ALU.add).then_inc(s.v9_ready, 1)

            def rms_rows(L):
                for n, (bank, o, w) in enumerate(((pA, 0, 512), (pB, 512, 512), (pA, 1024, TS))):
                    dve.wait_ge(s.rb_full, 3 * L + n + 1)
                    v.tensor_copy(rb[:, o:o + w], bank[:, 0:w]).then_inc(s.rb_free, 1)
                dve.wait_ge(s.rb_free, 3 * L + 3)

            def bank(at, k):
                return acc[:, 3 * (at.t % 2) + k, 0:SL[k][1]]

            def down(at, L=None):
                for half in range(2):
                    convert(at.after(half, 4 * half))
                    for jj in range(4):
                        j = 4 * half + jj
                        u = at.after(half, j)
                        for k, (o, n) in enumerate(SL):
                            dve.wait_ge(s.acc_full, u.slices(k + 1))
                            v.tensor_tensor(xT[:, j, o:o + n], xT[:, j, o:o + n], bank(u, k), ALU.add).then_inc(s.acc_free, 1)
                        if L is not None:
                            refresh(L, j)

            v.memset(stage[:, 0, :], 0.0).then_inc(s.gate_zero, 1)
            v.memset(cols[:], 0.0).then_inc(s.row_link, 1)
            dve.wait_ge(s.vecT_full, 1)
            v.tensor_copy(vecs[:], pA[:, 0:NV * KD])
            v.tensor_copy(nT_all[:, :, :, :].rearrange("p b h t -> p (b h t)"), pA[:, P:P + 64]).then_inc(s.vec_ready, 1)
            for c in range(NT):
                dve.wait_ge(s.xt_full, c + 1)
                b, n = 2 * (c % 3), ntok(c)
                src = acc[:, b:b + 2, :].rearrange("p a (k n) -> p (a k) n", n=P)[:, :, 0:n]
                v.tensor_copy(xT[:, :, tok(c)], src).then_inc(s.xt_free, 1)
            dve.wait_ge(s.w_hi, 1)
            v.tensor_tensor(wl[:, 0, :], stage[:, 0, :], wh[:, 0, :].bitcast(F32), ALU.subtract).then_inc(s.w_lo, 1)
            dve.wait_ge(s.xt_free, NT)
            dve.wait_ge(s.vec_ready, 1)
            for j in range(KD):
                refresh(0, j)
            convert(G_AT)
            mean_square(0)
            rms_rows(0)
            for k, (o, n) in enumerate(SL):
                dve.wait_ge(s.acc_full, k + 1)
                v.tensor_tensor(rows[0:36, 0, o:o + n], bank(G_AT, k)[0:36, :], rb[0:36, o:o + n], ALU.mult).then_inc(s.acc_free, 1)

            R = lambda k, p=0: rows[p:p + H, k, :]
            done = [1]

            def link(ins):
                done[0] += 1
                ins.then_inc(s.row_link, 1)
                dve.wait_ge(s.row_link, done[0])

            def starts(r):
                return (r[:, 0:SEQ].rearrange("p (c l) -> p c l", l=P)[:, :, 0:1].rearrange("p c l -> p (c l)"),
                        r[:, SEQ:T].rearrange("p (c l) -> p c l", l=DS)[:, :, 0:1].rearrange("p c l -> p (c l)"))

            def ends(r):
                return (r[:, 0:SEQ].rearrange("p (c l) -> p c l", l=P)[:, :, P - 1:P].rearrange("p c l -> p (c l)"),
                        r[:, SEQ:T].rearrange("p (c l) -> p c l", l=DS)[:, :, DS - 1:DS].rearrange("p c l -> p (c l)"))

            def chunks(r):
                return (r[:, 0:SEQ].rearrange("p (c l) -> p c l", l=P), r[:, SEQ:T].rearrange("p (c l) -> p c l", l=DS))

            def spread(m):
                return (m[:, 0:NC].rearrange("p (c l) -> p c l", l=1).to_broadcast([H, NC, P]),
                        m[:, NC:2 * NC].rearrange("p (c l) -> p c l", l=1).to_broadcast([H, DB, DS]))

            halves = (slice(0, NC), slice(NC, 2 * NC))
            M_IN, B_L, U_MAX, BU, M_L, M_DIFF, A_, M_OUT = range(8)

            def rows_gates():
                dve.wait_ge(s.m_ld, 48)
                dve.wait_ge(s.acc_free, 3)
                link(v.tensor_scalar(R(1), R(0), bcol[0:H, :], None, ALU.add))
                link(v.tensor_scalar(R(2), R(0, 32), bcol[32:32 + H, :], None, ALU.add))
                v.scalar_tensor_tensor(out=R(3), in0=R(2), scalar=-1.0, in1=R(2), op0=ALU.mult, op1=ALU.max).then_inc(s.row_full, 1)

            def rows_cumsum():
                dve.wait_ge(s.row_act, 2)
                link(v.tensor_scalar(R(2), R(2), 0.0, None, ALU.min))
                link(v.tensor_tensor(R(4), R(2), R(3), ALU.subtract))
                link(v.memset(R(0), 1.0))
                for part in starts(R(0)):
                    link(v.memset(part, 0.0))
                link(v.tensor_tensor_scan(R(2), R(0), R(4), 0.0, ALU.mult, ALU.add))
                link(v.memset(rows[:, 7, :], 0.0))
                link(v.tensor_tensor(R(7), R(1), R(2), ALU.subtract))

            def rows_starts():
                for part, src in zip(halves, ends(R(2))):
                    link(v.tensor_copy(sm[:, B_L, part], src))
                link(v.tensor_reduce(sm[:, U_MAX, 0:NC], chunks(R(7))[0], AX.X, ALU.max))
                link(v.tensor_tensor(sm[:, BU, 0:NC], sm[:, B_L, 0:NC], sm[:, U_MAX, 0:NC], ALU.add))
                link(v.memset(sm[:, M_IN, 0:1], 0.0))
                link(v.tensor_tensor_scan(sm[:, M_IN, 1:NC], sm[:, B_L, 0:NC - 1], sm[:, BU, 0:NC - 1], 0.0, ALU.add, ALU.max))

            def rows_max():
                link(v.tensor_copy(R(3), R(7)))
                for part, at in zip(halves, starts(R(3))):
                    link(v.tensor_tensor(at, at, sm[:, M_IN, part], ALU.max))
                link(v.memset(R(0), BIG))
                for part in starts(R(0)):
                    link(v.memset(part, -BIG))
                link(v.tensor_tensor_scan(R(1), R(0), R(3), 0.0, ALU.min, ALU.max))

            def rows_args():
                parts = list(zip(spread(sm[:, M_IN, :]), chunks(R(1)), chunks(R(3))))
                link(v.tensor_tensor(parts[0][2], parts[0][0], parts[0][1], ALU.subtract))
                v.tensor_tensor(parts[1][2], parts[1][0], parts[1][1], ALU.subtract).then_inc(s.row_full, 1)
                v.tensor_tensor(R(0), R(2), R(1), ALU.add).then_inc(s.row_full, 1)
                for part, src in zip(halves, ends(R(1))):
                    link(v.tensor_copy(sm[:, M_L, part], src))
                link(v.tensor_tensor(sm[:, M_DIFF, :], sm[:, M_IN, :], sm[:, M_L, :], ALU.subtract))
                parts = list(zip(chunks(R(7)), spread(sm[:, M_L, :]), chunks(R(5))))
                link(v.tensor_tensor(parts[0][2], parts[0][0], parts[0][1], ALU.subtract))
                v.tensor_tensor(parts[1][2], parts[1][0], parts[1][1], ALU.subtract).then_inc(s.row_full, 1)
                link(v.tensor_scalar(R(4), R(1), -1.0, None, ALU.mult))
                v.tensor_tensor(sm[:, M_OUT, :], sm[:, B_L, :], sm[:, M_L, :], ALU.add).then_inc(s.row_ready, 1)

            def cols_first():
                for n, bk in enumerate((pA, pB)):
                    dve.wait_ge(s.rowT_full, n + 1)
                    for c in range(4):
                        src = bk[:, c * P:(c + 1) * P].rearrange("p (k h) -> p h k", h=32)[:, 0:H, :]
                        last = v.tensor_copy(cols[:, :, 4 * n + c, 0:4], src)
                    last.then_inc(s.cols_ready, 1)

            def cols_last():
                dve.wait_ge(s.rowT_full, 3)
                src = pA[0:TS, 0:P].rearrange("p (k h) -> p h k", h=32)[:, 0:H, :]
                v.tensor_copy(cols[0:TS, :, NC, 0:4], src)
                src = pA[:, P:P + 4 * NT].rearrange("p (c h) -> p h c", h=H)
                v.tensor_copy(cols[:, :, 0:NC, M_:M_ + 1].rearrange("p h c a -> p h (c a)"), src[:, :, 0:NC])
                v.tensor_copy(cols[0:TS, :, NC, M_:M_ + 1].rearrange("p h a -> p (h a)"), pA[0:TS, P + 4 * NC:P + 4 * NT])
                v.tensor_copy(abc[:, :, :].rearrange("p h c -> p (h c)"), pA[:, 256:256 + 2 * NC * H]).then_inc(s.cols_ready, 1)

            def up_head(at, hooks, start=None):
                for j in range(6):
                    u = at.after(j, j)
                    convert(u)
                    if j == 0 and start:
                        start()
                    for k, (o, n) in enumerate(SL):
                        dve.wait_ge(s.acc_full, u.slices(k + 1))
                        if j < 2:
                            last = v.scalar_tensor_tensor(out=work[:, j, o:o + n], in0=bank(u, k), scalar=DK ** -0.5,
                                                          in1=rb[:, o:o + n], op0=ALU.mult, op1=ALU.mult)
                        else:
                            last = v.tensor_tensor(work[:, j, o:o + n], bank(u, k), rb[:, o:o + n], ALU.mult)
                        last.then_inc(s.acc_free, 1)
                    if j in hooks:
                        hooks[j]()

            def mix(at, h, before):
                st, hc = h * NT, h * NC

                def drain(c, p):
                    f = filler(at, before, c, p)
                    if f is None or f[3] == 0:
                        return
                    u, j, k, _ = f
                    o, n = SL[k]
                    dve.wait_ge(s.acc_full, u.slices(k + 1))
                    if j is not None:
                        v.tensor_tensor(xT[:, j, o:o + n], xT[:, j, o:o + n], acc[:, 2, 0:n], ALU.add).then_inc(s.acc_free, 1)
                    else:
                        v.tensor_tensor(work[:, 6 + (c - 4) // 2, o:o + n], acc[:, 2, 0:n], rb[:, o:o + n], ALU.mult).then_inc(s.acc_free, 1)

                hs = slice(h, h + 1) if isinstance(h, int) else bass.ds(h, 1)
                v.tensor_copy(cc[:], cols[:, hs].rearrange("p a c k -> p (a c) k"))
                v.tensor_copy(ca[:], abc[:, hs].rearrange("p a c -> p (a c)"))
                v.tensor_copy(cn[:], nT_all[:, :, hs, :].rearrange("p b a t -> p (a t) b"))
                v.tensor_copy(cg[:], vecs[:, bass.ds(h * 2 + 5 * KD, 2)])
                v.memset(kvc[:, 2 * DK:2 * DK + 1], 1.0)
                v.memset(kvs[:, 2 * DK:2 * DK + 1], 1.0)
                v.memset(CT[:], 0.0).then_inc(s.cur_ready, 1)
                dve.wait_ge(s.cur_ready, h + 1)
                dve.wait_ge(s.kv_ready, st + 1)
                v.tensor_scalar(wgm[:], blocksel[:], cc[0:TS, NC, G_:G_ + 1], None, ALU.mult).then_inc(s.wgm_ready, 1)

                def scores(c):
                    n = ntok(c)
                    dve.wait_ge(s.qk_full, st + (c + 1))
                    dve.wait_ge(s.dx_ready, st + (c + 1))
                    v.tensor_tensor(dx[0:n, 0:n], acc[0:n, 3, P:P + n], dx[0:n, 0:n], ALU.mult).then_inc(s.sd_ready, 1)

                def weigh(c):
                    dve.wait_ge(s.kv_ready, st + (c + 2))
                    if c >= 1:
                        dve.wait_ge(s.up_full, hc + c)
                    v.tensor_scalar(wgv[:], kvc[:, DK:2 * DK + 1], cc[:, c, G_:G_ + 1], None, ALU.mult).then_inc(s.wgv_ready, 1)

                scores(0)
                weigh(0)
                for c in range(NT):
                    n = ntok(c)
                    if c < NC:
                        drain(c, 0)
                        dve.wait_ge(s.up_full, hc + (c + 1))
                        v.scalar_tensor_tensor(out=CT[:, :, 0:DK], in0=CT[:, :, 0:DK], scalar=ca[:, c:c + 1],
                                               in1=acc[:, 5, :].rearrange("p (a v) -> p a v", a=2), op0=ALU.mult, op1=ALU.add)
                        v.scalar_tensor_tensor(out=CT[:, :, DK:DK + 1], in0=CT[:, :, DK:DK + 1], scalar=ca[:, c:c + 1],
                                               in1=acc[:, 1, 300:302].rearrange("p (a v) -> p a v", v=1),
                                               op0=ALU.mult, op1=ALU.add).then_inc(s.ct_ready, 1)
                    dve.wait_ge(s.ia_full, st + (c + 1))
                    dve.wait_ge(s.t1_ready, st + (c + 1))
                    if c == NC:
                        v.scalar_tensor_tensor(out=qd[:], in0=acc[0:TS, 1, 340:340 + DB], scalar=1.0, in1=blocksel[:],
                                               op0=ALU.mult, op1=ALU.mult, accum_out=sc[0:TS, 6:7]).then_inc(s.smp_link, 1)
                        dve.wait_ge(s.smp_link, h * 3 + 1)
                        v.tensor_tensor(t1[0:TS, DK:DK + 1], sc[0:TS, 6:7], cc[0:TS, NC, W_:W_ + 1], ALU.mult).then_inc(s.smp_link, 1)
                        v.tensor_tensor(nn[:], cn[:], ca[:, NC:2 * NC].rearrange("p (a b) -> p a b", a=1).to_broadcast([P, 2, DB]),
                                        ALU.mult).then_inc(s.smp_link, 1)
                        dve.wait_ge(s.smp_link, h * 3 + 3)
                        v.tensor_tensor(nT_all[:, :, hs, :].rearrange("p b a t -> p (a t) b"), nn[:],
                                        acc[:, 1, 320:336].rearrange("p (t b) -> p t b", t=2), ALU.add)
                    if c >= 1:
                        dve.wait_ge(s.ht_full, st + c)
                    v.tensor_tensor(num[0:n, :], acc[0:n, 1, 0:DK + 1], t1[0:n, :], ALU.add).then_inc(s.num_ready, 1)
                    if c < NC:
                        drain(c, 1)
                        drain(c, 2)
                        scores(c + 1)
                        if c + 1 < NC:
                            weigh(c + 1)
                        drain(c, 3)
                        if filler_unit(at, before, c):
                            convert(filler_unit(at, before, c))
                        dve.wait_ge(s.upb_full, hc + (c + 1))
                        cr = cring[:, c % 2].rearrange("p t k -> p (t k)")
                        v.scalar_tensor_tensor(out=cr, in0=cr, scalar=ca[:, NC + c:NC + c + 1], in1=acc[:, 5, :],
                                               op0=ALU.mult, op1=ALU.add).then_inc(s.cb_ready, 1)
                        drain(c, 4)
                        dve.wait_ge(s.iv_full, hc + (c + 1))
                        v.tensor_copy(ivs[:, :, c * DS:(c + 1) * DS], pA[:, 0:2 * DS].rearrange("p (t s) -> p t s", t=2)).then_inc(s.iv_free, 1)
                        drain(c, 5)
                    dve.wait_ge(s.num_ready, st + (c + 1))
                    den = num[0:n, DK:DK + 1]
                    v.scalar_tensor_tensor(out=sc[0:n, 1:2], in0=den, scalar=-1.0, in1=den, op0=ALU.mult, op1=ALU.max).then_inc(s.den_link, 1)
                    dve.wait_ge(s.den_link, h * (4 * NT) + (4 * c + 1))
                    v.tensor_scalar(sc[0:n, 1:2], sc[0:n, 1:2], cc[0:n, c, T_:T_ + 1], None, ALU.max).then_inc(s.den_link, 1)
                    dve.wait_ge(s.den_link, h * (4 * NT) + (4 * c + 2))
                    v.reciprocal(sc[0:n, 2:3], sc[0:n, 1:2]).then_inc(s.den_link, 1)
                    dve.wait_ge(s.den_link, h * (4 * NT) + (4 * c + 3))
                    dve.wait_ge(s.ss_ready, st + (c + 1))
                    v.tensor_scalar(sc[0:n, 7:8], sc[0:n, 0:1], 1.0 / DK, sc[0:n, 2:3], ALU.mult, ALU.mult).then_inc(s.den_link, 1)
                    dve.wait_ge(s.den_link, h * (4 * NT) + (4 * c + 4))
                    v.tensor_scalar(sc[0:n, 3:4], sc[0:n, 7:8], sc[0:n, 2:3], EPS, ALU.mult, ALU.add).then_inc(s.ms_ready, 1)
                    if c >= 1:
                        tail(h, c - 1)
                    dve.wait_ge(s.rs0_ready, st + (c + 1))
                    v.tensor_tensor(sc[0:n, 5:6], sc[0:n, 4:5], sc[0:n, 2:3], ALU.mult).then_inc(s.rs_ready, 1)

            def tail(h, c):
                dve.wait_ge(s.ht_full, h * NT + (c + 1))
                v.tensor_copy(work[:, 0:2, tok(c)], pB[:, 0:2 * P].rearrange("p (e n) -> p e n", e=2)[:, :, 0:ntok(c)]).then_inc(s.ho_ready, 1)

            def gate(h):
                dve.wait_ge(s.ho_ready, h * NT + NT)
                for k, (o, n) in enumerate(SL):
                    dve.wait_ge(s.so_ready, h * 3 + (k + 1))
                    for e in range(2):
                        last = v.scalar_tensor_tensor(out=work[:, e, o:o + n], in0=work[:, e, o:o + n], scalar=cg[:, e:e + 1],
                                                      in1=work[:, 6 + e, o:o + n], op0=ALU.mult, op1=ALU.mult)
                    last.then_inc(s.hg_ready, 1)
                for k, (o, n) in enumerate(SL):
                    dve.wait_ge(s.hhm_ready, h * 3 + (k + 1))
                    v.tensor_tensor(hl0[:, :, o:o + n], work[:, 0:2, o:o + n], hh0[:, :, o:o + n].bitcast(F32), ALU.subtract).then_inc(s.hlm_ready, 1)
                dve.wait_ge(s.hlm_ready, h * 3 + 3)

            def mix_tail(h):
                tail(h, NT - 1)
                gate(h)
                dve.wait_ge(s.ot_full, h + 1)
                v.tensor_copy(ct0[:], pA[:, :].rearrange("p (a v) -> p a v", a=2)).then_inc(s.cp_ready, 1)
                hs = slice(h, h + 1) if isinstance(h, int) else bass.ds(h, 1)
                v.tensor_copy(ncol[:, hs, :].rearrange("p a t -> p (a t)"), CT[:, :, DK:DK + 1].rearrange("p t a -> p (t a)"))

            rows_gates()
            up_head(M_AT, {0: rows_cumsum, 1: rows_starts, 2: rows_max, 3: rows_args, 4: cols_first, 5: cols_last})
            dve.wait_ge(s.m_st, 32)
            dve.wait_ge(s.cols_ready, 3)
            mix(M_AT.after(6, 6), 0, False)
            with dve.Fori(0, H - 1) as h:
                at = At(M_AT.u + 8, M_AT.t + 8, h, HEAD_DU, HEAD_DT)
                up_head(at, {}, lambda: mix_tail(h))
                mix(at.after(6, 6), h + 1, True)
            mix_tail(H - 1)
            down(M_AT.after(38, 56), 1)

            def up_ffn(at, i, q):
                for t in range(2):
                    u = at.after(2 * t, 2 * t)
                    convert(u)
                    for k, (o, n) in enumerate(SL):
                        c0 = q + (3 * t + k + 1)
                        dve.wait_ge(s.acc_full, u.slices(k + 1))
                        v.tensor_tensor(work[:, 0, o:o + n], bank(u, k), rb[:, o:o + n], ALU.mult).then_inc(s.acc_free, 1)
                        dve.wait_ge(s.acc_free, u.slices(k + 1))
                        v.tensor_tensor(work[:, 2, o:o + n], work[:, 0, o:o + n], rb[:, o:o + n], ALU.mult).then_inc(s.g2_ready, 1)
                        dve.wait_ge(s.g2_ready, c0)
                        dve.wait_ge(s.sg_ready, c0)
                        v.tensor_tensor(work[:, 2, o:o + n], work[:, 2, o:o + n], work[:, 1, o:o + n], ALU.mult).then_inc(s.g3_ready, 1)
                    u = at.after(2 * t + 1, 2 * t + 1)
                    convert(u)
                    for k, (o, n) in enumerate(SL):
                        c0 = q + (3 * t + k + 1)
                        dve.wait_ge(s.acc_full, u.slices(k + 1))
                        dve.wait_ge(s.g3_ready, c0)
                        v.tensor_tensor(work[:, 3, o:o + n], bank(u, k), work[:, 2, o:o + n], ALU.mult).then_inc(s.acc_free, 1)
                        dve.wait_ge(s.acc_free, u.slices(k + 1))
                        dve.wait_ge(s.hh_ready, c0)
                        v.tensor_tensor(HL[i % 2][:, t, o:o + n], work[:, 3, o:o + n], HH[i % 2][:, t, o:o + n].bitcast(F32),
                                        ALU.subtract).then_inc(s.hl_ready, 1)

            def ffn(base, l, L, hook=None):
                q = 6 * FB * l
                mean_square(L - 1)
                rms_rows(L - 1)
                up_ffn(base, 0, q)
                if hook:
                    hook()
                with dve.Fori(0, ffn_turns // 2) as i:
                    at = At(base.u + 4, base.t + 4, i, FFN_DU, FFN_DT)
                    for e in range(2):
                        up_ffn(at.after(6 * e, 12 * e), 1 + e, i * 12 + (q + 6 + 6 * e))
                        down(at.after(6 * e + 4, 12 * e + 4))
                down(base.after(6 * FB - 2, 12 * FB - 8), L)

            ffn(F0_AT, 0, 2)

            dve.wait_ge(s.cs_full, 1)
            v.tensor_copy(cstT.rearrange("p b r k -> p (b r k)"), pB[:, 0:P]).then_inc(s.cs_ready, 1)
            v.memset(ub[:, 0:2], 0.0)
            dve.wait_ge(s.cs_ready, 1)
            ncv = [0]

            def clink(ins):
                ncv[0] += 1
                ins.then_inc(s.cv_link, 1)
                dve.wait_ge(s.cv_link, ncv[0])

            def up_conv(at, i):
                for t in range(2):
                    ct = 2 * i + t
                    tap = lambda r: gain(6 + r, ct)
                    u = at.after(3 * t, 3 * t)
                    convert(u)
                    for k, (o, n) in enumerate(SL):
                        dve.wait_ge(s.acc_full, u.slices(k + 1))
                        v.tensor_tensor(work[:, 0, o:o + n], bank(u, k), rb[:, o:o + n], ALU.mult).then_inc(s.acc_free, 1)
                        dve.wait_ge(s.acc_free, u.slices(k + 1))
                        clink(v.tensor_tensor(work[:, 0, o:o + n], work[:, 0, o:o + n], rb[:, o:o + n], ALU.mult))
                    u = at.after(3 * t + 1, 3 * t + 1)
                    convert(u)
                    clink(v.tensor_copy(us[:, :, 0:2], cstT[:, :, :, ct:ct + 1].rearrange("p b r a -> p b (r a)")))
                    for k, (o, n) in enumerate(SL):
                        dve.wait_ge(s.acc_full, u.slices(k + 1))
                        w = min(n, SEQ - o)
                        if w < n:
                            v.tensor_tensor(us[:, :, 2:2 + DS], bank(u, k)[:, w:n].rearrange("p (b s) -> p b s", b=DB),
                                            work[:, 0, SEQ:T].rearrange("p (b s) -> p b s", b=DB), ALU.mult)
                        v.tensor_tensor(ub[:, 2 + o:2 + o + w], bank(u, k)[:, 0:w], work[:, 0, o:o + w], ALU.mult).then_inc(s.acc_free, 1)
                    dve.wait_ge(s.acc_free, u.slices(3))
                    v.tensor_copy(cpo[:, :, ct:ct + 1].rearrange("p r a -> p (r a)"), ub[:, SEQ:SEQ + 2])
                    v.tensor_copy(cso[:, :, :, ct:ct + 1].rearrange("p b r a -> p b (r a)"), us[:, :, DS:DS + 2])
                    cv = work[:, 1, 0:SEQ]
                    cvs = work[:, 1, SEQ:T].rearrange("p (b s) -> p b s", b=DB)
                    v.tensor_scalar(cv, ub[:, 0:SEQ], tap(0), None, ALU.mult)
                    clink(v.tensor_scalar(cvs, us[:, :, 0:DS], tap(0), None, ALU.mult))
                    for r in (1, 2):
                        v.scalar_tensor_tensor(out=cv, in0=ub[:, r:r + SEQ], scalar=tap(r), in1=cv, op0=ALU.mult, op1=ALU.add)
                        clink(v.scalar_tensor_tensor(out=cvs, in0=us[:, :, r:r + DS], scalar=tap(r), in1=cvs, op0=ALU.mult, op1=ALU.add))
                    clink(v.tensor_tensor(work[:, 1, :], work[:, 1, :], rb[:], ALU.mult))
                    u = at.after(3 * t + 2, 3 * t + 2)
                    convert(u)
                    for k, (o, n) in enumerate(SL):
                        dve.wait_ge(s.acc_full, u.slices(k + 1))
                        v.tensor_tensor(work[:, 2, o:o + n], bank(u, k), work[:, 1, o:o + n], ALU.mult).then_inc(s.acc_free, 1)
                        dve.wait_ge(s.acc_free, u.slices(k + 1))
                        dve.wait_ge(s.chh_ready, 6 * i + 3 * t + k + 1)
                        v.tensor_tensor(HL[i % 2][:, t, o:o + n], work[:, 2, o:o + n], HH[i % 2][:, t, o:o + n].bitcast(F32),
                                        ALU.subtract).then_inc(s.chl_ready, 1)

            mean_square(2)
            rms_rows(2)
            up_conv(C_AT, 0)
            for i in range(CB):
                if i + 1 < CB:
                    up_conv(C_AT.after(6 + 8 * i, 6 + 14 * i), i + 1)
                    down(C_AT.after(12 + 8 * i, 12 + 14 * i))
                else:
                    down(C_AT.after(8 * CB - 2, 14 * CB - 8), 3)

            def small_out():
                dve.wait_ge(s.so_full, 1)
                for n, p in enumerate((64, 8, P, 16)):
                    v.tensor_copy(outv[0:p, n, :], pA[0:p, n * P:(n + 1) * P]).then_inc(s.so_evict, 1)

            ffn(F1_AT, 1, 4, small_out)
            mean_square(4)
            dve.wait_ge(s.rcol_ready, 5)
            dve.wait_ge(s.so_st, 64)
            for c in range(1, NT, 2):
                dve.wait_ge(s.fin_full, c + 1)
                b = 2 * (c % 3)
                v.tensor_scalar(workf[:, c * D:(c + 1) * D].rearrange("p (a n) -> p a n", a=2), acc[:, b:b + 2, :],
                                rcol[:, c:c + 1], None, ALU.mult).then_inc(s.yd_ready, 1)

        @block.tensor
        def _(pe):
            mm = nc.tensor.matmul

            def flip(out, in_, n):
                k = in_.shape[0]
                if n == P:
                    return nc.tensor.transpose(out, in_, ident[0:k, 0:k])
                return mm(out, in_, ident[0:k, 0:k], start=True, stop=True)

            def three(out, ah, al, bh, bl, first, last):
                mm(out, ah, bh, start=first, stop=False)
                mm(out, ah, bl, start=False, stop=False)
                return mm(out, al, bh, start=False, stop=last)

            def bank(at, k):
                return acc[:, 3 * (at.t % 2) + k, 0:SL[k][1]]

            def free(at, k):
                if at.t >= 2:
                    pe.wait_ge(s.acc_free, at.slices(k - 5))

            def up(at, L=None, hooks={}):
                pe.wait_ge(s.w_lo, at.units(1))
                j = at.slot()
                for k, (o, n) in enumerate(SL):
                    free(at, k)
                    for kk in range(KD):
                        if L is not None and k == 0:
                            pe.wait_ge(s.x_ready, 8 * L + kk + 1)
                        ws = slice(kk * P, (kk + 1) * P)
                        last = three(bank(at, k), wh[:, j, ws], wl[:, j, ws], xh[:, kk, o:o + n], xl[:, kk, o:o + n],
                                     kk == 0, kk == KD - 1)
                    last.then_inc(s.acc_full, 1)
                    if k in hooks:
                        hooks[k]()

            def down(at, hh, hl):
                for half in range(2):
                    pe.wait_ge(s.w_lo, at.after(half, 0).units(1))
                    j = at.after(half, 0).slot()
                    for jj in range(4):
                        u = at.after(half, 4 * half + jj)
                        for k, (o, n) in enumerate(SL):
                            free(u, k)
                            for kk in range(2):
                                ws = slice(kk * 512 + jj * P, kk * 512 + (jj + 1) * P)
                                last = three(bank(u, k), wh[:, j, ws], wl[:, j, ws], hh[:, kk, o:o + n], hl[:, kk, o:o + n],
                                             kk == 0, kk == 1)
                            last.then_inc(s.acc_full, 1)

            def square_sums(L):
                pe.wait_ge(s.ssq_ready, 8 * (L + 1))
                if L == 2:
                    pe.wait_ge(s.cs_ready, 1)
                for c in range(NT):
                    last = mm(pA[0:ntok(c), c:c + 1], ssq[:, tok(c)], ones[:, 0:1], start=True, stop=True)
                last.then_inc(s.st_full, 1)

            def rms_rows(L):
                pe.wait_ge(s.rcol_ready, L + 1)
                for c in range(NT):
                    n = ntok(c)
                    if c == NC:
                        pe.wait_ge(s.rb_free, 3 * L + 1)
                    out = (pA, pB, pA)[c // 4][:, (c % 4) * P:(c % 4) * P + n]
                    last = mm(out, rcol[0:n, c:c + 1].to_broadcast([n, P]), ident[0:n, 0:n], start=True, stop=True)
                    if c % 4 == 3 or c == NC:
                        last.then_inc(s.rb_full, 1)

            pe.wait_ge(s.const_ready, 1)
            pe.wait_ge(s.vec_ld, 160)
            nc.tensor.transpose(pA[:, 0:NV * KD], rows[0:NV * KD, 7, 0:P], ident[0:NV * KD, 0:NV * KD])
            nc.tensor.transpose(pA[:, P:P + 64], rows[0:64, 7, P:2 * P], ident[0:64, 0:64]).then_inc(s.vecT_full, 1)
            for c in range(NT):
                n, b = ntok(c), 2 * (c % 3)
                pe.wait_ge(s.x_ld, 16 * NT)
                if c >= 3:
                    pe.wait_ge(s.xt_free, c - 2)
                src = workf[:, c * D:(c + 1) * D] if c < NC else rb[0:TS, 0:D]
                for k in range(KD):
                    last = nc.tensor.transpose(acc[:, b + k // 4, (k % 4) * P:(k % 4) * P + n], src[:, k * P:(k + 1) * P], ident[0:n, 0:n])
                last.then_inc(s.xt_full, 1)
            up(G_AT, 0, {0: lambda: square_sums(0), 1: lambda: rms_rows(0)})

            def rows_first():
                pe.wait_ge(s.row_act, 6)
                pe.wait_ge(s.row_ready, 1)
                for n, bk in enumerate((pA, pB)):
                    for c in range(4):
                        last = nc.tensor.transpose(bk[:, c * P:(c + 1) * P], rows[:, 7, tok(4 * n + c)], ident[:])
                    last.then_inc(s.rowT_full, 1)

            def rows_last():
                pe.wait_ge(s.cols_ready, 1)
                mm(pA[0:TS, 0:P], rows[:, 7, tok(NC)], ident[:], start=True, stop=True)
                for c in range(NT):
                    n = ntok(c)
                    mm(pA[0:n, P + 4 * c:P + 4 * c + 4], rows[0:H, 4, tok(c)], ident[0:H, 0:H], start=True, stop=True)
                for h in range(H):
                    last = mm(pA[:, 256 + 2 * NC * h:256 + 2 * NC * (h + 1)], ident[0:H, h:h + 1].to_broadcast([H, P]), sm[:, 6, :],
                              start=True, stop=True)
                last.then_inc(s.rowT_full, 1)

            def up_head(at, hooks={}, tail=None):
                for j in range(6):
                    up(at.after(j, j), None, {0: tail} if tail and j == 0 else {})
                    if j in hooks:
                        hooks[j]()

            def out_rows(h, c):
                n, st = ntok(c), h * NT
                pe.wait_ge(s.hn_ready, st + (c + 1))
                if c >= 1:
                    pe.wait_ge(s.ho_ready, st + c)
                for e in range(2):
                    if n == P:
                        last = nc.tensor.transpose(pB[:, e * P:e * P + n], num[:, e * P:(e + 1) * P], ident[:])
                    else:
                        last = mm(pB[:, e * P:e * P + n], num[0:n, e * P:(e + 1) * P], ident[0:n, 0:n], start=True, stop=True)
                last.then_inc(s.ht_full, 1)

            def mix(at, h, before):
                st, hc = h * NT, h * NC

                def fill(c, p):
                    f = filler(at, before, c, p)
                    if f is None:
                        return
                    u, tile, k, part = f
                    (o, n), j = SL[k], u.slot()
                    if filler_unit(at, before, c) and p == (0 if tile is not None else 1):
                        pe.wait_ge(s.w_lo, u.units(1))
                        if tile == 0:
                            pe.wait_ge(s.hlm_ready, h * 3)
                    if part != 1:
                        pe.wait_ge(s.acc_free, u.slices(k))
                    if tile is not None:
                        for kk in range(2):
                            ws = slice(kk * 512 + (tile % 4) * P, kk * 512 + (tile % 4 + 1) * P)
                            last = three(acc[:, 2, 0:n], wh[:, j, ws], wl[:, j, ws], hh0[:, kk, o:o + n], hl0[:, kk, o:o + n],
                                         kk == 0, kk == 1)
                    else:
                        for kk in range(4 * part, 4 * part + 4):
                            ws = slice(kk * P, (kk + 1) * P)
                            last = three(acc[:, 2, 0:n], wh[:, j, ws], wl[:, j, ws], xh[:, kk, o:o + n], xl[:, kk, o:o + n],
                                         kk == 0, kk == KD - 1)
                    if part != 0:
                        last.then_inc(s.acc_full, 1)

                pe.wait_ge(s.acc_free, at.slices(0))
                pe.wait_ge(s.cur_ready, h + 1)

                def key_value(c):
                    if c >= 0:
                        pe.wait_ge(s.kv_ready, st + (c + 1))
                    ts = tok(NC if c < 0 else c)
                    n = TS if c < 0 else P
                    for j in range(4):
                        last = flip(acc[0:n, 4, j * P:(j + 1) * P], work[:, 2 + j, ts], n)
                    last.then_inc(s.kvp_full, 1)

                def prepare(c):
                    n, ts = ntok(c), tok(c)
                    if c >= 1:
                        pe.wait_ge(s.sd_ready, st + c)
                    mm(acc[0:n, 3, 0:n], cc[:, c, M_:M_ + 1].to_broadcast([P, n]), ident[:, 0:n], start=True, stop=False)
                    mm(acc[0:n, 3, 0:n], identb[0:n, 0:n], causal[:] if c < NC else blockneg[:], start=False, stop=True).then_inc(s.db_full, 1)
                    if c < NC:
                        key_value(c)
                    pe.wait_ge(s.dx_ready, st + (c + 1))
                    for e in range(2):
                        last = mm(acc[0:n, 3, P:P + n], work[:, 2 + e, ts], work[:, e, ts], start=e == 0, stop=e == 1)
                    last.then_inc(s.qk_full, 1)

                key_value(-1)
                prepare(0)
                for c in range(NC):
                    ts = tok(c)
                    if c >= 1:
                        pe.wait_ge(s.ct_ready, hc + c)
                        pe.wait_ge(s.t1_ready, st + c)
                    for e in range(2):
                        last = mm(acc[:, 0, 0:DK + 1], work[:, e, ts], CT[:, e, :], start=e == 0, stop=e == 1)
                    last.then_inc(s.in_full, 1)
                    fill(c, 0)
                    pe.wait_ge(s.sd_ready, st + (c + 1))
                    pe.wait_ge(s.wgv_ready, hc + (c + 1))
                    if c >= 1:
                        pe.wait_ge(s.num_ready, st + c)
                    mm(acc[:, 1, 0:DK + 1], dx[:], kvc[:, DK:2 * DK + 1], start=True, stop=True)
                    for e in range(2):
                        last = mm(acc[:, 1, 300 + e:301 + e], kvc[:, e * P:(e + 1) * P], wgv[:, DK:DK + 1], start=True, stop=True)
                    last.then_inc(s.ia_full, 1)
                    if c >= 1:
                        pe.wait_ge(s.cb_ready, hc + c)
                    for e in range(2):
                        last = mm(acc[:, 5, e * DK:(e + 1) * DK], kvc[:, e * P:(e + 1) * P], wgv[:, 0:DK], start=True, stop=True)
                    last.then_inc(s.up_full, 1)
                    fill(c, 1)
                    if c >= 1:
                        out_rows(h, c - 1)
                    pe.wait_ge(c_ld[c % 2], h * 64 + 16 * (c // 2 + 1))
                    if c >= 1:
                        pe.wait_ge(s.iv_free, hc + c)
                    for e in range(2):
                        for t in range(2):
                            last = nc.tensor.transpose(pA[:, e * DK + t * P:e * DK + (t + 1) * P], cring[:, c % 2, t, e * P:(e + 1) * P], ident[:])
                    last.then_inc(s.tr_full, 1)
                    fill(c, 2)
                    prepare(c + 1)
                    fill(c, 3)
                    pe.wait_ge(s.wgvb_ready, hc + (c + 1))
                    pe.wait_ge(s.ct_ready, hc + (c + 1))
                    for t in range(2):
                        last = mm(acc[:, 5, t * DK:(t + 1) * DK], wgvb[:, t * P:(t + 1) * P], kvs[:, 0:DK], start=True, stop=True)
                    last.then_inc(s.upb_full, 1)
                    fill(c, 4)
                    pe.wait_ge(s.ct0_ready, hc + (c + 1))
                    for t in range(2):
                        for e in range(2):
                            last = mm(pA[:, t * DS:(t + 1) * DS], ct0[:, e, t * P:(t + 1) * P], work[:, e, SEQ + c * DS:SEQ + (c + 1) * DS],
                                      start=e == 0, stop=e == 1)
                    last.then_inc(s.iv_full, 1)
                    fill(c, 5)
                c = NC
                pe.wait_ge(s.iv_free, hc + NC)
                pe.wait_ge(s.t1_ready, st + c)
                for t in range(2):
                    last = flip(acc[0:TS, 0, t * P:(t + 1) * P], ivs[:, t, :], TS)
                last.then_inc(s.in_full, 1)
                pe.wait_ge(s.sd_ready, st + (c + 1))
                pe.wait_ge(s.wgm_ready, h + 1)
                pe.wait_ge(s.num_ready, st + c)
                for e in range(2):
                    mm(acc[:, 1, 320 + e * DB:320 + (e + 1) * DB], kvs[:, e * P:(e + 1) * P], wgm[:], start=True, stop=True)
                mm(acc[0:TS, 1, 0:DK + 1], dx[0:TS, 0:TS], kvs[:, DK:2 * DK + 1], start=True, stop=True)
                for e in range(2):
                    last = mm(acc[0:TS, 1, 340:340 + DB], work[:, e, SEQ:T], cn[:, e, :], start=e == 0, stop=e == 1)
                last.then_inc(s.ia_full, 1)
                out_rows(h, NC - 1)
                pe.wait_ge(s.cb_ready, hc + NC)

            def mix_tail(h):
                out_rows(h, NT - 1)
                for t in range(2):
                    for e in range(2):
                        last = nc.tensor.transpose(pA[:, t * DK + e * P:t * DK + (e + 1) * P], CT[:, e, t * P:(t + 1) * P], ident[:])
                last.then_inc(s.ot_full, 1)

            up_head(M_AT, {4: rows_first, 5: rows_last})
            pe.wait_ge(s.cols_ready, 3)
            mix(M_AT.after(6, 6), 0, False)
            with pe.Fori(0, H - 1) as h:
                at = At(M_AT.u + 8, M_AT.t + 8, h, HEAD_DU, HEAD_DT)
                up_head(at, tail=lambda: mix_tail(h))
                mix(at.after(6, 6), h + 1, True)
            mix_tail(H - 1)
            pe.wait_ge(s.hlm_ready, H * 3)
            down(M_AT.after(38, 56), hh0, hl0)

            def up_ffn(at, L=None):
                for j in range(4):
                    first = L is not None and j == 0
                    up(at.after(j, j), L if first else None,
                       {0: lambda: square_sums(L), 1: lambda: rms_rows(L)} if first else {})

            def ffn(base, l, L, hook=None):
                q = 6 * FB * l
                up_ffn(base, L)
                if hook:
                    hook()
                with pe.Fori(0, ffn_turns // 2) as i:
                    at = At(base.u + 4, base.t + 4, i, FFN_DU, FFN_DT)
                    for e in range(2):
                        up_ffn(at.after(6 * e, 12 * e))
                        pe.wait_ge(s.hl_ready, i * 12 + (q + 6 + 6 * e))
                        down(at.after(6 * e + 4, 12 * e + 4), HH[e], HL[e])
                pe.wait_ge(s.hl_ready, q + 6 * FB)
                down(base.after(6 * FB - 2, 12 * FB - 8), HH[(FB - 1) % 2], HL[(FB - 1) % 2])

            ffn(F0_AT, 0, 1)
            pe.wait_ge(s.cs_ld, 16)
            nc.tensor.transpose(pB[:, 0:P], workf[:, 5 * T:5 * T + P], ident[:]).then_inc(s.cs_full, 1)

            def up_conv(at, L=None):
                for j in range(6):
                    first = L is not None and j == 0
                    up(at.after(j, j), L if first else None,
                       {0: lambda: square_sums(L), 1: lambda: rms_rows(L)} if first else {})

            up_conv(C_AT, 2)
            for i in range(CB):
                if i + 1 < CB:
                    up_conv(C_AT.after(6 + 8 * i, 6 + 14 * i))
                pe.wait_ge(s.chl_ready, 6 * (i + 1))
                at = C_AT.after(12 + 8 * i, 12 + 14 * i) if i + 1 < CB else C_AT.after(8 * CB - 2, 14 * CB - 8)
                down(at, HH[i % 2], HL[i % 2])

            def small_out():
                pe.wait_ge(s.rb_free, 12)
                flip(pA[0:64, 0:P], nT_all[:, :, :, :].rearrange("p b h t -> p (b h t)"), 64)
                flip(pA[0:8, P:2 * P], ncol[:, :, :].rearrange("p h t -> p (h t)"), 8)
                flip(pA[:, 2 * P:3 * P], cso.rearrange("p b r k -> p (b r k)"), P)
                flip(pA[0:16, 3 * P:4 * P], cpo.rearrange("p r k -> p (r k)"), 16).then_inc(s.so_full, 1)

            ffn(F1_AT, 1, 3, small_out)
            square_sums(4)
            pe.wait_ge(s.xh_ready, 40)
            for c in range(NT):
                n, b = ntok(c), 2 * (c % 3)
                if c >= 3:
                    pe.wait_ge(s.yd_ready if (c - 3) % 2 else s.ya_ready, (c - 3) // 2 + 1)
                for k in range(KD):
                    last = flip(acc[0:n, b + k // 4, (k % 4) * P:(k % 4 + 1) * P], xT[:, k, tok(c)], n)
                last.then_inc(s.fin_full, 1)


_IN = ["x_prompt", "x_sample", "state_mlstm_C", "state_mlstm_n", "state_mlstm_m", "state_conv", "norm_mix", "norm_ffn",
       "norm_final", "w_mlstm_in", "b_mlstm_gate", "mlstm_head_norm", "w_mlstm_out", "w_conv_in", "w_conv_taps",
       "w_conv_out", "w_ffn_gate_up", "w_ffn_down"]


def kernel(**inputs):
    import numpy as np
    import concourse.bacc as bacc
    from concourse.bass_utils import run_bass_kernel_spmd

    nc = bacc.Bacc("TRN2", target_bir_lowering=False, num_devices=1)
    arrays = {f"in_{n}": np.ascontiguousarray(inputs[n]) for n in _IN}
    args = [nc.dram_tensor(n, a.shape, mybir.dt.from_np(a.dtype), kind="ExternalInput").ap() for n, a in arrays.items()]
    shape = {n: a.shape for n, a in zip(_IN, arrays.values())}
    (B, S, D), (DB, DS, _) = shape["x_prompt"], shape["x_sample"]
    NM, _, H, DV, DK = shape["state_mlstm_C"]
    N2, _, R, _ = shape["state_conv"]
    outs = [(B, S, D), (DB, DS, D), (NM, B, H, DV, DK), (NM, B, H, DK), (NM, B, H), (N2, B, R, D),
            (NM, DB, H, DV, DK), (NM, DB, H, DK), (NM, DB, H), (N2, DB, R, D)]
    for i, o in enumerate(outs):
        args.append(nc.dram_tensor(f"out_{i}", o, F32, kind="ExternalOutput").ap())
    build(nc, *args)
    r = run_bass_kernel_spmd(nc, [arrays], core_ids=[0])
    return tuple(r.results[0][f"out_{i}"] for i in range(len(outs)))
```

```python
from contextlib import ExitStack

import concourse.bass as bass
from concourse import mybir

F32 = mybir.dt.float32
F32R = mybir.dt.float32r
BF16 = mybir.dt.bfloat16
ALU = mybir.AluOpType
ACT = mybir.ActivationFunctionType
AX = mybir.AxisListType

P = 128
EPS = 1e-6
BIG = 3.0e38
NEG = -1.0e30


class At:

    def __init__(self, u, t, i=0, du=0, dt=0):
        self.u, self.t, self.i, self.du, self.dt = u, t, i, du, dt

    def after(self, units, tiles):
        return At(self.u + units, self.t + tiles, self.i, self.du, self.dt)

    def slot(self):
        return self.u % 2

    def units(self, more):
        return self.i * self.du + (self.u + more)

    def loads(self):
        return self.i * (8 * self.du) + 16 * ((self.u + 1) // 2)

    def slices(self, more):
        return self.i * (3 * self.dt) + (3 * self.t + more)


class Semaphores:

    def __init__(self, sem):
        self.mask_ready = sem("mask_ready")
        self.const_ready = sem("const_ready")
        self.vec_ld = sem("vec_ld")
        self.vecT_full = sem("vecT_full")
        self.vec_ready = sem("vec_ready")
        self.xt_full = sem("xt_full")
        self.xt_free = sem("xt_free")
        self.gate_zero = sem("gate_zero")
        self.gate_ld = sem("gate_ld")
        self.w_hi = sem("w_hi")
        self.w_lo = sem("w_lo")
        self.acc_full = sem("acc_full")
        self.acc_free = sem("acc_free")
        self.xh_ready = sem("xh_ready")
        self.x_ready = sem("x_ready")
        self.sq_ready = sem("sq_ready")
        self.ssq_ready = sem("ssq_ready")
        self.st_full = sem("st_full")
        self.v9_ready = sem("v9_ready")
        self.rcol_ready = sem("rcol_ready")
        self.rb_full = sem("rb_full")
        self.rb_free = sem("rb_free")
        self.row_link = sem("row_link")
        self.row_full = sem("row_full")
        self.row_act = sem("row_act")
        self.row_ready = sem("row_ready")
        self.rowT_full = sem("rowT_full")
        self.cols_ready = sem("cols_ready")
        self.so_ready = sem("so_ready")
        self.cur_ready = sem("cur_ready")
        self.db_full = sem("db_full")
        self.dx_ready = sem("dx_ready")
        self.qk_full = sem("qk_full")
        self.sd_ready = sem("sd_ready")
        self.kvp_full = sem("kvp_full")
        self.kv_ready = sem("kv_ready")
        self.wgv_ready = sem("wgv_ready")
        self.in_full = sem("in_full")
        self.t1_ready = sem("t1_ready")
        self.ia_full = sem("ia_full")
        self.num_ready = sem("num_ready")
        self.up_full = sem("up_full")
        self.ct_ready = sem("ct_ready")
        self.wgm_ready = sem("wgm_ready")
        self.wgvb_ready = sem("wgvb_ready")
        self.tr_full = sem("tr_full")
        self.ct0_ready = sem("ct0_ready")
        self.iv_full = sem("iv_full")
        self.iv_free = sem("iv_free")
        self.upb_full = sem("upb_full")
        self.cb_ready = sem("cb_ready")
        self.ss_ready = sem("ss_ready")
        self.ms_ready = sem("ms_ready")
        self.rs0_ready = sem("rs0_ready")
        self.rs_ready = sem("rs_ready")
        self.hn_ready = sem("hn_ready")
        self.ht_full = sem("ht_full")
        self.ho_ready = sem("ho_ready")
        self.hg_ready = sem("hg_ready")
        self.hhm_ready = sem("hhm_ready")
        self.hlm_ready = sem("hlm_ready")
        self.den_link = sem("den_link")
        self.smp_link = sem("smp_link")
        self.ot_full = sem("ot_full")
        self.cp_ready = sem("cp_ready")
        self.cp_st = sem("cp_st")
        self.sg_ready = sem("sg_ready")
        self.g2_ready = sem("g2_ready")
        self.g3_ready = sem("g3_ready")
        self.hh_ready = sem("hh_ready")
        self.hl_ready = sem("hl_ready")
        self.chh_ready = sem("chh_ready")
        self.chl_ready = sem("chl_ready")
        self.cv_link = sem("cv_link")
        self.m_ld = sem("m_ld")
        self.m_st = sem("m_st")
        self.fin_full = sem("fin_full")
        self.ya_ready = sem("ya_ready")
        self.yd_ready = sem("yd_ready")
        self.y_st = sem("y_st")
        self.so_full = sem("so_full")
        self.so_evict = sem("so_evict")
        self.so_st = sem("so_st")
        self.cs_ld = sem("cs_ld")
        self.cs_full = sem("cs_full")
        self.cs_ready = sem("cs_ready")


def build(nc, x_prompt, x_sample, state_C, state_n, state_m, state_conv, norm_mix, norm_ffn, norm_final,
          w_mlstm_in, b_gate, head_norm, w_mlstm_out, w_conv_in, w_conv_taps, w_conv_out, w_gate_up, w_down,
          y_prompt, y_sample, C_prompt, n_prompt, m_prompt, conv_prompt, C_sample, n_sample, m_sample, conv_sample):
    D = x_prompt.shape[2]
    SEQ = x_prompt.shape[1]
    DB, DS = x_sample.shape[0], x_sample.shape[1]
    H = state_C.shape[2]
    DK = state_C.shape[4]
    F = w_down.shape[1]
    KD = D // P
    TS = DB * DS
    T = SEQ + TS
    NC = SEQ // P
    NT = NC + 1
    SL = [(0, 384), (384, 384), (768, T - 768)]
    FB = F // 256
    CB = D // 256
    RING = 4
    assert D == 1024 and SEQ == 1024 and TS == 64 and H == 4 and DK == 256 and KD == 8 and F % 256 == 0

    def tok(c):
        return slice(c * P, min((c + 1) * P, T))

    def ntok(c):
        return min(P, T - c * P)

    G_AT = At(0, 0)
    M_AT = G_AT.after(1, 1)
    F0_AT = M_AT.after(H * 10, H * 16)
    C_AT = F0_AT.after(FB * 6, FB * 12)
    F1_AT = C_AT.after(CB * 8, CB * 14)
    UNITS = F1_AT.u + FB * 6
    SLICES = 3 * (F1_AT.t + FB * 12)
    assert (F1_AT.t + FB * 12) % 2 == 1
    PAIR = (4, 0, 2)

    ctx = ExitStack()
    with ctx:
        def sb(name, shape, dt=F32, c=ctx):
            return c.enter_context(nc.sbuf_tensor(name, shape, dt))

        def sem(name):
            return ctx.enter_context(nc.semaphore(name))

        xT = sb("xT", [P, KD, T])
        xh = sb("xh", [P, KD, T], F32R)
        xl = sb("xl", [P, KD, T], F32R)
        stage = sb("stage", [P, 2, 1024])
        wh = sb("wh", [P, 2, 1024], F32R)
        wl = sb("wl", [P, 2, 1024], F32R)
        rb = sb("rb", [P, T])
        work = sb("work", [P, 8, T])
        workf = work[:, :, :].rearrange("p a t -> p (a t)")
        ssq = work[:, 6, :]
        sqt = [work[:, 7, :], work[:, 5, :]]
        ident = sb("ident", [P, P])
        identb = sb("identb", [P, P], BF16)
        causal = sb("causal", [P, P], BF16)
        blockneg = sb("blockneg", [TS, TS], BF16)
        blocksel = sb("blocksel", [TS, DB])
        ones = sb("ones", [P, 1])
        halfneg = sb("halfneg", [P, NT])
        rcol = sb("rcol", [P, NT])
        v9 = sb("v9", [P, NT])
        NV = 9
        vecs = sb("vecs", [P, NV * KD])
        nT_all = sb("nT_all", [P, DB, H, 2])
        cols = sb("cols", [P, H, NT, 5])
        abc = sb("abc", [P, H, 2 * NC])
        ncol = sb("ncol", [P, H, 2])
        U_, W_, T_, G_, M_ = range(5)

        def gain(v, k):
            return vecs[:, v * KD + k:v * KD + k + 1]

        LAYER_GAIN = [0, 2, 1, 3, 4]

        with ExitStack() as c1:
            rows = sb("rows", [P, 8, T], F32, c1)
            sm = sb("sm", [4, 8, 2 * NC], F32, c1)
            bcol = sb("bcol", [P, 1], F32, c1)
        xin = [rows[:, :, :].rearrange("p a t -> p (a t)")[:, c * D:(c + 1) * D] for c in range(NC - 1)] + \
            [workf[:, 0:D], rb[0:TS, 0:D]]
        hh0 = sb("hh0", [P, 2, T], F32R)
        hl0 = sb("hl0", [P, 2, T], F32R)
        with ExitStack() as c2:
            CT = sb("CT", [P, 2, DK + 1], F32, c2)
            cring = sb("cring", [P, RING, 2, DK], F32, c2)
            ct0 = sb("ct0", [P, 2, DK], F32, c2)
            kvc = sb("kvc", [P, 2 * DK + 1], F32, c2)
            kvs = sb("kvs", [TS, 2 * DK + 1], F32, c2)
            wgv = sb("wgv", [P, DK + 1], F32, c2)
            wgvb = sb("wgvb", [TS, DK], F32, c2)
            dx = sb("dx", [P, P], F32, c2)
            t1 = sb("t1", [P, DK + 1], F32, c2)
            num = sb("num", [P, DK + 1], F32, c2)
            ivs = sb("ivs", [P, 2, TS], F32, c2)
            cc = sb("cc", [P, NT, 5], F32, c2)
            ca = sb("ca", [P, 2 * NC], F32, c2)
            cn = sb("cn", [P, 2, DB], F32, c2)
            cg = sb("cg", [P, 2], F32, c2)
            nn = sb("nn", [P, 2, DB], F32, c2)
            wgm = sb("wgm", [TS, DB], F32, c2)
            qd = sb("qd", [TS, DB], F32, c2)
            sc = sb("sc", [P, 8], F32, c2)
        with ExitStack() as c3:
            hh1 = sb("hh1", [P, 2, T], F32R, c3)
            hl1 = sb("hl1", [P, 2, T], F32R, c3)
        HH, HL = [hh0, hh1], [hl0, hl1]
        ub = workf[:, 3 * T:3 * T + SEQ + 2]
        us = workf[:, 4 * T:4 * T + DB * (DS + 2)].rearrange("p (b s) -> p b s", b=DB)
        cstT = workf[:, 4 * T + 128:4 * T + 256].rearrange("p (b r k) -> p b r k", b=DB, r=2)
        cso = workf[:, 4 * T + 256:4 * T + 384].rearrange("p (b r k) -> p b r k", b=DB, r=2)
        cpo = workf[:, 4 * T + 384:4 * T + 400].rearrange("p (r k) -> p r k", r=2)
        outv = workf[:, 4 * T + 512:4 * T + 512 + 4 * P].rearrange("p (a n) -> p a n", a=4)

        acc = ctx.enter_context(nc.psum_tensor("acc", [P, 6, 512], F32))
        pA = ctx.enter_context(nc.psum_tensor("pA", [P, 512], F32))
        pB = ctx.enter_context(nc.psum_tensor("pB", [P, 512], F32))

        s = Semaphores(sem)
        w_ld = [sem("w_ld0"), sem("w_ld1")]
        x_ld = [sem(f"x_ld{k}") for k in range(3)]
        c_ld = [sem(f"c_ld{j}") for j in range(RING)]
        c_st = [sem(f"c_st{j}") for j in range(RING)]
        TURNS = DB // RING


        w_in_v = w_mlstm_in[0].rearrange("(k p) n -> p k n", p=P)
        w_conv_v = w_conv_in[0].rearrange("(k p) n -> p k n", p=P)
        w_gu_v = [w_gate_up[l].rearrange("(k p) n -> p k n", p=P) for l in range(2)]
        stage_col = [stage[:, j, :].rearrange("p (k n) -> p k n", k=KD) for j in range(2)]
        stage_row = [stage[:, j, :].rearrange("p (k n) -> p k n", k=2) for j in range(2)]
        gate0 = 4 * D

        ffn_turns = FB - 1
        assert ffn_turns % 2 == 0
        FFN_DU, FFN_DT = 12, 24
        PIECES = [[(j, k) for k in range(3) for j in range(KD)]] + \
            4 * [[(j, None) for j in range(4)] + [(j, k) for k in range(3) for j in range(4, KD)]]

        def pieces_before(L, i):
            return sum(len(x) for x in PIECES[:L]) + i

        def sums_before(L, i):
            every = [x for layer in PIECES[:L] for x in layer] + PIECES[L][:i]
            return sum(j > 0 for j, _ in every)

        def piece_count(L, j, k):
            return pieces_before(L, next(i for i, x in enumerate(PIECES[L]) if x in ((j, k), (j, None)))) + 1

        def piece_span(L, i):
            j, k = PIECES[L][i]
            o, n = (0, T) if k is None else SL[k]
            return j, slice(o, o + n)

        HEAD_DU, HEAD_DT = 10, 16

        def filler(at, before, c, p):
            if c < 4:
                if not before:
                    return None
                i = 12 * (c // 2) + 6 * (c % 2) + p
                return at.after(c // 2, i // 3), i // 3, i % 3, None
            if p % 2 == 0:
                return None
            i = 3 * (c % 2) + p // 2
            gate = at.after(2, 8) if before else at
            return gate.after((c - 4) // 2, (c - 4) // 2), None, i // 2, i % 2

        def filler_unit(at, before, c):
            f = None if c % 2 else filler(at, before, c, 1)
            return f and (f[0] if f[1] is None else at.after(c // 2, 2 * c))

        block = ctx.enter_context(nc.Block())

        @block.sync
        def _(sp):
            def load(at, src, row):
                if at.u >= 2:
                    sp.wait_ge(s.w_lo, at.units(-1))
                j = at.slot()
                sp.dma_start((stage_row if row else stage_col)[j], src).then_inc(w_ld[j], 16)

            def load_up(at, w, col):
                load(at, w[:, :, bass.ds(col, P)] if not isinstance(col, int) else w[:, :, col:col + P], False)

            def load_down(at, w, i):
                v = w.rearrange("(i k p) n -> p i k n", k=2, p=P)
                for half in range(2):
                    cs = slice(half * 512, (half + 1) * 512)
                    src = v[:, i, :, cs] if isinstance(i, int) else \
                        v[:, bass.ds(i, 1), :, cs].rearrange("p a k n -> p (a k) n")
                    load(at.after(half, 0), src, True)

            def load_up_head(at, h, first, last, hooks={}):
                for j in range(first, last):
                    if j in hooks:
                        hooks[j]()
                    load_up(at.after(j - first, 0), w_in_v, h * 256 + ((j // 2) * D + (j % 2) * P))

            def load_up_ffn(at, l, i):
                for j in range(4):
                    load_up(at.after(j, 0), w_gu_v[l], i * 256 + ((j % 2) * F + (j // 2) * P))

            def load_up_conv(at, i):
                for j in range(6):
                    which = [1, 2, 0][j % 3]
                    load_up(at.after(j, 0), w_conv_v, i * 256 + which * D + (j // 3) * P)

            def store_head(h):
                sp.wait_ge(s.cp_ready, h + 1)
                dst = C_prompt[0, 0].rearrange("h (t p) k -> p h t k", p=P)
                dst = dst[:, h] if isinstance(h, int) else dst[:, bass.ds(h, 1)].rearrange("p a t k -> p (a t) k")
                sp.dma_start(dst, ct0[:]).then_inc(s.cp_st, 16)

            def load_x(k):
                for c in range(3 * k, 3 * k + 3):
                    src = x_prompt[0, c * P:(c + 1) * P, :] if c < NC else x_sample.rearrange("b s d -> (b s) d")
                    sp.dma_start(xin[c], src).then_inc(x_ld[k], 16)

            load_x(0)
            sp.wait_ge(s.gate_zero, 1)
            with nc.allow_non_contiguous_dma(reason="eight columns"):
                sp.dma_start(stage_col[0][:, :, 0:H], w_in_v[:, :, gate0:gate0 + H]).then_inc(s.gate_ld, 16)
                sp.dma_start(stage_col[0][:, :, 32:32 + H], w_in_v[:, :, gate0 + H:gate0 + 2 * H]).then_inc(s.gate_ld, 16)
            load_x(1)
            load_x(2)
            load_up_head(M_AT, 0, 0, 8)
            with sp.Fori(0, H - 1) as h:
                at = At(M_AT.u + 8, 0, h, HEAD_DU, HEAD_DT)
                load_up_head(at, h + 1, 0, 6, {4: lambda: store_head(h)})
                load_down(at.after(6, 0), w_mlstm_out[0], h)
                load_up_head(at.after(8, 0), h + 1, 6, 8)
            load_down(At(M_AT.u + 38, 0), w_mlstm_out[0], H - 1)
            store_head(H - 1)

            def load_ffn(base, l):
                load_up_ffn(base, l, 0)
                with sp.Fori(0, ffn_turns // 2) as i:
                    at = At(base.u + 4, 0, i, FFN_DU, FFN_DT)
                    for e in range(2):
                        load_up_ffn(at.after(6 * e, 0), l, i * 2 + (1 + e))
                        load_down(at.after(6 * e + 4, 0), w_down[l], i * 2 + e)
                load_down(base.after(6 * FB - 2, 0), w_down[l], FB - 1)

            load_ffn(F0_AT, 0)
            load_up_conv(C_AT, 0)
            for i in range(CB):
                if i + 1 < CB:
                    load_up_conv(C_AT.after(6 + 8 * i, 0), i + 1)
                load_down(C_AT.after(8 * i + 12 if i + 1 < CB else 8 * CB - 2, 0), w_conv_out[0], i)
            load_ffn(F1_AT, 1)

            for c in range(NT):
                sp.wait_ge(s.yd_ready if c % 2 else s.ya_ready, c // 2 + 1)
                if c < NC:
                    sp.dma_start(y_prompt[0, c * P:(c + 1) * P, :], workf[:, c * D:(c + 1) * D]).then_inc(s.y_st, 16)
                else:
                    sp.dma_start(y_sample.rearrange("b s d -> (b s) d"), rb[0:TS, 0:D]).then_inc(s.y_st, 16)
            sp.wait_ge(s.y_st, 16 * NT)
            sp.wait_ge(s.cp_st, 16 * H)

        @block.gpsimd
        def _(pool):
            g = nc.gpsimd
            g.memset(ident[:], 0.0).then_inc(s.mask_ready, 1)
            g.memset(identb[:], 0.0).then_inc(s.mask_ready, 1)
            g.memset(causal[:], 0.0).then_inc(s.mask_ready, 1)
            g.memset(blockneg[:], 0.0).then_inc(s.mask_ready, 1)
            g.memset(blocksel[:], 1.0).then_inc(s.mask_ready, 1)
            g.memset(ones[:], 1.0).then_inc(s.mask_ready, 1)
            g.memset(halfneg[:], -0.5).then_inc(s.mask_ready, 1)
            pool.wait_ge(s.mask_ready, 7)
            for m in (ident, identb):
                g.affine_select(out=m[:], in_=m[:], compare_op=ALU.not_equal, fill=1.0, base=0,
                                pattern=[[-1, P]], channel_multiplier=1).then_inc(s.mask_ready, 1)
            g.affine_select(out=causal[:], in_=causal[:], compare_op=ALU.is_ge, fill=NEG, base=0,
                            pattern=[[1, P]], channel_multiplier=-1).then_inc(s.mask_ready, 1)
            g.affine_select(out=blockneg[:], in_=blockneg[:], compare_op=ALU.is_ge, fill=NEG, base=0,
                            pattern=[[1, TS]], channel_multiplier=-1).then_inc(s.mask_ready, 1)
            bn = blockneg[:, :].rearrange("p (b s) -> p b s", b=DB)
            pool.wait_ge(s.mask_ready, 11)
            g.affine_select(out=bn, in_=bn, compare_op=ALU.is_ge, fill=NEG, base=0,
                            pattern=[[-DS, DB], [0, DS]], channel_multiplier=1).then_inc(s.mask_ready, 1)
            g.affine_select(out=blocksel[:], in_=blocksel[:], compare_op=ALU.is_ge, fill=0.0, base=0,
                            pattern=[[-DS, DB]], channel_multiplier=1).then_inc(s.mask_ready, 1)
            pool.wait_ge(s.mask_ready, 13)
            g.affine_select(out=bn, in_=bn, compare_op=ALU.is_ge, fill=NEG, base=DS - 1,
                            pattern=[[DS, DB], [0, DS]], channel_multiplier=-1).then_inc(s.mask_ready, 1)
            g.affine_select(out=blocksel[:], in_=blocksel[:], compare_op=ALU.is_ge, fill=0.0, base=DS - 1,
                            pattern=[[DS, DB]], channel_multiplier=-1).then_inc(s.mask_ready, 1)
            pool.wait_ge(s.mask_ready, 15)
            g.memset(v9[:], 1.0).then_inc(s.const_ready, 1)

            def rstd(L):
                pool.wait_ge(s.v9_ready, 2 * (L + 1))
                g.tensor_tensor(rcol[:], v9[:], halfneg[:], ALU.pow).then_inc(s.rcol_ready, 1)

            def sum_piece(L, i):
                j, span = piece_span(L, i)
                if j == 0:
                    return
                before = sums_before(L, i)
                pool.wait_ge(s.sq_ready, pieces_before(L, i) + 1)
                if before > 0:
                    pool.wait_ge(s.ssq_ready, before)
                g.tensor_tensor(ssq[:, span], ssq[:, span], sqt[before % 2][:, span], ALU.add).then_inc(s.ssq_ready, 1)

            def sums(L):
                for i in range(len(PIECES[L])):
                    sum_piece(L, i)

            def head(v, h):
                return v[:, h] if isinstance(h, int) else v[:, bass.ds(h, 1)].rearrange("p a t k -> p (a t) k")

            def c_load(h, b):
                pool.dma_start(cring[:, b % RING], head(state_C[0, b].rearrange("h (t p) k -> p h t k", p=P), h)).then_inc(c_ld[b % RING], 16)

            def c_store(h, b):
                pool.dma_start(head(C_sample[0, b].rearrange("h (t p) k -> p h t k", p=P), h), cring[:, b % RING]).then_inc(c_st[b % RING], 16)

            def mix(h, last):
                for c in range(NT):
                    n = ntok(c)
                    pool.wait_ge(s.ms_ready, h * NT + (c + 1))
                    if c < NC:
                        pool.wait_ge(s.cb_ready, h * NC + (c + 1))
                    ahead = c + 2
                    if RING <= ahead < NC:
                        pool.wait_ge(c_st[ahead % RING], h * (16 * TURNS) + 16 * (ahead // RING))
                    if c == NC and not last:
                        for b in range(RING):
                            pool.wait_ge(c_st[b], h * (16 * TURNS) + 16 * TURNS)
                    g.tensor_tensor(sc[0:n, 4:5], sc[0:n, 3:4], halfneg[0:n, 0:1], ALU.pow).then_inc(s.rs0_ready, 1)
                    if c < NC:
                        c_store(h, c)
                    if ahead < NC:
                        c_load(h, ahead)
                    if c == NC and not last:
                        for b in range(2):
                            c_load(h + 1, b)

            sums(0)
            rstd(0)
            pool.wait_ge(s.cols_ready, 3)
            pool.wait_ge(s.m_st, 32)
            c_load(0, 0)
            c_load(0, 1)
            with pool.Fori(0, H - 1) as h:
                mix(h, False)
            mix(H - 1, True)
            for L in range(1, 4):
                sums(L)
                rstd(L)
            for j in range(RING):
                pool.wait_ge(c_st[j], 16 * TURNS * H)
            pool.wait_ge(s.so_evict, 1)
            pool.dma_start(n_sample[0].rearrange("b h (t p) -> (b h t) p", p=P), outv[0:64, 0, :]).then_inc(s.so_st, 16)
            pool.wait_ge(s.so_evict, 2)
            pool.dma_start(n_prompt[0, 0].rearrange("h (t p) -> (h t) p", p=P), outv[0:8, 1, :]).then_inc(s.so_st, 16)
            pool.wait_ge(s.so_evict, 3)
            pool.dma_start(conv_sample[0].rearrange("b r (k p) -> (b r k) p", p=P), outv[:, 2, :]).then_inc(s.so_st, 16)
            pool.wait_ge(s.so_evict, 4)
            pool.dma_start(conv_prompt[0, 0].rearrange("r (k p) -> (r k) p", p=P), outv[0:16, 3, :]).then_inc(s.so_st, 16)
            def last_rstd(k):
                pool.wait_ge(s.v9_ready, 9 + k + (k == 2))
                cs = slice(3 * k, 3 * k + 3)
                g.tensor_tensor(rcol[:, cs], v9[:, cs], halfneg[:, cs], ALU.pow).then_inc(s.rcol_ready, 1)

            for i, (j, k) in enumerate(PIECES[4]):
                sum_piece(4, i)
                if j == KD - 1 and k > 0:
                    last_rstd(k - 1)
            last_rstd(2)
            pool.wait_ge(s.so_st, 64)

        @block.scalar
        def _(act):
            a = nc.scalar

            def convert(at):
                nx = at.after(1, 0)
                if nx.u >= UNITS:
                    return
                act.wait_ge(w_ld[nx.slot()], nx.loads())
                if nx.u >= 2:
                    act.wait_ge(s.acc_full, at.slices(0))
                a.activation(wh[:, nx.slot(), :], stage[:, nx.slot(), :], ACT.Copy).then_inc(s.w_hi, 1)

            def square(L, i):
                j, span = piece_span(L, i)
                before = sums_before(L, i)
                if j > 0 and before >= 2:
                    act.wait_ge(s.ssq_ready, before - 1)
                to = ssq if j == 0 else sqt[before % 2]
                a.activation(to[:, span], xT[:, j, span], ACT.Square).then_inc(s.sq_ready, 1)

            def high(L, i):
                j, span = piece_span(L, i)
                a.activation(xh[:, j, span], xT[:, j, span], ACT.Copy, scale=gain(LAYER_GAIN[L], j)).then_inc(s.xh_ready, 1)

            def down(at, L=None):
                for half in range(2):
                    u = at.after(half, 4 * half)
                    convert(u)
                    if L is None:
                        continue
                    for m in range(12 if half else 4):
                        i = 4 * half + m
                        act.wait_ge(s.acc_free, u.slices(m + 1 if half else 3 * (m + 1)))
                        if L < 4:
                            high(L, i)
                        square(L, i)

            for n, v in enumerate((norm_mix[0:1, :], norm_mix[1:2, :], norm_ffn[0:1, :], norm_ffn[1:2, :],
                                   norm_final.rearrange("(a d) -> a d", a=1), head_norm,
                                   w_conv_taps[0, 0:1, :], w_conv_taps[0, 1:2, :], w_conv_taps[0, 2:3, :])):
                act.dma_start(rows[n * KD:(n + 1) * KD, 7, 0:P], v.rearrange("a (k p) -> (a k) p", p=P)).then_inc(s.vec_ld, 16)
            act.dma_start(rows[0:64, 7, P:2 * P], state_n[0].rearrange("b h (t p) -> (b h t) p", p=P)).then_inc(s.vec_ld, 16)
            with nc.allow_non_contiguous_dma(reason="a few words"):
                act.dma_start(sm[0:H, 0, NC:2 * NC], state_m[0].rearrange("b h -> h b")).then_inc(s.m_ld, 16)
                act.dma_start(bcol[0:H, :], b_gate[0, 0:H].rearrange("(h a) -> h a", a=1)).then_inc(s.m_ld, 16)
                act.dma_start(bcol[32:32 + H, :], b_gate[0, H:2 * H].rearrange("(h a) -> h a", a=1)).then_inc(s.m_ld, 16)

            act.wait_ge(s.gate_ld, 32)
            a.activation(wh[:, 0, :], stage[:, 0, :], ACT.Copy).then_inc(s.w_hi, 1)
            act.wait_ge(s.vec_ready, 1)
            for k in range(3):
                act.wait_ge(s.xt_free, 3 * (k + 1))
                for i in range(KD * k, KD * (k + 1)):
                    high(0, i)
                for i in range(KD * k, KD * (k + 1)):
                    square(0, i)
                if k == 1:
                    convert(G_AT)
            R = lambda k, p=0, n=H: rows[p:p + n, k, :]
            act.wait_ge(s.row_full, 1)
            a.activation(R(3), R(3), ACT.Exp, scale=-1.0).then_inc(s.row_act, 1)
            act.wait_ge(s.row_act, 1)
            a.activation(R(3), R(3), ACT.Ln, bias=1.0).then_inc(s.row_act, 1)

            def row_exps():
                act.wait_ge(s.row_full, 2)
                a.activation(R(7, 32), R(3), ACT.Exp).then_inc(s.row_act, 1)
                act.wait_ge(s.row_full, 3)
                a.activation(R(7, 64), R(0), ACT.Exp, scale=-1.0).then_inc(s.row_act, 1)
                act.wait_ge(s.row_full, 4)
                a.activation(R(7, 96), R(5), ACT.Exp).then_inc(s.row_act, 1)
                a.activation(sm[:, 6, :], sm[:, 5, :], ACT.Exp).then_inc(s.row_act, 1)
                act.wait_ge(s.row_ready, 1)
                with nc.allow_non_contiguous_dma(reason="a few words"):
                    act.dma_start(m_prompt[0].rearrange("b h -> h b"), sm[:, 7, NC - 1:NC]).then_inc(s.m_st, 16)
                    act.dma_start(m_sample[0].rearrange("b h -> h b"), sm[:, 7, NC:2 * NC]).then_inc(s.m_st, 16)
                act.wait_ge(s.m_st, 32)

            def up_head(at, hooks):
                for j in range(6):
                    convert(at.after(j, j))
                    if j in hooks:
                        hooks[j]()

            def mix(at, h, before):
                st = h * NT
                act.wait_ge(s.cur_ready, h + 1)

                def kv(c):
                    act.wait_ge(s.kvp_full, st + (c + 2))
                    if c >= 1:
                        act.wait_ge(s.up_full, h * NC + c)
                    if c < 0:
                        a.activation(kvs[:, 0:2 * DK], acc[0:TS, 4, :], ACT.Copy).then_inc(s.kv_ready, 1)
                    else:
                        a.activation(kvc[:, 0:2 * DK], acc[:, 4, :], ACT.Copy).then_inc(s.kv_ready, 1)

                def decay(c):
                    n = ntok(c)
                    act.wait_ge(s.db_full, st + (c + 1))
                    if c >= 1:
                        act.wait_ge(s.ia_full, st + c)
                    a.activation(dx[0:n, 0:n], acc[0:n, 3, 0:n], ACT.Exp, bias=cc[0:n, c, U_:U_ + 1]).then_inc(s.dx_ready, 1)

                kv(-1)
                decay(0)
                kv(0)
                for c in range(NT):
                    n = ntok(c)
                    act.wait_ge(s.in_full, st + (c + 1))
                    if c >= 1:
                        act.wait_ge(s.ss_ready, st + c)
                    w = DK + 1 if c < NC else DK
                    a.activation(t1[0:n, 0:w], acc[0:n, 0, 0:w], ACT.Copy, scale=cc[0:n, c, W_:W_ + 1]).then_inc(s.t1_ready, 1)
                    if c < NC:
                        act.wait_ge(s.wgm_ready, h + 1)
                        if c >= 1:
                            act.wait_ge(s.upb_full, h * NC + c)
                        a.activation(wgvb[:], kvs[:, DK:2 * DK], ACT.Copy, scale=wgm[:, c:c + 1]).then_inc(s.wgvb_ready, 1)
                        if filler_unit(at, before, c):
                            convert(filler_unit(at, before, c))
                        act.wait_ge(s.tr_full, h * NC + (c + 1))
                        if c >= 1:
                            act.wait_ge(s.iv_full, h * NC + c)
                        a.activation(ct0[:], pA[:, :].rearrange("p (a v) -> p a v", a=2), ACT.Copy).then_inc(s.ct0_ready, 1)
                        decay(c + 1)
                        if c + 1 < NC:
                            kv(c + 1)
                    else:
                        past = at.after(4, 10) if before else at.after(2, 2)
                        act.wait_ge(s.acc_free, past.slices(0))
                        for o, m in SL:
                            a.activation(work[:, 6:8, o:o + m], work[:, 6:8, o:o + m], ACT.Sigmoid).then_inc(s.so_ready, 1)
                    act.wait_ge(s.num_ready, st + (c + 1))
                    a.activation(t1[0:n, 0:DK], num[0:n, 0:DK], ACT.Square, accum_out=sc[0:n, 0:1]).then_inc(s.ss_ready, 1)
                    act.wait_ge(s.rs_ready, st + (c + 1))
                    a.activation(num[0:n, 0:DK], num[0:n, 0:DK], ACT.Copy, scale=sc[0:n, 5:6]).then_inc(s.hn_ready, 1)

            def gate(h):
                for k, (o, n) in enumerate(SL):
                    act.wait_ge(s.hg_ready, h * 3 + (k + 1))
                    a.activation(hh0[:, :, o:o + n], work[:, 0:2, o:o + n], ACT.Copy).then_inc(s.hhm_ready, 1)

            def stored(h):
                act.wait_ge(s.cp_st, h * 16 + 16)

            up_head(M_AT, {4: row_exps})
            mix(M_AT.after(6, 6), 0, False)
            with act.Fori(0, H - 1) as h:
                at = At(M_AT.u + 8, M_AT.t + 8, h, HEAD_DU, HEAD_DT)
                up_head(at, {0: lambda: gate(h), 5: lambda: stored(h)})
                mix(at.after(6, 6), h + 1, True)
            gate(H - 1)
            down(M_AT.after(38, 56), 1)

            act.dma_start(outv[:, 0, :], state_conv[0].rearrange("b r (k p) -> (b r k) p", p=P)).then_inc(s.cs_ld, 16)

            def up_ffn(at, i, q):
                for t in range(2):
                    u = at.after(2 * t, 2 * t)
                    convert(u)
                    for k, (o, n) in enumerate(SL):
                        act.wait_ge(s.acc_free, u.slices(k + 1))
                        a.activation(work[:, 1, o:o + n], work[:, 0, o:o + n], ACT.Sigmoid).then_inc(s.sg_ready, 1)
                    u = at.after(2 * t + 1, 2 * t + 1)
                    convert(u)
                    for k, (o, n) in enumerate(SL):
                        act.wait_ge(s.acc_free, u.slices(k + 1))
                        a.activation(HH[i % 2][:, t, o:o + n], work[:, 3, o:o + n], ACT.Copy).then_inc(s.hh_ready, 1)

            def ffn(base, l, L):
                q = 6 * FB * l
                up_ffn(base, 0, q)
                with act.Fori(0, ffn_turns // 2) as i:
                    at = At(base.u + 4, base.t + 4, i, FFN_DU, FFN_DT)
                    for e in range(2):
                        up_ffn(at.after(6 * e, 12 * e), 1 + e, i * 12 + (q + 6 + 6 * e))
                        down(at.after(6 * e + 4, 12 * e + 4))
                down(base.after(6 * FB - 2, 12 * FB - 8), L)

            def up_conv(at, i):
                for t in range(2):
                    for j in range(3):
                        convert(at.after(3 * t + j, 3 * t + j))
                    u = at.after(3 * t + 2, 3 * t + 2)
                    for k, (o, n) in enumerate(SL):
                        act.wait_ge(s.acc_free, u.slices(k + 1))
                        a.activation(HH[i % 2][:, t, o:o + n], work[:, 2, o:o + n], ACT.Copy).then_inc(s.chh_ready, 1)

            for j in range(RING):
                act.wait_ge(c_st[j], 16 * TURNS * H)
            act.wait_ge(s.cp_st, 16 * H)
            ffn(F0_AT, 0, 2)
            up_conv(C_AT, 0)
            for i in range(CB):
                if i + 1 < CB:
                    up_conv(C_AT.after(6 + 8 * i, 6 + 14 * i), i + 1)
                    down(C_AT.after(12 + 8 * i, 12 + 14 * i))
                else:
                    down(C_AT.after(8 * CB - 2, 14 * CB - 8), 3)
            ffn(F1_AT, 1, 4)

            act.wait_ge(s.so_st, 64)
            for c in range(0, NT, 2):
                n = ntok(c)
                act.wait_ge(s.rcol_ready, 5 + c // 3)
                act.wait_ge(s.fin_full, c + 1)
                b = PAIR[c % 3]
                dst = workf[:, c * D:(c + 1) * D] if c < NC else rb[:, 0:D]
                a.activation(dst[0:n, :].rearrange("p (a n) -> p a n", a=2), acc[0:n, b:b + 2, :], ACT.Copy,
                             scale=rcol[0:n, c:c + 1]).then_inc(s.ya_ready, 1)

        @block.vector
        def _(dve):
            v = nc.vector

            def convert(at):
                nx = at.after(1, 0)
                if nx.u >= UNITS:
                    return
                dve.wait_ge(s.w_hi, nx.units(1))
                j = nx.slot()
                v.tensor_tensor(wl[:, j, :], stage[:, j, :], wh[:, j, :].bitcast(F32), ALU.subtract).then_inc(s.w_lo, 1)

            def low(L, i):
                j, span = piece_span(L, i)
                if L < 4:
                    dve.wait_ge(s.xh_ready, pieces_before(L, i) + 1)
                    v.scalar_tensor_tensor(out=xl[:, j, span], in0=xT[:, j, span], scalar=gain(LAYER_GAIN[L], j),
                                           in1=xh[:, j, span].bitcast(F32), op0=ALU.mult, op1=ALU.subtract).then_inc(s.x_ready, 1)
                else:
                    dve.wait_ge(s.sq_ready, pieces_before(L, i) + 1)
                    v.tensor_scalar(xT[:, j, span], xT[:, j, span], gain(4, j), None, ALU.mult).then_inc(s.x_ready, 1)

            def mean_square(L):
                dve.wait_ge(s.st_full, L + 1)
                v.tensor_scalar(v9[:, 0:NC], pA[:, 0:NC], 1.0 / D, EPS, ALU.mult, ALU.add).then_inc(s.v9_ready, 1)
                v.tensor_scalar(v9[0:TS, NC:NT], pA[0:TS, NC:NT], 1.0 / D, EPS, ALU.mult, ALU.add).then_inc(s.v9_ready, 1)

            def rms_rows(L):
                for n, (bank, o, w) in enumerate(((pA, 0, 512), (pB, 512, 512), (pA, 1024, TS))):
                    dve.wait_ge(s.rb_full, 3 * L + n + 1)
                    v.tensor_copy(rb[:, o:o + w], bank[:, 0:w]).then_inc(s.rb_free, 1)
                dve.wait_ge(s.rb_free, 3 * L + 3)

            def bank(at, k):
                return acc[:, 3 * (at.t % 2) + k, 0:SL[k][1]]

            def bank_in_turn(at, m):
                return acc[:, (3 * (at.t % 2) + m) % 6, :]

            def down(at, L=None, hook=None):
                late = None
                for half in range(2):
                    u = at.after(half, 4 * half)
                    convert(u)
                    for m in range(12):
                        j, k = (4 + m % 4, m // 4) if half and L is not None else (4 * half + m // 3, m % 3)
                        o, n = SL[k]
                        dve.wait_ge(s.acc_full, u.slices(m + 1))
                        v.tensor_tensor(xT[:, j, o:o + n], xT[:, j, o:o + n], bank_in_turn(u, m)[:, 0:n], ALU.add).then_inc(s.acc_free, 1)
                        if L is None or (not half and k < 2):
                            continue
                        if late is not None:
                            low(L, late)
                        late = 4 + m if half else j
                        if hook and half and m % 4 == 3 and k < 2:
                            low(L, late)
                            late = None
                            if k == 1:
                                hook(0)
                if L is not None:
                    low(L, late)

            v.memset(stage[:, 0, :], 0.0).then_inc(s.gate_zero, 1)
            v.memset(cols[:], 0.0).then_inc(s.row_link, 1)
            dve.wait_ge(s.vecT_full, 1)
            v.tensor_copy(vecs[:], pA[:, 0:NV * KD])
            v.tensor_copy(nT_all[:, :, :, :].rearrange("p b h t -> p (b h t)"), pA[:, P:P + 64]).then_inc(s.vec_ready, 1)

            def from_psum(k):
                for c in range(3 * k, 3 * k + 3):
                    dve.wait_ge(s.xt_full, c + 1)
                    b, n = 2 * (c % 3), ntok(c)
                    src = acc[:, b:b + 2, :].rearrange("p a (k n) -> p (a k) n", n=P)[:, :, 0:n]
                    v.tensor_copy(xT[:, :, tok(c)], src).then_inc(s.xt_free, 1)

            from_psum(0)
            dve.wait_ge(s.w_hi, 1)
            v.tensor_tensor(wl[:, 0, :], stage[:, 0, :], wh[:, 0, :].bitcast(F32), ALU.subtract).then_inc(s.w_lo, 1)
            from_psum(1)
            for k in range(3):
                for i in range(KD * k, KD * (k + 1)):
                    low(0, i)
                if k == 0:
                    from_psum(2)
                if k == 1:
                    convert(G_AT)
            mean_square(0)
            rms_rows(0)
            for k, (o, n) in enumerate(SL):
                dve.wait_ge(s.acc_full, k + 1)
                v.tensor_tensor(rows[0:36, 0, o:o + n], bank(G_AT, k)[0:36, :], rb[0:36, o:o + n], ALU.mult).then_inc(s.acc_free, 1)

            R = lambda k, p=0: rows[p:p + H, k, :]
            done = [1]

            def link(ins):
                done[0] += 1
                ins.then_inc(s.row_link, 1)
                dve.wait_ge(s.row_link, done[0])

            def starts(r):
                return (r[:, 0:SEQ].rearrange("p (c l) -> p c l", l=P)[:, :, 0:1].rearrange("p c l -> p (c l)"),
                        r[:, SEQ:T].rearrange("p (c l) -> p c l", l=DS)[:, :, 0:1].rearrange("p c l -> p (c l)"))

            def ends(r):
                return (r[:, 0:SEQ].rearrange("p (c l) -> p c l", l=P)[:, :, P - 1:P].rearrange("p c l -> p (c l)"),
                        r[:, SEQ:T].rearrange("p (c l) -> p c l", l=DS)[:, :, DS - 1:DS].rearrange("p c l -> p (c l)"))

            def chunks(r):
                return (r[:, 0:SEQ].rearrange("p (c l) -> p c l", l=P), r[:, SEQ:T].rearrange("p (c l) -> p c l", l=DS))

            def spread(m):
                return (m[:, 0:NC].rearrange("p (c l) -> p c l", l=1).to_broadcast([H, NC, P]),
                        m[:, NC:2 * NC].rearrange("p (c l) -> p c l", l=1).to_broadcast([H, DB, DS]))

            halves = (slice(0, NC), slice(NC, 2 * NC))
            M_IN, B_L, U_MAX, BU, M_L, M_DIFF, A_, M_OUT = range(8)

            def rows_gates():
                dve.wait_ge(s.m_ld, 48)
                dve.wait_ge(s.acc_free, 3)
                link(v.tensor_scalar(R(1), R(0), bcol[0:H, :], None, ALU.add))
                link(v.tensor_scalar(R(2), R(0, 32), bcol[32:32 + H, :], None, ALU.add))
                v.scalar_tensor_tensor(out=R(3), in0=R(2), scalar=-1.0, in1=R(2), op0=ALU.mult, op1=ALU.max).then_inc(s.row_full, 1)

            def rows_cumsum():
                dve.wait_ge(s.row_act, 2)
                link(v.tensor_scalar(R(2), R(2), 0.0, None, ALU.min))
                link(v.tensor_tensor(R(4), R(2), R(3), ALU.subtract))
                link(v.memset(R(0), 1.0))
                for part in starts(R(0)):
                    link(v.memset(part, 0.0))
                link(v.tensor_tensor_scan(R(2), R(0), R(4), 0.0, ALU.mult, ALU.add))
                link(v.memset(rows[:, 7, :], 0.0))
                link(v.tensor_tensor(R(7), R(1), R(2), ALU.subtract))

            def rows_starts():
                for part, src in zip(halves, ends(R(2))):
                    link(v.tensor_copy(sm[:, B_L, part], src))
                link(v.tensor_reduce(sm[:, U_MAX, 0:NC], chunks(R(7))[0], AX.X, ALU.max))
                link(v.tensor_tensor(sm[:, BU, 0:NC], sm[:, B_L, 0:NC], sm[:, U_MAX, 0:NC], ALU.add))
                link(v.memset(sm[:, M_IN, 0:1], 0.0))
                link(v.tensor_tensor_scan(sm[:, M_IN, 1:NC], sm[:, B_L, 0:NC - 1], sm[:, BU, 0:NC - 1], 0.0, ALU.add, ALU.max))

            def rows_max():
                link(v.tensor_copy(R(3), R(7)))
                for part, at in zip(halves, starts(R(3))):
                    link(v.tensor_tensor(at, at, sm[:, M_IN, part], ALU.max))
                link(v.memset(R(0), BIG))
                for part in starts(R(0)):
                    link(v.memset(part, -BIG))
                link(v.tensor_tensor_scan(R(1), R(0), R(3), 0.0, ALU.min, ALU.max))

            def rows_args():
                parts = list(zip(spread(sm[:, M_IN, :]), chunks(R(1)), chunks(R(3))))
                link(v.tensor_tensor(parts[0][2], parts[0][0], parts[0][1], ALU.subtract))
                v.tensor_tensor(parts[1][2], parts[1][0], parts[1][1], ALU.subtract).then_inc(s.row_full, 1)
                v.tensor_tensor(R(0), R(2), R(1), ALU.add).then_inc(s.row_full, 1)
                for part, src in zip(halves, ends(R(1))):
                    link(v.tensor_copy(sm[:, M_L, part], src))
                link(v.tensor_tensor(sm[:, M_DIFF, :], sm[:, M_IN, :], sm[:, M_L, :], ALU.subtract))
                parts = list(zip(chunks(R(7)), spread(sm[:, M_L, :]), chunks(R(5))))
                link(v.tensor_tensor(parts[0][2], parts[0][0], parts[0][1], ALU.subtract))
                v.tensor_tensor(parts[1][2], parts[1][0], parts[1][1], ALU.subtract).then_inc(s.row_full, 1)
                link(v.tensor_scalar(R(4), R(1), -1.0, None, ALU.mult))
                v.tensor_tensor(sm[:, M_OUT, :], sm[:, B_L, :], sm[:, M_L, :], ALU.add).then_inc(s.row_ready, 1)

            def cols_first():
                for n, bk in enumerate((pA, pB)):
                    dve.wait_ge(s.rowT_full, n + 1)
                    for c in range(4):
                        src = bk[:, c * P:(c + 1) * P].rearrange("p (k h) -> p h k", h=32)[:, 0:H, :]
                        last = v.tensor_copy(cols[:, :, 4 * n + c, 0:4], src)
                    last.then_inc(s.cols_ready, 1)

            def cols_last():
                dve.wait_ge(s.rowT_full, 3)
                src = pA[0:TS, 0:P].rearrange("p (k h) -> p h k", h=32)[:, 0:H, :]
                v.tensor_copy(cols[0:TS, :, NC, 0:4], src)
                src = pA[:, P:P + 4 * NT].rearrange("p (c h) -> p h c", h=H)
                v.tensor_copy(cols[:, :, 0:NC, M_:M_ + 1].rearrange("p h c a -> p h (c a)"), src[:, :, 0:NC])
                v.tensor_copy(cols[0:TS, :, NC, M_:M_ + 1].rearrange("p h a -> p (h a)"), pA[0:TS, P + 4 * NC:P + 4 * NT])
                v.tensor_copy(abc[:, :, :].rearrange("p h c -> p (h c)"), pA[:, 256:256 + 2 * NC * H]).then_inc(s.cols_ready, 1)

            def up_head(at, hooks, start=None):
                for j in range(6):
                    u = at.after(j, j)
                    convert(u)
                    if j == 0 and start:
                        start()
                    for k, (o, n) in enumerate(SL):
                        dve.wait_ge(s.acc_full, u.slices(k + 1))
                        if j < 2:
                            last = v.scalar_tensor_tensor(out=work[:, j, o:o + n], in0=bank(u, k), scalar=DK ** -0.5,
                                                          in1=rb[:, o:o + n], op0=ALU.mult, op1=ALU.mult)
                        else:
                            last = v.tensor_tensor(work[:, j, o:o + n], bank(u, k), rb[:, o:o + n], ALU.mult)
                        last.then_inc(s.acc_free, 1)
                    if j in hooks:
                        hooks[j]()

            def mix(at, h, before):
                st, hc = h * NT, h * NC

                def drain(c, p):
                    f = filler(at, before, c, p)
                    if f is None or f[3] == 0:
                        return
                    u, j, k, _ = f
                    o, n = SL[k]
                    dve.wait_ge(s.acc_full, u.slices(k + 1))
                    if j is not None:
                        v.tensor_tensor(xT[:, j, o:o + n], xT[:, j, o:o + n], acc[:, 2, 0:n], ALU.add).then_inc(s.acc_free, 1)
                    else:
                        v.tensor_tensor(work[:, 6 + (c - 4) // 2, o:o + n], acc[:, 2, 0:n], rb[:, o:o + n], ALU.mult).then_inc(s.acc_free, 1)

                hs = slice(h, h + 1) if isinstance(h, int) else bass.ds(h, 1)
                v.tensor_copy(cc[:], cols[:, hs].rearrange("p a c k -> p (a c) k"))
                v.tensor_copy(ca[:], abc[:, hs].rearrange("p a c -> p (a c)"))
                v.tensor_copy(cn[:], nT_all[:, :, hs, :].rearrange("p b a t -> p (a t) b"))
                v.tensor_copy(cg[:], vecs[:, bass.ds(h * 2 + 5 * KD, 2)])
                v.memset(kvc[:, 2 * DK:2 * DK + 1], 1.0)
                v.memset(kvs[:, 2 * DK:2 * DK + 1], 1.0)
                v.memset(CT[:], 0.0).then_inc(s.cur_ready, 1)
                dve.wait_ge(s.cur_ready, h + 1)
                dve.wait_ge(s.kv_ready, st + 1)
                v.tensor_scalar(wgm[:], blocksel[:], cc[0:TS, NC, G_:G_ + 1], None, ALU.mult).then_inc(s.wgm_ready, 1)

                def scores(c):
                    n = ntok(c)
                    dve.wait_ge(s.qk_full, st + (c + 1))
                    dve.wait_ge(s.dx_ready, st + (c + 1))
                    v.tensor_tensor(dx[0:n, 0:n], acc[0:n, 3, P:P + n], dx[0:n, 0:n], ALU.mult).then_inc(s.sd_ready, 1)

                def weigh(c):
                    dve.wait_ge(s.kv_ready, st + (c + 2))
                    if c >= 1:
                        dve.wait_ge(s.up_full, hc + c)
                    v.tensor_scalar(wgv[:], kvc[:, DK:2 * DK + 1], cc[:, c, G_:G_ + 1], None, ALU.mult).then_inc(s.wgv_ready, 1)

                scores(0)
                weigh(0)
                for c in range(NT):
                    n = ntok(c)
                    if c < NC:
                        drain(c, 0)
                        dve.wait_ge(s.up_full, hc + (c + 1))
                        v.scalar_tensor_tensor(out=CT[:, :, 0:DK], in0=CT[:, :, 0:DK], scalar=ca[:, c:c + 1],
                                               in1=acc[:, 5, :].rearrange("p (a v) -> p a v", a=2), op0=ALU.mult, op1=ALU.add)
                        v.scalar_tensor_tensor(out=CT[:, :, DK:DK + 1], in0=CT[:, :, DK:DK + 1], scalar=ca[:, c:c + 1],
                                               in1=acc[:, 1, 300:302].rearrange("p (a v) -> p a v", v=1),
                                               op0=ALU.mult, op1=ALU.add).then_inc(s.ct_ready, 1)
                    dve.wait_ge(s.ia_full, st + (c + 1))
                    dve.wait_ge(s.t1_ready, st + (c + 1))
                    if c == NC:
                        v.scalar_tensor_tensor(out=qd[:], in0=acc[0:TS, 1, 340:340 + DB], scalar=1.0, in1=blocksel[:],
                                               op0=ALU.mult, op1=ALU.mult, accum_out=sc[0:TS, 6:7]).then_inc(s.smp_link, 1)
                        dve.wait_ge(s.smp_link, h * 3 + 1)
                        v.tensor_tensor(t1[0:TS, DK:DK + 1], sc[0:TS, 6:7], cc[0:TS, NC, W_:W_ + 1], ALU.mult).then_inc(s.smp_link, 1)
                        v.tensor_tensor(nn[:], cn[:], ca[:, NC:2 * NC].rearrange("p (a b) -> p a b", a=1).to_broadcast([P, 2, DB]),
                                        ALU.mult).then_inc(s.smp_link, 1)
                        dve.wait_ge(s.smp_link, h * 3 + 3)
                        v.tensor_tensor(nT_all[:, :, hs, :].rearrange("p b a t -> p (a t) b"), nn[:],
                                        acc[:, 1, 320:336].rearrange("p (t b) -> p t b", t=2), ALU.add)
                    if c >= 1:
                        dve.wait_ge(s.ht_full, st + c)
                    v.tensor_tensor(num[0:n, :], acc[0:n, 1, 0:DK + 1], t1[0:n, :], ALU.add).then_inc(s.num_ready, 1)
                    if c < NC:
                        drain(c, 1)
                        drain(c, 2)
                        scores(c + 1)
                        if c + 1 < NC:
                            weigh(c + 1)
                        drain(c, 3)
                        if filler_unit(at, before, c):
                            convert(filler_unit(at, before, c))
                        dve.wait_ge(s.upb_full, hc + (c + 1))
                        cr = cring[:, c % RING].rearrange("p t k -> p (t k)")
                        v.scalar_tensor_tensor(out=cr, in0=cr, scalar=ca[:, NC + c:NC + c + 1], in1=acc[:, 5, :],
                                               op0=ALU.mult, op1=ALU.add).then_inc(s.cb_ready, 1)
                        drain(c, 4)
                        dve.wait_ge(s.iv_full, hc + (c + 1))
                        v.tensor_copy(ivs[:, :, c * DS:(c + 1) * DS], pA[:, 0:2 * DS].rearrange("p (t s) -> p t s", t=2)).then_inc(s.iv_free, 1)
                        drain(c, 5)
                    dve.wait_ge(s.num_ready, st + (c + 1))
                    den = num[0:n, DK:DK + 1]
                    v.scalar_tensor_tensor(out=sc[0:n, 1:2], in0=den, scalar=-1.0, in1=den, op0=ALU.mult, op1=ALU.max).then_inc(s.den_link, 1)
                    dve.wait_ge(s.den_link, h * (4 * NT) + (4 * c + 1))
                    v.tensor_scalar(sc[0:n, 1:2], sc[0:n, 1:2], cc[0:n, c, T_:T_ + 1], None, ALU.max).then_inc(s.den_link, 1)
                    dve.wait_ge(s.den_link, h * (4 * NT) + (4 * c + 2))
                    v.reciprocal(sc[0:n, 2:3], sc[0:n, 1:2]).then_inc(s.den_link, 1)
                    dve.wait_ge(s.den_link, h * (4 * NT) + (4 * c + 3))
                    dve.wait_ge(s.ss_ready, st + (c + 1))
                    v.tensor_scalar(sc[0:n, 7:8], sc[0:n, 0:1], 1.0 / DK, sc[0:n, 2:3], ALU.mult, ALU.mult).then_inc(s.den_link, 1)
                    dve.wait_ge(s.den_link, h * (4 * NT) + (4 * c + 4))
                    v.tensor_scalar(sc[0:n, 3:4], sc[0:n, 7:8], sc[0:n, 2:3], EPS, ALU.mult, ALU.add).then_inc(s.ms_ready, 1)
                    if c >= 1:
                        tail(h, c - 1)
                    dve.wait_ge(s.rs0_ready, st + (c + 1))
                    v.tensor_tensor(sc[0:n, 5:6], sc[0:n, 4:5], sc[0:n, 2:3], ALU.mult).then_inc(s.rs_ready, 1)

            def tail(h, c):
                dve.wait_ge(s.ht_full, h * NT + (c + 1))
                v.tensor_copy(work[:, 0:2, tok(c)], pB[:, 0:2 * P].rearrange("p (e n) -> p e n", e=2)[:, :, 0:ntok(c)]).then_inc(s.ho_ready, 1)

            def gate(h, k):
                o, n = SL[k]
                dve.wait_ge(s.ho_ready, h * NT + 3 * (k + 1))
                dve.wait_ge(s.so_ready, h * 3 + (k + 1))
                for e in range(2):
                    last = v.scalar_tensor_tensor(out=work[:, e, o:o + n], in0=work[:, e, o:o + n], scalar=cg[:, e:e + 1],
                                                  in1=work[:, 6 + e, o:o + n], op0=ALU.mult, op1=ALU.mult)
                last.then_inc(s.hg_ready, 1)

            def gated_low(h, k):
                o, n = SL[k]
                dve.wait_ge(s.hhm_ready, h * 3 + (k + 1))
                v.tensor_tensor(hl0[:, :, o:o + n], work[:, 0:2, o:o + n], hh0[:, :, o:o + n].bitcast(F32), ALU.subtract).then_inc(s.hlm_ready, 1)

            def mix_tail(h):
                gate(h, 0)
                gate(h, 1)
                gated_low(h, 0)
                tail(h, NT - 1)
                gate(h, 2)
                gated_low(h, 1)
                gated_low(h, 2)
                dve.wait_ge(s.hlm_ready, h * 3 + 3)
                dve.wait_ge(s.ot_full, h + 1)
                v.tensor_copy(ct0[:], pA[:, :].rearrange("p (a v) -> p a v", a=2)).then_inc(s.cp_ready, 1)
                hs = slice(h, h + 1) if isinstance(h, int) else bass.ds(h, 1)
                v.tensor_copy(ncol[:, hs, :].rearrange("p a t -> p (a t)"), CT[:, :, DK:DK + 1].rearrange("p t a -> p (t a)"))

            rows_gates()
            up_head(M_AT, {0: rows_cumsum, 1: rows_starts, 2: rows_max, 3: rows_args, 4: cols_first, 5: cols_last})
            dve.wait_ge(s.m_st, 32)
            dve.wait_ge(s.cols_ready, 3)
            mix(M_AT.after(6, 6), 0, False)
            with dve.Fori(0, H - 1) as h:
                at = At(M_AT.u + 8, M_AT.t + 8, h, HEAD_DU, HEAD_DT)
                up_head(at, {}, lambda: mix_tail(h))
                mix(at.after(6, 6), h + 1, True)
            mix_tail(H - 1)
            down(M_AT.after(38, 56), 1)

            def up_ffn(at, i, q):
                for t in range(2):
                    u = at.after(2 * t, 2 * t)
                    convert(u)
                    for k, (o, n) in enumerate(SL):
                        c0 = q + (3 * t + k + 1)
                        dve.wait_ge(s.acc_full, u.slices(k + 1))
                        v.tensor_tensor(work[:, 0, o:o + n], bank(u, k), rb[:, o:o + n], ALU.mult).then_inc(s.acc_free, 1)
                        dve.wait_ge(s.acc_free, u.slices(k + 1))
                        v.tensor_tensor(work[:, 2, o:o + n], work[:, 0, o:o + n], rb[:, o:o + n], ALU.mult).then_inc(s.g2_ready, 1)
                        dve.wait_ge(s.g2_ready, c0)
                        dve.wait_ge(s.sg_ready, c0)
                        v.tensor_tensor(work[:, 2, o:o + n], work[:, 2, o:o + n], work[:, 1, o:o + n], ALU.mult).then_inc(s.g3_ready, 1)
                    u = at.after(2 * t + 1, 2 * t + 1)
                    convert(u)
                    for k, (o, n) in enumerate(SL):
                        c0 = q + (3 * t + k + 1)
                        dve.wait_ge(s.acc_full, u.slices(k + 1))
                        dve.wait_ge(s.g3_ready, c0)
                        v.tensor_tensor(work[:, 3, o:o + n], bank(u, k), work[:, 2, o:o + n], ALU.mult).then_inc(s.acc_free, 1)
                        dve.wait_ge(s.acc_free, u.slices(k + 1))
                        dve.wait_ge(s.hh_ready, c0)
                        v.tensor_tensor(HL[i % 2][:, t, o:o + n], work[:, 3, o:o + n], HH[i % 2][:, t, o:o + n].bitcast(F32),
                                        ALU.subtract).then_inc(s.hl_ready, 1)

            def ffn(base, l, L, hook=None, last_hook=None):
                q = 6 * FB * l
                mean_square(L - 1)
                rms_rows(L - 1)
                up_ffn(base, 0, q)
                if hook:
                    hook()
                with dve.Fori(0, ffn_turns // 2) as i:
                    at = At(base.u + 4, base.t + 4, i, FFN_DU, FFN_DT)
                    for e in range(2):
                        up_ffn(at.after(6 * e, 12 * e), 1 + e, i * 12 + (q + 6 + 6 * e))
                        down(at.after(6 * e + 4, 12 * e + 4))
                down(base.after(6 * FB - 2, 12 * FB - 8), L, last_hook)

            ffn(F0_AT, 0, 2)

            dve.wait_ge(s.cs_full, 1)
            v.tensor_copy(cstT.rearrange("p b r k -> p (b r k)"), pB[:, 0:P]).then_inc(s.cs_ready, 1)
            v.memset(ub[:, 0:2], 0.0)
            dve.wait_ge(s.cs_ready, 1)
            ncv = [0]

            def clink(ins):
                ncv[0] += 1
                ins.then_inc(s.cv_link, 1)
                dve.wait_ge(s.cv_link, ncv[0])

            def up_conv(at, i):
                for t in range(2):
                    ct = 2 * i + t
                    tap = lambda r: gain(6 + r, ct)
                    u = at.after(3 * t, 3 * t)
                    convert(u)
                    for k, (o, n) in enumerate(SL):
                        dve.wait_ge(s.acc_full, u.slices(k + 1))
                        v.tensor_tensor(work[:, 0, o:o + n], bank(u, k), rb[:, o:o + n], ALU.mult).then_inc(s.acc_free, 1)
                        dve.wait_ge(s.acc_free, u.slices(k + 1))
                        clink(v.tensor_tensor(work[:, 0, o:o + n], work[:, 0, o:o + n], rb[:, o:o + n], ALU.mult))
                    u = at.after(3 * t + 1, 3 * t + 1)
                    convert(u)
                    clink(v.tensor_copy(us[:, :, 0:2], cstT[:, :, :, ct:ct + 1].rearrange("p b r a -> p b (r a)")))
                    for k, (o, n) in enumerate(SL):
                        dve.wait_ge(s.acc_full, u.slices(k + 1))
                        w = min(n, SEQ - o)
                        if w < n:
                            v.tensor_tensor(us[:, :, 2:2 + DS], bank(u, k)[:, w:n].rearrange("p (b s) -> p b s", b=DB),
                                            work[:, 0, SEQ:T].rearrange("p (b s) -> p b s", b=DB), ALU.mult)
                        v.tensor_tensor(ub[:, 2 + o:2 + o + w], bank(u, k)[:, 0:w], work[:, 0, o:o + w], ALU.mult).then_inc(s.acc_free, 1)
                    dve.wait_ge(s.acc_free, u.slices(3))
                    v.tensor_copy(cpo[:, :, ct:ct + 1].rearrange("p r a -> p (r a)"), ub[:, SEQ:SEQ + 2])
                    v.tensor_copy(cso[:, :, :, ct:ct + 1].rearrange("p b r a -> p b (r a)"), us[:, :, DS:DS + 2])
                    cv = work[:, 1, 0:SEQ]
                    cvs = work[:, 1, SEQ:T].rearrange("p (b s) -> p b s", b=DB)
                    v.tensor_scalar(cv, ub[:, 0:SEQ], tap(0), None, ALU.mult)
                    clink(v.tensor_scalar(cvs, us[:, :, 0:DS], tap(0), None, ALU.mult))
                    for r in (1, 2):
                        v.scalar_tensor_tensor(out=cv, in0=ub[:, r:r + SEQ], scalar=tap(r), in1=cv, op0=ALU.mult, op1=ALU.add)
                        clink(v.scalar_tensor_tensor(out=cvs, in0=us[:, :, r:r + DS], scalar=tap(r), in1=cvs, op0=ALU.mult, op1=ALU.add))
                    clink(v.tensor_tensor(work[:, 1, :], work[:, 1, :], rb[:], ALU.mult))
                    u = at.after(3 * t + 2, 3 * t + 2)
                    convert(u)
                    for k, (o, n) in enumerate(SL):
                        dve.wait_ge(s.acc_full, u.slices(k + 1))
                        v.tensor_tensor(work[:, 2, o:o + n], bank(u, k), work[:, 1, o:o + n], ALU.mult).then_inc(s.acc_free, 1)
                        dve.wait_ge(s.acc_free, u.slices(k + 1))
                        dve.wait_ge(s.chh_ready, 6 * i + 3 * t + k + 1)
                        v.tensor_tensor(HL[i % 2][:, t, o:o + n], work[:, 2, o:o + n], HH[i % 2][:, t, o:o + n].bitcast(F32),
                                        ALU.subtract).then_inc(s.chl_ready, 1)

            mean_square(2)
            rms_rows(2)
            up_conv(C_AT, 0)
            for i in range(CB):
                if i + 1 < CB:
                    up_conv(C_AT.after(6 + 8 * i, 6 + 14 * i), i + 1)
                    down(C_AT.after(12 + 8 * i, 12 + 14 * i))
                else:
                    down(C_AT.after(8 * CB - 2, 14 * CB - 8), 3)

            def small_out():
                dve.wait_ge(s.so_full, 1)
                for n, p in enumerate((64, 8, P, 16)):
                    v.tensor_copy(outv[0:p, n, :], pA[0:p, n * P:(n + 1) * P]).then_inc(s.so_evict, 1)

            def last_mean_square(k):
                dve.wait_ge(s.st_full, 5 + k)
                whole = min(3 * k + 3, NC)
                v.tensor_scalar(v9[:, 3 * k:whole], pA[:, 3 * k:whole], 1.0 / D, EPS, ALU.mult, ALU.add).then_inc(s.v9_ready, 1)
                if whole < 3 * k + 3:
                    v.tensor_scalar(v9[0:TS, NC:NT], pA[0:TS, NC:NT], 1.0 / D, EPS, ALU.mult, ALU.add).then_inc(s.v9_ready, 1)

            ffn(F1_AT, 1, 4, small_out, last_mean_square)
            last_mean_square(1)
            dve.wait_ge(s.so_st, 64)
            for c in range(1, NT, 2):
                if c == 5:
                    last_mean_square(2)
                dve.wait_ge(s.rcol_ready, 5 + c // 3)
                dve.wait_ge(s.fin_full, c + 1)
                b = PAIR[c % 3]
                v.tensor_scalar(workf[:, c * D:(c + 1) * D].rearrange("p (a n) -> p a n", a=2), acc[:, b:b + 2, :],
                                rcol[:, c:c + 1], None, ALU.mult).then_inc(s.yd_ready, 1)

        @block.tensor
        def _(pe):
            mm = nc.tensor.matmul

            def flip(out, in_, n):
                k = in_.shape[0]
                if n == P:
                    return nc.tensor.transpose(out, in_, ident[0:k, 0:k])
                return mm(out, in_, ident[0:k, 0:k], start=True, stop=True)

            def three(out, ah, al, bh, bl, first, last):
                mm(out, ah, bh, start=first, stop=False)
                mm(out, ah, bl, start=False, stop=False)
                return mm(out, al, bh, start=False, stop=last)

            def bank(at, k):
                return acc[:, 3 * (at.t % 2) + k, 0:SL[k][1]]

            def free(at, k):
                if at.t >= 2:
                    pe.wait_ge(s.acc_free, at.slices(k - 5))

            def up(at, L=None, hooks={}):
                pe.wait_ge(s.w_lo, at.units(1))
                j = at.slot()
                for k, (o, n) in enumerate(SL):
                    free(at, k)
                    for kk in range(KD):
                        if L is not None:
                            pe.wait_ge(s.x_ready, piece_count(L, kk, k))
                        ws = slice(kk * P, (kk + 1) * P)
                        last = three(bank(at, k), wh[:, j, ws], wl[:, j, ws], xh[:, kk, o:o + n], xl[:, kk, o:o + n],
                                     kk == 0, kk == KD - 1)
                    last.then_inc(s.acc_full, 1)
                    if k in hooks:
                        hooks[k]()

            def down(at, hh, hl, L=None, wait_slice=None, hook=None):
                for half in range(2):
                    u = at.after(half, 4 * half)
                    pe.wait_ge(s.w_lo, u.units(1))
                    j = u.slot()
                    for m in range(12):
                        jj, k = (m % 4, m // 4) if half and L is not None else (m // 3, m % 3)
                        o, n = SL[k]
                        out = acc[:, (3 * (u.t % 2) + m) % 6, 0:n]
                        pe.wait_ge(s.acc_free, u.slices(m - 5))
                        if wait_slice and not half and jj == 0:
                            wait_slice(k)
                        for kk in range(2):
                            ws = slice(kk * 512 + jj * P, kk * 512 + (jj + 1) * P)
                            last = three(out, wh[:, j, ws], wl[:, j, ws], hh[:, kk, o:o + n], hl[:, kk, o:o + n], kk == 0, kk == 1)
                        last.then_inc(s.acc_full, 1)
                        if hook and half and jj == 3:
                            hook(k)

            def square_sums(L):
                pe.wait_ge(s.ssq_ready, sums_before(L, len(PIECES[L])))
                if L == 2:
                    pe.wait_ge(s.cs_ready, 1)
                for c in range(NT):
                    last = mm(pA[0:ntok(c), c:c + 1], ssq[:, tok(c)], ones[:, 0:1], start=True, stop=True)
                last.then_inc(s.st_full, 1)

            def rms_rows(L):
                pe.wait_ge(s.rcol_ready, L + 1)
                for c in range(NT):
                    n = ntok(c)
                    if c == NC:
                        pe.wait_ge(s.rb_free, 3 * L + 1)
                    out = (pA, pB, pA)[c // 4][:, (c % 4) * P:(c % 4) * P + n]
                    last = mm(out, rcol[0:n, c:c + 1].to_broadcast([n, P]), ident[0:n, 0:n], start=True, stop=True)
                    if c % 4 == 3 or c == NC:
                        last.then_inc(s.rb_full, 1)

            pe.wait_ge(s.const_ready, 1)
            pe.wait_ge(s.vec_ld, 160)
            nc.tensor.transpose(pA[:, 0:NV * KD], rows[0:NV * KD, 7, 0:P], ident[0:NV * KD, 0:NV * KD])
            nc.tensor.transpose(pA[:, P:P + 64], rows[0:64, 7, P:2 * P], ident[0:64, 0:64]).then_inc(s.vecT_full, 1)

            def x_transpose(k):
                pe.wait_ge(x_ld[k], 48)
                for c in range(3 * k, 3 * k + 3):
                    n, b = ntok(c), 2 * (c % 3)
                    if c >= 3:
                        pe.wait_ge(s.xt_free, c - 2)
                    for kk in range(KD):
                        last = nc.tensor.transpose(acc[:, b + kk // 4, (kk % 4) * P:(kk % 4) * P + n],
                                                   xin[c][:, kk * P:(kk + 1) * P], ident[0:n, 0:n])
                    last.then_inc(s.xt_full, 1)

            for k in range(3):
                x_transpose(k)
            pe.wait_ge(s.xt_free, NT)
            up(G_AT, 0, {1: lambda: square_sums(0), 2: lambda: rms_rows(0)})

            def rows_first():
                pe.wait_ge(s.row_act, 6)
                pe.wait_ge(s.row_ready, 1)
                for n, bk in enumerate((pA, pB)):
                    for c in range(4):
                        last = nc.tensor.transpose(bk[:, c * P:(c + 1) * P], rows[:, 7, tok(4 * n + c)], ident[:])
                    last.then_inc(s.rowT_full, 1)

            def rows_last():
                pe.wait_ge(s.cols_ready, 1)
                mm(pA[0:TS, 0:P], rows[:, 7, tok(NC)], ident[:], start=True, stop=True)
                for c in range(NT):
                    n = ntok(c)
                    mm(pA[0:n, P + 4 * c:P + 4 * c + 4], rows[0:H, 4, tok(c)], ident[0:H, 0:H], start=True, stop=True)
                for h in range(H):
                    last = mm(pA[:, 256 + 2 * NC * h:256 + 2 * NC * (h + 1)], ident[0:H, h:h + 1].to_broadcast([H, P]), sm[:, 6, :],
                              start=True, stop=True)
                last.then_inc(s.rowT_full, 1)

            def up_head(at, hooks={}, tail=None):
                for j in range(6):
                    up(at.after(j, j), None, {0: tail} if tail and j == 0 else {})
                    if j in hooks:
                        hooks[j]()

            def out_rows(h, c):
                n, st = ntok(c), h * NT
                pe.wait_ge(s.hn_ready, st + (c + 1))
                if c >= 1:
                    pe.wait_ge(s.ho_ready, st + c)
                for e in range(2):
                    if n == P:
                        last = nc.tensor.transpose(pB[:, e * P:e * P + n], num[:, e * P:(e + 1) * P], ident[:])
                    else:
                        last = mm(pB[:, e * P:e * P + n], num[0:n, e * P:(e + 1) * P], ident[0:n, 0:n], start=True, stop=True)
                last.then_inc(s.ht_full, 1)

            def mix(at, h, before):
                st, hc = h * NT, h * NC

                def fill(c, p):
                    f = filler(at, before, c, p)
                    if f is None:
                        return
                    u, tile, k, part = f
                    (o, n), j = SL[k], u.slot()
                    if filler_unit(at, before, c) and p == (0 if tile is not None else 1):
                        pe.wait_ge(s.w_lo, u.units(1))
                        if tile == 0:
                            pe.wait_ge(s.hlm_ready, h * 3)
                    if part != 1:
                        pe.wait_ge(s.acc_free, u.slices(k))
                    if tile is not None:
                        for kk in range(2):
                            ws = slice(kk * 512 + (tile % 4) * P, kk * 512 + (tile % 4 + 1) * P)
                            last = three(acc[:, 2, 0:n], wh[:, j, ws], wl[:, j, ws], hh0[:, kk, o:o + n], hl0[:, kk, o:o + n],
                                         kk == 0, kk == 1)
                    else:
                        for kk in range(4 * part, 4 * part + 4):
                            ws = slice(kk * P, (kk + 1) * P)
                            last = three(acc[:, 2, 0:n], wh[:, j, ws], wl[:, j, ws], xh[:, kk, o:o + n], xl[:, kk, o:o + n],
                                         kk == 0, kk == KD - 1)
                    if part != 0:
                        last.then_inc(s.acc_full, 1)

                pe.wait_ge(s.acc_free, at.slices(0))
                pe.wait_ge(s.cur_ready, h + 1)

                def key_value(c):
                    if c >= 0:
                        pe.wait_ge(s.kv_ready, st + (c + 1))
                    ts = tok(NC if c < 0 else c)
                    n = TS if c < 0 else P
                    for j in range(4):
                        last = flip(acc[0:n, 4, j * P:(j + 1) * P], work[:, 2 + j, ts], n)
                    last.then_inc(s.kvp_full, 1)

                def prepare(c):
                    n, ts = ntok(c), tok(c)
                    if c >= 1:
                        pe.wait_ge(s.sd_ready, st + c)
                    mm(acc[0:n, 3, 0:n], cc[:, c, M_:M_ + 1].to_broadcast([P, n]), ident[:, 0:n], start=True, stop=False)
                    mm(acc[0:n, 3, 0:n], identb[0:n, 0:n], causal[:] if c < NC else blockneg[:], start=False, stop=True).then_inc(s.db_full, 1)
                    if c < NC:
                        key_value(c)
                    pe.wait_ge(s.dx_ready, st + (c + 1))
                    for e in range(2):
                        last = mm(acc[0:n, 3, P:P + n], work[:, 2 + e, ts], work[:, e, ts], start=e == 0, stop=e == 1)
                    last.then_inc(s.qk_full, 1)

                key_value(-1)
                prepare(0)
                for c in range(NC):
                    ts = tok(c)
                    if c >= 1:
                        pe.wait_ge(s.ct_ready, hc + c)
                        pe.wait_ge(s.t1_ready, st + c)
                    for e in range(2):
                        last = mm(acc[:, 0, 0:DK + 1], work[:, e, ts], CT[:, e, :], start=e == 0, stop=e == 1)
                    last.then_inc(s.in_full, 1)
                    fill(c, 0)
                    pe.wait_ge(s.sd_ready, st + (c + 1))
                    pe.wait_ge(s.wgv_ready, hc + (c + 1))
                    if c >= 1:
                        pe.wait_ge(s.num_ready, st + c)
                    mm(acc[:, 1, 0:DK + 1], dx[:], kvc[:, DK:2 * DK + 1], start=True, stop=True)
                    for e in range(2):
                        last = mm(acc[:, 1, 300 + e:301 + e], kvc[:, e * P:(e + 1) * P], wgv[:, DK:DK + 1], start=True, stop=True)
                    last.then_inc(s.ia_full, 1)
                    if c >= 1:
                        pe.wait_ge(s.cb_ready, hc + c)
                    for e in range(2):
                        last = mm(acc[:, 5, e * DK:(e + 1) * DK], kvc[:, e * P:(e + 1) * P], wgv[:, 0:DK], start=True, stop=True)
                    last.then_inc(s.up_full, 1)
                    fill(c, 1)
                    if c >= 1:
                        out_rows(h, c - 1)
                    pe.wait_ge(c_ld[c % RING], h * (16 * TURNS) + 16 * (c // RING + 1))
                    if c >= 1:
                        pe.wait_ge(s.iv_free, hc + c)
                    for e in range(2):
                        for t in range(2):
                            last = nc.tensor.transpose(pA[:, e * DK + t * P:e * DK + (t + 1) * P], cring[:, c % RING, t, e * P:(e + 1) * P], ident[:])
                    last.then_inc(s.tr_full, 1)
                    fill(c, 2)
                    prepare(c + 1)
                    fill(c, 3)
                    pe.wait_ge(s.wgvb_ready, hc + (c + 1))
                    pe.wait_ge(s.ct_ready, hc + (c + 1))
                    for t in range(2):
                        last = mm(acc[:, 5, t * DK:(t + 1) * DK], wgvb[:, t * P:(t + 1) * P], kvs[:, 0:DK], start=True, stop=True)
                    last.then_inc(s.upb_full, 1)
                    fill(c, 4)
                    pe.wait_ge(s.ct0_ready, hc + (c + 1))
                    for t in range(2):
                        for e in range(2):
                            last = mm(pA[:, t * DS:(t + 1) * DS], ct0[:, e, t * P:(t + 1) * P], work[:, e, SEQ + c * DS:SEQ + (c + 1) * DS],
                                      start=e == 0, stop=e == 1)
                    last.then_inc(s.iv_full, 1)
                    fill(c, 5)
                c = NC
                pe.wait_ge(s.iv_free, hc + NC)
                pe.wait_ge(s.t1_ready, st + c)
                for t in range(2):
                    last = flip(acc[0:TS, 0, t * P:(t + 1) * P], ivs[:, t, :], TS)
                last.then_inc(s.in_full, 1)
                pe.wait_ge(s.sd_ready, st + (c + 1))
                pe.wait_ge(s.wgm_ready, h + 1)
                pe.wait_ge(s.num_ready, st + c)
                for e in range(2):
                    mm(acc[:, 1, 320 + e * DB:320 + (e + 1) * DB], kvs[:, e * P:(e + 1) * P], wgm[:], start=True, stop=True)
                mm(acc[0:TS, 1, 0:DK + 1], dx[0:TS, 0:TS], kvs[:, DK:2 * DK + 1], start=True, stop=True)
                for e in range(2):
                    last = mm(acc[0:TS, 1, 340:340 + DB], work[:, e, SEQ:T], cn[:, e, :], start=e == 0, stop=e == 1)
                last.then_inc(s.ia_full, 1)
                out_rows(h, NC - 1)
                pe.wait_ge(s.cb_ready, hc + NC)

            def mix_tail(h):
                out_rows(h, NT - 1)
                for t in range(2):
                    for e in range(2):
                        last = nc.tensor.transpose(pA[:, t * DK + e * P:t * DK + (e + 1) * P], CT[:, e, t * P:(t + 1) * P], ident[:])
                last.then_inc(s.ot_full, 1)

            up_head(M_AT, {4: rows_first, 5: rows_last})
            pe.wait_ge(s.cols_ready, 3)
            mix(M_AT.after(6, 6), 0, False)
            with pe.Fori(0, H - 1) as h:
                at = At(M_AT.u + 8, M_AT.t + 8, h, HEAD_DU, HEAD_DT)
                up_head(at, tail=lambda: mix_tail(h))
                mix(at.after(6, 6), h + 1, True)
            mix_tail(H - 1)
            down(M_AT.after(38, 56), hh0, hl0, 1, lambda k: pe.wait_ge(s.hlm_ready, (H - 1) * 3 + k + 1))

            def up_ffn(at, L=None):
                for j in range(4):
                    first = L is not None and j == 0
                    up(at.after(j, j), L if first else None,
                       {1: lambda: square_sums(L), 2: lambda: rms_rows(L)} if first else {})

            def ffn(base, l, L, hook=None, last_hook=None):
                q = 6 * FB * l
                up_ffn(base, L)
                if hook:
                    hook()
                with pe.Fori(0, ffn_turns // 2) as i:
                    at = At(base.u + 4, base.t + 4, i, FFN_DU, FFN_DT)
                    for e in range(2):
                        up_ffn(at.after(6 * e, 12 * e))
                        pe.wait_ge(s.hl_ready, i * 12 + (q + 6 + 6 * e))
                        down(at.after(6 * e + 4, 12 * e + 4), HH[e], HL[e])
                pe.wait_ge(s.hl_ready, q + 6 * FB)
                down(base.after(6 * FB - 2, 12 * FB - 8), HH[(FB - 1) % 2], HL[(FB - 1) % 2], L + 1, None, last_hook)

            ffn(F0_AT, 0, 1)
            pe.wait_ge(s.cs_ld, 16)
            nc.tensor.transpose(pB[:, 0:P], outv[:, 0, :], ident[:]).then_inc(s.cs_full, 1)

            def up_conv(at, L=None):
                for j in range(6):
                    first = L is not None and j == 0
                    up(at.after(j, j), L if first else None,
                       {1: lambda: square_sums(L), 2: lambda: rms_rows(L)} if first else {})

            up_conv(C_AT, 2)
            for i in range(CB):
                if i + 1 < CB:
                    up_conv(C_AT.after(6 + 8 * i, 6 + 14 * i))
                pe.wait_ge(s.chl_ready, 6 * (i + 1))
                at = C_AT.after(12 + 8 * i, 12 + 14 * i) if i + 1 < CB else C_AT.after(8 * CB - 2, 14 * CB - 8)
                down(at, HH[i % 2], HL[i % 2], 3 if i + 1 == CB else None)

            def small_out():
                pe.wait_ge(s.rb_free, 12)
                flip(pA[0:64, 0:P], nT_all[:, :, :, :].rearrange("p b h t -> p (b h t)"), 64)
                flip(pA[0:8, P:2 * P], ncol[:, :, :].rearrange("p h t -> p (h t)"), 8)
                flip(pA[:, 2 * P:3 * P], cso.rearrange("p b r k -> p (b r k)"), P)
                flip(pA[0:16, 3 * P:4 * P], cpo.rearrange("p r k -> p (r k)"), 16).then_inc(s.so_full, 1)

            def last_square_sums(k):
                pe.wait_ge(s.ssq_ready, sums_before(4, 4 + 4 * (k + 1)))
                if k > 0:
                    pe.wait_ge(s.v9_ready, 8 + k)
                for c in range(3 * k, 3 * k + 3):
                    last = mm(pA[0:ntok(c), c:c + 1], ssq[:, tok(c)], ones[:, 0:1], start=True, stop=True)
                last.then_inc(s.st_full, 1)

            ffn(F1_AT, 1, 3, small_out, lambda k: last_square_sums(k - 1) if k else None)
            for c in range(NT):
                n, b = ntok(c), PAIR[c % 3]
                if c == 3:
                    last_square_sums(2)
                if c < 3:
                    pe.wait_ge(s.acc_free, SLICES - (3, 1, 0)[c])
                pe.wait_ge(s.x_ready, piece_count(4, KD - 1, c // 3))
                if c >= 3:
                    pe.wait_ge(s.yd_ready if (c - 3) % 2 else s.ya_ready, (c - 3) // 2 + 1)
                for k in range(KD):
                    last = flip(acc[0:n, b + k // 4, (k % 4) * P:(k % 4 + 1) * P], xT[:, k, tok(c)], n)
                last.then_inc(s.fin_full, 1)


_IN = ["x_prompt", "x_sample", "state_mlstm_C", "state_mlstm_n", "state_mlstm_m", "state_conv", "norm_mix", "norm_ffn",
       "norm_final", "w_mlstm_in", "b_mlstm_gate", "mlstm_head_norm", "w_mlstm_out", "w_conv_in", "w_conv_taps",
       "w_conv_out", "w_ffn_gate_up", "w_ffn_down"]


def kernel(**inputs):
    import numpy as np
    import concourse.bacc as bacc
    from concourse.bass_utils import run_bass_kernel_spmd

    nc = bacc.Bacc("TRN2", target_bir_lowering=False, num_devices=1)
    arrays = {f"in_{n}": np.ascontiguousarray(inputs[n]) for n in _IN}
    args = [nc.dram_tensor(n, a.shape, mybir.dt.from_np(a.dtype), kind="ExternalInput").ap() for n, a in arrays.items()]
    shape = {n: a.shape for n, a in zip(_IN, arrays.values())}
    (B, S, D), (DB, DS, _) = shape["x_prompt"], shape["x_sample"]
    NM, _, H, DV, DK = shape["state_mlstm_C"]
    N2, _, R, _ = shape["state_conv"]
    outs = [(B, S, D), (DB, DS, D), (NM, B, H, DV, DK), (NM, B, H, DK), (NM, B, H), (N2, B, R, D),
            (NM, DB, H, DV, DK), (NM, DB, H, DK), (NM, DB, H), (N2, DB, R, D)]
    for i, o in enumerate(outs):
        args.append(nc.dram_tensor(f"out_{i}", o, F32, kind="ExternalOutput").ap())
    build(nc, *args)
    r = run_bass_kernel_spmd(nc, [arrays], core_ids=[0])
    return tuple(r.results[0][f"out_{i}"] for i in range(len(outs)))
```

```python
from contextlib import ExitStack

import concourse.bass as bass
from concourse import mybir

F32 = mybir.dt.float32
F32R = mybir.dt.float32r
BF16 = mybir.dt.bfloat16
ALU = mybir.AluOpType
ACT = mybir.ActivationFunctionType
AX = mybir.AxisListType

P = 128
EPS = 1e-6
BIG = 3.0e38
NEG = -1.0e30


class At:

    def __init__(self, u, t, i=0, du=0, dt=0):
        self.u, self.t, self.i, self.du, self.dt = u, t, i, du, dt

    def after(self, units, tiles):
        return At(self.u + units, self.t + tiles, self.i, self.du, self.dt)

    def slot(self):
        return self.u % 2

    def units(self, more):
        return self.i * self.du + (self.u + more)

    def loads(self):
        return self.i * (8 * self.du) + 16 * ((self.u + 1) // 2)

    def slices(self, more):
        return self.i * (3 * self.dt) + (3 * self.t + more)


class Semaphores:

    def __init__(self, sem):
        self.mask_ready = sem("mask_ready")
        self.const_ready = sem("const_ready")
        self.vec_ld = sem("vec_ld")
        self.n_ld = sem("n_ld")
        self.nT_full = sem("nT_full")
        self.ssqv_ready = sem("ssqv_ready")
        self.vecT_full = sem("vecT_full")
        self.vec_ready = sem("vec_ready")
        self.xt_full = sem("xt_full")
        self.xt_free = sem("xt_free")
        self.gate_zero = sem("gate_zero")
        self.gate_ld = sem("gate_ld")
        self.w_hi = sem("w_hi")
        self.w_lo = sem("w_lo")
        self.acc_full = sem("acc_full")
        self.acc_free = sem("acc_free")
        self.xh_ready = sem("xh_ready")
        self.x_ready = sem("x_ready")
        self.sq_ready = sem("sq_ready")
        self.ssq_ready = sem("ssq_ready")
        self.st_full = sem("st_full")
        self.v9_ready = sem("v9_ready")
        self.rcol_ready = sem("rcol_ready")
        self.rb_full = sem("rb_full")
        self.rb_free = sem("rb_free")
        self.row_link = sem("row_link")
        self.row_full = sem("row_full")
        self.row_act = sem("row_act")
        self.row_ready = sem("row_ready")
        self.rowT_full = sem("rowT_full")
        self.cols_ready = sem("cols_ready")
        self.so_ready = sem("so_ready")
        self.cur_ready = sem("cur_ready")
        self.db_full = sem("db_full")
        self.dx_ready = sem("dx_ready")
        self.qk_full = sem("qk_full")
        self.sd_ready = sem("sd_ready")
        self.kvp_full = sem("kvp_full")
        self.kv_ready = sem("kv_ready")
        self.wgv_ready = sem("wgv_ready")
        self.in_full = sem("in_full")
        self.t1_ready = sem("t1_ready")
        self.ia_full = sem("ia_full")
        self.num_ready = sem("num_ready")
        self.up_full = sem("up_full")
        self.ct_ready = sem("ct_ready")
        self.wgm_ready = sem("wgm_ready")
        self.wgvb_ready = sem("wgvb_ready")
        self.tr_full = sem("tr_full")
        self.ct0_ready = sem("ct0_ready")
        self.iv_full = sem("iv_full")
        self.iv_free = sem("iv_free")
        self.upb_full = sem("upb_full")
        self.cb_ready = sem("cb_ready")
        self.ss_ready = sem("ss_ready")
        self.ms_ready = sem("ms_ready")
        self.rs0_ready = sem("rs0_ready")
        self.rs_ready = sem("rs_ready")
        self.hn_ready = sem("hn_ready")
        self.ht_full = sem("ht_full")
        self.ho_ready = sem("ho_ready")
        self.hg_ready = sem("hg_ready")
        self.hhm_ready = sem("hhm_ready")
        self.hlm_ready = sem("hlm_ready")
        self.den_link = sem("den_link")
        self.smp_link = sem("smp_link")
        self.ot_full = sem("ot_full")
        self.cp_ready = sem("cp_ready")
        self.cp_st = sem("cp_st")
        self.sg_ready = sem("sg_ready")
        self.g2_ready = sem("g2_ready")
        self.g3_ready = sem("g3_ready")
        self.hh_ready = sem("hh_ready")
        self.hl_ready = sem("hl_ready")
        self.chh_ready = sem("chh_ready")
        self.chl_ready = sem("chl_ready")
        self.cv_link = sem("cv_link")
        self.m_ld = sem("m_ld")
        self.m_st = sem("m_st")
        self.fin_full = sem("fin_full")
        self.ya_ready = sem("ya_ready")
        self.yd_ready = sem("yd_ready")
        self.y_st = sem("y_st")
        self.so_full = sem("so_full")
        self.so_evict = sem("so_evict")
        self.so_st = sem("so_st")
        self.cs_ld = sem("cs_ld")
        self.cs_full = sem("cs_full")
        self.cs_ready = sem("cs_ready")


def build(nc, x_prompt, x_sample, state_C, state_n, state_m, state_conv, norm_mix, norm_ffn, norm_final,
          w_mlstm_in, b_gate, head_norm, w_mlstm_out, w_conv_in, w_conv_taps, w_conv_out, w_gate_up, w_down,
          y_prompt, y_sample, C_prompt, n_prompt, m_prompt, conv_prompt, C_sample, n_sample, m_sample, conv_sample):
    D = x_prompt.shape[2]
    SEQ = x_prompt.shape[1]
    DB, DS = x_sample.shape[0], x_sample.shape[1]
    H = state_C.shape[2]
    DK = state_C.shape[4]
    F = w_down.shape[1]
    KD = D // P
    TS = DB * DS
    T = SEQ + TS
    NC = SEQ // P
    NT = NC + 1
    SL = [(0, 384), (384, 384), (768, T - 768)]
    FB = F // 256
    CB = D // 256
    RING = 4
    assert D == 1024 and SEQ == 1024 and TS == 64 and H == 4 and DK == 256 and KD == 8 and F % 256 == 0

    def tok(c):
        return slice(c * P, min((c + 1) * P, T))

    def ntok(c):
        return min(P, T - c * P)

    G_AT = At(0, 0)
    M_AT = G_AT.after(1, 1)
    F0_AT = M_AT.after(H * 10, H * 16)
    C_AT = F0_AT.after(FB * 6, FB * 12)
    F1_AT = C_AT.after(CB * 8, CB * 14)
    UNITS = F1_AT.u + FB * 6
    SLICES = 3 * (F1_AT.t + FB * 12)
    assert (F1_AT.t + FB * 12) % 2 == 1
    PAIR = (4, 0, 2)
    X_PAIR = (0, 2, 4, 0, 2, 4, 2, 4, None)

    ctx = ExitStack()
    with ctx:
        def sb(name, shape, dt=F32, c=ctx):
            return c.enter_context(nc.sbuf_tensor(name, shape, dt))

        def sem(name):
            return ctx.enter_context(nc.semaphore(name))

        xT = sb("xT", [P, KD, T])
        xh = sb("xh", [P, KD, T], F32R)
        xl = sb("xl", [P, KD, T], F32R)
        stage = sb("stage", [P, 2, 1024])
        wh = sb("wh", [P, 2, 1024], F32R)
        wl = sb("wl", [P, 2, 1024], F32R)
        rb = sb("rb", [P, T])
        work = sb("work", [P, 8, T])
        workf = work[:, :, :].rearrange("p a t -> p (a t)")
        ssq = work[:, 6, :]
        ident = sb("ident", [P, P])
        identb = sb("identb", [P, P], BF16)
        causal = sb("causal", [P, P], BF16)
        blockneg = sb("blockneg", [TS, TS], BF16)
        blocksel = sb("blocksel", [TS, DB])
        ones = sb("ones", [P, 1])
        halfneg = sb("halfneg", [P, NT])
        rcol = sb("rcol", [P, NT])
        v9 = sb("v9", [P, NT])
        NV = 9
        vecs = sb("vecs", [P, NV * KD])
        nT_all = sb("nT_all", [P, DB, H, 2])
        cols = sb("cols", [P, H, NT, 5])
        abc = sb("abc", [P, H, 2 * NC])
        ncol = sb("ncol", [P, H, 2])
        U_, W_, T_, G_, M_ = range(5)

        def gain(v, k):
            return vecs[:, v * KD + k:v * KD + k + 1]

        LAYER_GAIN = [0, 2, 1, 3, 4]

        with ExitStack() as c1:
            rows = sb("rows", [P, 8, T], F32, c1)
            sm = sb("sm", [4, 8, 2 * NC], F32, c1)
            bcol = sb("bcol", [P, 1], F32, c1)
        xin = [rows[:, :, :].rearrange("p a t -> p (a t)")[:, c * D:(c + 1) * D] for c in range(NC - 1)] + \
            [workf[:, 0:D], rb[0:TS, 0:D]]
        hh0 = sb("hh0", [P, 2, T], F32R)
        hl0 = sb("hl0", [P, 2, T], F32R)
        with ExitStack() as c2:
            CT = sb("CT", [P, 2, DK + 1], F32, c2)
            cring = sb("cring", [P, RING, 2, DK], F32, c2)
            ct0 = sb("ct0", [P, 2, DK], F32, c2)
            kvc = sb("kvc", [P, 2 * DK + 1], F32, c2)
            kvs = sb("kvs", [TS, 2 * DK + 1], F32, c2)
            wgv = sb("wgv", [P, DK + 1], F32, c2)
            wgvb = sb("wgvb", [TS, DK], F32, c2)
            dx = sb("dx", [P, P], F32, c2)
            t1 = sb("t1", [P, DK + 1], F32, c2)
            num = sb("num", [P, DK + 1], F32, c2)
            ivs = sb("ivs", [P, 2, TS], F32, c2)
            cc = sb("cc", [P, NT, 5], F32, c2)
            ca = sb("ca", [P, 2 * NC], F32, c2)
            cn = sb("cn", [P, 2, DB], F32, c2)
            cg = sb("cg", [P, 2], F32, c2)
            nn = sb("nn", [P, 2, DB], F32, c2)
            wgm = sb("wgm", [TS, DB], F32, c2)
            qd = sb("qd", [TS, DB], F32, c2)
            sc = sb("sc", [P, 8], F32, c2)
        with ExitStack() as c3:
            hh1 = sb("hh1", [P, 2, T], F32R, c3)
            hl1 = sb("hl1", [P, 2, T], F32R, c3)
        HH, HL = [hh0, hh1], [hl0, hl1]
        ub = workf[:, 3 * T:3 * T + SEQ + 2]
        us = workf[:, 4 * T:4 * T + DB * (DS + 2)].rearrange("p (b s) -> p b s", b=DB)
        cstT = workf[:, 4 * T + 128:4 * T + 256].rearrange("p (b r k) -> p b r k", b=DB, r=2)
        cso = workf[:, 4 * T + 256:4 * T + 384].rearrange("p (b r k) -> p b r k", b=DB, r=2)
        cpo = workf[:, 4 * T + 384:4 * T + 400].rearrange("p (r k) -> p r k", r=2)
        outv = workf[:, 4 * T + 512:4 * T + 512 + 4 * P].rearrange("p (a n) -> p a n", a=4)

        acc = ctx.enter_context(nc.psum_tensor("acc", [P, 6, 512], F32))
        pA = ctx.enter_context(nc.psum_tensor("pA", [P, 512], F32))
        pB = ctx.enter_context(nc.psum_tensor("pB", [P, 512], F32))

        s = Semaphores(sem)
        w_ld = [sem("w_ld0"), sem("w_ld1")]
        x_ld = [sem(f"x_ld{c}") for c in range(NT)]
        c_ld = [sem(f"c_ld{j}") for j in range(RING)]
        c_st = [sem(f"c_st{j}") for j in range(RING)]
        TURNS = DB // RING

        w_in_v = w_mlstm_in[0].rearrange("(k p) n -> p k n", p=P)
        w_conv_v = w_conv_in[0].rearrange("(k p) n -> p k n", p=P)
        w_gu_v = [w_gate_up[l].rearrange("(k p) n -> p k n", p=P) for l in range(2)]
        stage_col = [stage[:, j, :].rearrange("p (k n) -> p k n", k=KD) for j in range(2)]
        stage_row = [stage[:, j, :].rearrange("p (k n) -> p k n", k=2) for j in range(2)]
        gate0 = 4 * D

        ffn_turns = FB - 1
        assert ffn_turns % 2 == 0
        FFN_DU, FFN_DT = 12, 24
        def by_slices(L, half):
            return L is not None and (half == 1 or L == 1)

        def down_pieces(L):
            whole = [(j, k) for k in range(3) for j in range(4)] if by_slices(L, 0) else [(j, None) for j in range(4)]
            return whole + [(j, k) for k in range(3) for j in range(4, KD)]

        PIECES = [[(j, k) for k in range(3) for j in range(KD)]] + [down_pieces(L) for L in range(1, 5)]

        def pieces_before(L, i):
            return sum(len(x) for x in PIECES[:L]) + i

        def by_vector(L, k):
            return L in (0, 4) and k == 2

        def sums_before(L, i, vector=False):
            every = [(l, x) for l in range(L) for x in PIECES[l]] + [(L, x) for x in PIECES[L][:i]]
            return sum(j > 0 and by_vector(l, k) == vector for l, (j, k) in every)

        def square_at(L, i):
            j, k = PIECES[L][i]
            _, span = piece_span(L, i)
            if j == 0:
                return ssq[:, span]
            if L == 0:
                return work[:, (0, 1, 2, 3, 4, 5, 7, 1)[j], span]
            if by_vector(L, k):
                n = SL[k][1]
                return rb[:, (j - 4) * n:(j - 3) * n] if j < 7 else work[:, 7, span]
            return work[:, 5 + 2 * (sums_before(L, i) % 2), span]

        def piece_count(L, j, k):
            return pieces_before(L, next(i for i, x in enumerate(PIECES[L]) if x in ((j, k), (j, None)))) + 1

        def piece_span(L, i):
            j, k = PIECES[L][i]
            o, n = (0, T) if k is None else SL[k]
            return j, slice(o, o + n)

        HEAD_DU, HEAD_DT = 10, 16

        def filler(at, before, c, p):
            if not before:
                if p != 3 and (p != 5 or c % 2 == 0):
                    return None
                e, i = c // 4, c % 4 + (c % 4) // 2 + (p == 5)
                return at.after(e, e), None, e, i // 2, i % 2
            if c < 4:
                i = 6 * c + p
                return at.after(c // 2, i // 3), i // 3, None, i % 3, None
            if p % 2 == 0:
                return None
            e, i = (c - 4) // 2, 3 * (c % 2) + p // 2
            return at.after(2 + e, 8 + e), None, e, i // 2, i % 2

        def filler_unit(at, before, c):
            if not before:
                return None if c % 4 else at.after(c // 4, c // 4)
            if c % 2:
                return None
            return at.after(c // 2, 2 * c) if c < 4 else at.after(c // 2, 8 + (c - 4) // 2)

        block = ctx.enter_context(nc.Block())

        @block.sync
        def _(sp):
            def load(at, src, row):
                if at.u >= 2:
                    sp.wait_ge(s.w_lo, at.units(-1))
                j = at.slot()
                sp.dma_start((stage_row if row else stage_col)[j], src).then_inc(w_ld[j], 16)

            def load_up(at, w, col):
                load(at, w[:, :, bass.ds(col, P)] if not isinstance(col, int) else w[:, :, col:col + P], False)

            def load_down(at, w, i):
                v = w.rearrange("(i k p) n -> p i k n", k=2, p=P)
                for half in range(2):
                    cs = slice(half * 512, (half + 1) * 512)
                    src = v[:, i, :, cs] if isinstance(i, int) else \
                        v[:, bass.ds(i, 1), :, cs].rearrange("p a k n -> p (a k) n")
                    load(at.after(half, 0), src, True)

            def load_up_head(at, h, first, last, hooks={}):
                for j in range(first, last):
                    if j in hooks:
                        hooks[j]()
                    load_up(at.after(j - first, 0), w_in_v, h * 256 + ((j // 2) * D + (j % 2) * P))

            def load_up_ffn(at, l, i):
                for j in range(4):
                    load_up(at.after(j, 0), w_gu_v[l], i * 256 + ((j % 2) * F + (j // 2) * P))

            def load_up_conv(at, i):
                for j in range(6):
                    which = [1, 2, 0][j % 3]
                    load_up(at.after(j, 0), w_conv_v, i * 256 + which * D + (j // 3) * P)

            def store_head(h):
                sp.wait_ge(s.cp_ready, h + 1)
                dst = C_prompt[0, 0].rearrange("h (t p) k -> p h t k", p=P)
                dst = dst[:, h] if isinstance(h, int) else dst[:, bass.ds(h, 1)].rearrange("p a t k -> p (a t) k")
                sp.dma_start(dst, ct0[:]).then_inc(s.cp_st, 16)

            def load_x(k):
                for c in range(3 * k, 3 * k + 3):
                    src = x_prompt[0, c * P:(c + 1) * P, :] if c < NC else x_sample.rearrange("b s d -> (b s) d")
                    sp.dma_start(xin[c], src).then_inc(x_ld[c], 16)

            load_x(0)
            sp.wait_ge(s.gate_zero, 1)
            with nc.allow_non_contiguous_dma(reason="eight columns"):
                sp.dma_start(stage_col[0][:, :, 0:H], w_in_v[:, :, gate0:gate0 + H]).then_inc(s.gate_ld, 16)
                sp.dma_start(stage_col[0][:, :, 32:32 + H], w_in_v[:, :, gate0 + H:gate0 + 2 * H]).then_inc(s.gate_ld, 16)
            load_x(1)
            load_x(2)
            load_up_head(M_AT, 0, 0, 8)
            with sp.Fori(0, H - 1) as h:
                at = At(M_AT.u + 8, 0, h, HEAD_DU, HEAD_DT)
                load_up_head(at, h + 1, 0, 6, {4: lambda: store_head(h)})
                load_down(at.after(6, 0), w_mlstm_out[0], h)
                load_up_head(at.after(8, 0), h + 1, 6, 8)
            load_down(At(M_AT.u + 38, 0), w_mlstm_out[0], H - 1)
            store_head(H - 1)

            def load_ffn(base, l):
                load_up_ffn(base, l, 0)
                with sp.Fori(0, ffn_turns // 2) as i:
                    at = At(base.u + 4, 0, i, FFN_DU, FFN_DT)
                    for e in range(2):
                        load_up_ffn(at.after(6 * e, 0), l, i * 2 + (1 + e))
                        load_down(at.after(6 * e + 4, 0), w_down[l], i * 2 + e)
                load_down(base.after(6 * FB - 2, 0), w_down[l], FB - 1)

            load_ffn(F0_AT, 0)
            load_up_conv(C_AT, 0)
            for i in range(CB):
                if i + 1 < CB:
                    load_up_conv(C_AT.after(6 + 8 * i, 0), i + 1)
                load_down(C_AT.after(8 * i + 12 if i + 1 < CB else 8 * CB - 2, 0), w_conv_out[0], i)
            load_ffn(F1_AT, 1)

            for c in range(NT):
                sp.wait_ge(s.yd_ready if c % 2 else s.ya_ready, c // 2 + 1)
                if c < NC:
                    sp.dma_start(y_prompt[0, c * P:(c + 1) * P, :], workf[:, c * D:(c + 1) * D]).then_inc(s.y_st, 16)
                else:
                    sp.dma_start(y_sample.rearrange("b s d -> (b s) d"), rb[0:TS, 0:D]).then_inc(s.y_st, 16)
            sp.wait_ge(s.y_st, 16 * NT)
            sp.wait_ge(s.cp_st, 16 * H)

        @block.gpsimd
        def _(pool):
            g = nc.gpsimd
            g.memset(ident[:], 0.0).then_inc(s.mask_ready, 1)
            g.memset(identb[:], 0.0).then_inc(s.mask_ready, 1)
            g.memset(causal[:], 0.0).then_inc(s.mask_ready, 1)
            g.memset(blockneg[:], 0.0).then_inc(s.mask_ready, 1)
            g.memset(blocksel[:], 1.0).then_inc(s.mask_ready, 1)
            g.memset(ones[:], 1.0).then_inc(s.mask_ready, 1)
            g.memset(halfneg[:], -0.5).then_inc(s.mask_ready, 1)
            pool.wait_ge(s.mask_ready, 7)
            for m in (ident, identb):
                g.affine_select(out=m[:], in_=m[:], compare_op=ALU.not_equal, fill=1.0, base=0,
                                pattern=[[-1, P]], channel_multiplier=1).then_inc(s.mask_ready, 1)
            g.affine_select(out=causal[:], in_=causal[:], compare_op=ALU.is_ge, fill=NEG, base=0,
                            pattern=[[1, P]], channel_multiplier=-1).then_inc(s.mask_ready, 1)
            g.affine_select(out=blockneg[:], in_=blockneg[:], compare_op=ALU.is_ge, fill=NEG, base=0,
                            pattern=[[1, TS]], channel_multiplier=-1).then_inc(s.mask_ready, 1)
            bn = blockneg[:, :].rearrange("p (b s) -> p b s", b=DB)
            pool.wait_ge(s.mask_ready, 11)
            g.affine_select(out=bn, in_=bn, compare_op=ALU.is_ge, fill=NEG, base=0,
                            pattern=[[-DS, DB], [0, DS]], channel_multiplier=1).then_inc(s.mask_ready, 1)
            g.affine_select(out=blocksel[:], in_=blocksel[:], compare_op=ALU.is_ge, fill=0.0, base=0,
                            pattern=[[-DS, DB]], channel_multiplier=1).then_inc(s.mask_ready, 1)
            pool.wait_ge(s.mask_ready, 13)
            g.affine_select(out=bn, in_=bn, compare_op=ALU.is_ge, fill=NEG, base=DS - 1,
                            pattern=[[DS, DB], [0, DS]], channel_multiplier=-1).then_inc(s.mask_ready, 1)
            g.affine_select(out=blocksel[:], in_=blocksel[:], compare_op=ALU.is_ge, fill=0.0, base=DS - 1,
                            pattern=[[DS, DB]], channel_multiplier=-1).then_inc(s.mask_ready, 1)
            pool.wait_ge(s.mask_ready, 15)
            g.memset(v9[:], 1.0).then_inc(s.const_ready, 1)

            def rstd(L):
                pool.wait_ge(s.v9_ready, 2 * (L + 1))
                g.tensor_tensor(rcol[:], v9[:], halfneg[:], ALU.pow).then_inc(s.rcol_ready, 1)

            def sum_piece(L, i):
                j, span = piece_span(L, i)
                if j == 0 or by_vector(L, PIECES[L][i][1]):
                    return
                before = sums_before(L, i)
                pool.wait_ge(s.sq_ready, pieces_before(L, i) + 1)
                if before > 0:
                    pool.wait_ge(s.ssq_ready, before)
                g.tensor_tensor(ssq[:, span], ssq[:, span], square_at(L, i), ALU.add).then_inc(s.ssq_ready, 1)

            def sums(L):
                for i in range(len(PIECES[L])):
                    sum_piece(L, i)

            def head(v, h):
                return v[:, h] if isinstance(h, int) else v[:, bass.ds(h, 1)].rearrange("p a t k -> p (a t) k")

            def c_load(h, b):
                pool.dma_start(cring[:, b % RING], head(state_C[0, b].rearrange("h (t p) k -> p h t k", p=P), h)).then_inc(c_ld[b % RING], 16)

            def c_store(h, b):
                pool.dma_start(head(C_sample[0, b].rearrange("h (t p) k -> p h t k", p=P), h), cring[:, b % RING]).then_inc(c_st[b % RING], 16)

            def mix(h, last):
                for c in range(NT):
                    n = ntok(c)
                    pool.wait_ge(s.ms_ready, h * NT + (c + 1))
                    if c < NC:
                        pool.wait_ge(s.cb_ready, h * NC + (c + 1))
                    ahead = c + 2
                    if RING <= ahead < NC:
                        pool.wait_ge(c_st[ahead % RING], h * (16 * TURNS) + 16 * (ahead // RING))
                    if c == NC and not last:
                        for b in range(RING):
                            pool.wait_ge(c_st[b], h * (16 * TURNS) + 16 * TURNS)
                    g.tensor_tensor(sc[0:n, 4:5], sc[0:n, 3:4], halfneg[0:n, 0:1], ALU.pow).then_inc(s.rs0_ready, 1)
                    if c < NC:
                        c_store(h, c)
                    if ahead < NC:
                        c_load(h, ahead)
                    if c == NC and not last:
                        for b in range(2):
                            c_load(h + 1, b)

            sums(0)
            rstd(0)
            pool.wait_ge(s.cols_ready, 3)
            pool.wait_ge(s.m_st, 32)
            c_load(0, 0)
            c_load(0, 1)
            with pool.Fori(0, H - 1) as h:
                mix(h, False)
            mix(H - 1, True)
            for L in range(1, 4):
                sums(L)
                rstd(L)
            for j in range(RING):
                pool.wait_ge(c_st[j], 16 * TURNS * H)
            pool.wait_ge(s.so_evict, 1)
            pool.dma_start(n_sample[0].rearrange("b h (t p) -> (b h t) p", p=P), outv[0:64, 0, :]).then_inc(s.so_st, 16)
            pool.wait_ge(s.so_evict, 2)
            pool.dma_start(n_prompt[0, 0].rearrange("h (t p) -> (h t) p", p=P), outv[0:8, 1, :]).then_inc(s.so_st, 16)
            pool.wait_ge(s.so_evict, 3)
            pool.dma_start(conv_sample[0].rearrange("b r (k p) -> (b r k) p", p=P), outv[:, 2, :]).then_inc(s.so_st, 16)
            pool.wait_ge(s.so_evict, 4)
            pool.dma_start(conv_prompt[0, 0].rearrange("r (k p) -> (r k) p", p=P), outv[0:16, 3, :]).then_inc(s.so_st, 16)
            def last_rstd(k):
                pool.wait_ge(s.v9_ready, 9 + k + (k == 2))
                cs = slice(3 * k, 3 * k + 3)
                g.tensor_tensor(rcol[:, cs], v9[:, cs], halfneg[:, cs], ALU.pow).then_inc(s.rcol_ready, 1)

            for i, (j, k) in enumerate(PIECES[4]):
                sum_piece(4, i)
                if j == KD - 1 and k > 0:
                    last_rstd(k - 1)
            last_rstd(2)
            pool.wait_ge(s.so_st, 64)

        @block.scalar
        def _(act):
            a = nc.scalar

            def convert(at):
                nx = at.after(1, 0)
                if nx.u >= UNITS:
                    return
                act.wait_ge(w_ld[nx.slot()], nx.loads())
                if nx.u >= 2:
                    act.wait_ge(s.acc_full, at.slices(0))
                a.activation(wh[:, nx.slot(), :], stage[:, nx.slot(), :], ACT.Copy).then_inc(s.w_hi, 1)

            def square(L, i):
                j, span = piece_span(L, i)
                if L == 4 and by_vector(L, PIECES[L][i][1]):
                    act.wait_ge(s.ssq_ready, sums_before(4, 4))
                elif L > 0 and j > 0:
                    act.wait_ge(s.ssq_ready, sums_before(L, i) - 1)
                elif j == KD - 1:
                    vector = by_vector(L, PIECES[L][i][1])
                    act.wait_ge(s.ssqv_ready if vector else s.ssq_ready, sums_before(L, i, vector) - 5)
                a.activation(square_at(L, i), xT[:, j, span], ACT.Square).then_inc(s.sq_ready, 1)

            def high(L, i):
                j, span = piece_span(L, i)
                a.activation(xh[:, j, span], xT[:, j, span], ACT.Copy, scale=gain(LAYER_GAIN[L], j)).then_inc(s.xh_ready, 1)

            def down(at, L=None, first_hook=None):
                for half in range(2):
                    u = at.after(half, 4 * half)
                    convert(u)
                    if L is None:
                        continue
                    for m in range(12 if by_slices(L, half) else 4):
                        i = half * (len(PIECES[L]) - 12) + m
                        act.wait_ge(s.acc_free, u.slices(m + 1 if by_slices(L, half) else 3 * (m + 1)))
                        if L < 4:
                            high(L, i)
                        square(L, i)
                        if first_hook and not half and m == 3:
                            first_hook()

            at_row = 0
            for v in (norm_mix, norm_ffn, norm_final.rearrange("(a d) -> a d", a=1), head_norm, w_conv_taps[0]):
                n = v.shape[0] * KD
                act.dma_start(rows[at_row:at_row + n, 7, 0:P], v.rearrange("a (k p) -> (a k) p", p=P)).then_inc(s.vec_ld, 16)
                at_row += n
            act.dma_start(rows[0:64, 7, P:2 * P], state_n[0].rearrange("b h (t p) -> (b h t) p", p=P)).then_inc(s.n_ld, 16)
            with nc.allow_non_contiguous_dma(reason="a few words"):
                act.dma_start(sm[0:H, 0, NC:2 * NC], state_m[0].rearrange("b h -> h b")).then_inc(s.m_ld, 16)
                act.dma_start(bcol[0:H, :], b_gate[0, 0:H].rearrange("(h a) -> h a", a=1)).then_inc(s.m_ld, 16)
                act.dma_start(bcol[32:32 + H, :], b_gate[0, H:2 * H].rearrange("(h a) -> h a", a=1)).then_inc(s.m_ld, 16)

            act.wait_ge(s.gate_ld, 32)
            a.activation(wh[:, 0, :], stage[:, 0, :], ACT.Copy).then_inc(s.w_hi, 1)
            act.wait_ge(s.vec_ready, 1)
            def first_high(k):
                act.wait_ge(s.xt_free, 3 * (k + 1))
                for i in range(KD * k, KD * (k + 1)):
                    high(0, i)

            def first_square(k):
                for i in range(KD * k, KD * (k + 1)):
                    square(0, i)

            first_high(0)
            first_square(0)
            first_high(1)
            first_high(2)
            convert(G_AT)
            first_square(1)
            first_square(2)
            R = lambda k, p=0, n=H: rows[p:p + n, k, :]

            def row_log():
                act.wait_ge(s.row_full, 1)
                a.activation(R(3), R(3), ACT.Exp, scale=-1.0).then_inc(s.row_act, 1)
                act.wait_ge(s.row_act, 1)
                a.activation(R(3), R(3), ACT.Ln, bias=1.0).then_inc(s.row_act, 1)

            def row_exps():
                act.wait_ge(s.row_full, 2)
                a.activation(R(7, 32), R(3), ACT.Exp).then_inc(s.row_act, 1)
                act.wait_ge(s.row_full, 3)
                a.activation(R(7, 64), R(0), ACT.Exp, scale=-1.0).then_inc(s.row_act, 1)
                act.wait_ge(s.row_full, 4)
                a.activation(R(7, 96), R(5), ACT.Exp).then_inc(s.row_act, 1)
                a.activation(sm[:, 6, :], sm[:, 5, :], ACT.Exp).then_inc(s.row_act, 1)
                act.wait_ge(s.row_ready, 1)
                with nc.allow_non_contiguous_dma(reason="a few words"):
                    act.dma_start(m_prompt[0].rearrange("b h -> h b"), sm[:, 7, NC - 1:NC]).then_inc(s.m_st, 16)
                    act.dma_start(m_sample[0].rearrange("b h -> h b"), sm[:, 7, NC:2 * NC]).then_inc(s.m_st, 16)
                act.wait_ge(s.m_st, 32)

            def up_head(at, hooks):
                for j in range(6):
                    convert(at.after(j, j))
                    if j in hooks:
                        hooks[j]()

            def mix(at, h, before):
                st = h * NT
                act.wait_ge(s.cur_ready, h + 1)

                def kv(c):
                    act.wait_ge(s.kvp_full, st + (c + 2))
                    if c >= 1:
                        act.wait_ge(s.up_full, h * NC + c)
                    if c < 0:
                        a.activation(kvs[:, 0:2 * DK], acc[0:TS, 4, :], ACT.Copy).then_inc(s.kv_ready, 1)
                    else:
                        a.activation(kvc[:, 0:2 * DK], acc[:, 4, :], ACT.Copy).then_inc(s.kv_ready, 1)

                def decay(c):
                    n = ntok(c)
                    act.wait_ge(s.db_full, st + (c + 1))
                    if c >= 1:
                        act.wait_ge(s.ia_full, st + c)
                    a.activation(dx[0:n, 0:n], acc[0:n, 3, 0:n], ACT.Exp, bias=cc[0:n, c, U_:U_ + 1]).then_inc(s.dx_ready, 1)

                kv(-1)
                decay(0)
                kv(0)
                for c in range(NT):
                    n = ntok(c)
                    act.wait_ge(s.in_full, st + (c + 1))
                    if c >= 1:
                        act.wait_ge(s.ss_ready, st + c)
                    w = DK + 1 if c < NC else DK
                    a.activation(t1[0:n, 0:w], acc[0:n, 0, 0:w], ACT.Copy, scale=cc[0:n, c, W_:W_ + 1]).then_inc(s.t1_ready, 1)
                    if c < NC:
                        act.wait_ge(s.wgm_ready, h + 1)
                        if c >= 1:
                            act.wait_ge(s.upb_full, h * NC + c)
                        a.activation(wgvb[:], kvs[:, DK:2 * DK], ACT.Copy, scale=wgm[:, c:c + 1]).then_inc(s.wgvb_ready, 1)
                        if filler_unit(at, before, c):
                            convert(filler_unit(at, before, c))
                        act.wait_ge(s.tr_full, h * NC + (c + 1))
                        if c >= 1:
                            act.wait_ge(s.iv_full, h * NC + c)
                        a.activation(ct0[:], pA[:, :].rearrange("p (a v) -> p a v", a=2), ACT.Copy).then_inc(s.ct0_ready, 1)
                        decay(c + 1)
                        if c + 1 < NC:
                            kv(c + 1)
                    else:
                        past = at.after(4, 10) if before else at.after(2, 2)
                        act.wait_ge(s.acc_free, past.slices(0))
                        gate_sigmoid(0)
                    act.wait_ge(s.num_ready, st + (c + 1))
                    a.activation(t1[0:n, 0:DK], num[0:n, 0:DK], ACT.Square, accum_out=sc[0:n, 0:1]).then_inc(s.ss_ready, 1)
                    if c == NC:
                        gated_high(h, 0)
                    act.wait_ge(s.rs_ready, st + (c + 1))
                    a.activation(num[0:n, 0:DK], num[0:n, 0:DK], ACT.Copy, scale=sc[0:n, 5:6]).then_inc(s.hn_ready, 1)

            def gate_sigmoid(k):
                o, n = SL[k]
                a.activation(work[:, 6:8, o:o + n], work[:, 6:8, o:o + n], ACT.Sigmoid).then_inc(s.so_ready, 1)

            def gated_high(h, k):
                o, n = SL[k]
                act.wait_ge(s.hg_ready, h * 3 + (k + 1))
                a.activation(hh0[:, :, o:o + n], work[:, 0:2, o:o + n], ACT.Copy).then_inc(s.hhm_ready, 1)

            def gate_next(h):
                gate_sigmoid(1)
                gated_high(h, 1)
                gate_sigmoid(2)

            def stored(h):
                act.wait_ge(s.cp_st, h * 16 + 16)

            up_head(M_AT, {1: row_log, 4: row_exps})
            mix(M_AT.after(6, 6), 0, False)
            with act.Fori(0, H - 1) as h:
                at = At(M_AT.u + 8, M_AT.t + 8, h, HEAD_DU, HEAD_DT)
                up_head(at, {0: lambda: (gate_next(h), gated_high(h, 2)), 5: lambda: stored(h)})
                mix(at.after(6, 6), h + 1, True)
            gate_next(H - 1)
            down(M_AT.after(38, 56), 1, lambda: gated_high(H - 1, 2))

            act.dma_start(outv[:, 0, :], state_conv[0].rearrange("b r (k p) -> (b r k) p", p=P)).then_inc(s.cs_ld, 16)

            def up_ffn(at, i, q):
                for t in range(2):
                    u = at.after(2 * t, 2 * t)
                    convert(u)
                    for k, (o, n) in enumerate(SL):
                        act.wait_ge(s.acc_free, u.slices(k + 1))
                        a.activation(work[:, 1, o:o + n], work[:, 0, o:o + n], ACT.Sigmoid).then_inc(s.sg_ready, 1)
                    u = at.after(2 * t + 1, 2 * t + 1)
                    convert(u)
                    for k, (o, n) in enumerate(SL):
                        act.wait_ge(s.acc_free, u.slices(k + 1))
                        a.activation(HH[i % 2][:, t, o:o + n], work[:, 3, o:o + n], ACT.Copy).then_inc(s.hh_ready, 1)

            def ffn(base, l, L):
                q = 6 * FB * l
                up_ffn(base, 0, q)
                with act.Fori(0, ffn_turns // 2) as i:
                    at = At(base.u + 4, base.t + 4, i, FFN_DU, FFN_DT)
                    for e in range(2):
                        up_ffn(at.after(6 * e, 12 * e), 1 + e, i * 12 + (q + 6 + 6 * e))
                        down(at.after(6 * e + 4, 12 * e + 4))
                down(base.after(6 * FB - 2, 12 * FB - 8), L)

            def up_conv(at, i):
                for t in range(2):
                    for j in range(3):
                        convert(at.after(3 * t + j, 3 * t + j))
                    u = at.after(3 * t + 2, 3 * t + 2)
                    for k, (o, n) in enumerate(SL):
                        act.wait_ge(s.acc_free, u.slices(k + 1))
                        a.activation(HH[i % 2][:, t, o:o + n], work[:, 2, o:o + n], ACT.Copy).then_inc(s.chh_ready, 1)

            for j in range(RING):
                act.wait_ge(c_st[j], 16 * TURNS * H)
            act.wait_ge(s.cp_st, 16 * H)
            ffn(F0_AT, 0, 2)
            up_conv(C_AT, 0)
            for i in range(CB):
                if i + 1 < CB:
                    up_conv(C_AT.after(6 + 8 * i, 6 + 14 * i), i + 1)
                    down(C_AT.after(12 + 8 * i, 12 + 14 * i))
                else:
                    down(C_AT.after(8 * CB - 2, 14 * CB - 8), 3)
            ffn(F1_AT, 1, 4)

            act.wait_ge(s.so_st, 64)
            for c in range(0, NT, 2):
                n = ntok(c)
                act.wait_ge(s.rcol_ready, 5 + c // 3)
                act.wait_ge(s.fin_full, c + 1)
                b = PAIR[c % 3]
                dst = workf[:, c * D:(c + 1) * D] if c < NC else rb[:, 0:D]
                a.activation(dst[0:n, :].rearrange("p (a n) -> p a n", a=2), acc[0:n, b:b + 2, :], ACT.Copy,
                             scale=rcol[0:n, c:c + 1]).then_inc(s.ya_ready, 1)

        @block.vector
        def _(dve):
            v = nc.vector

            def convert(at):
                nx = at.after(1, 0)
                if nx.u >= UNITS:
                    return
                dve.wait_ge(s.w_hi, nx.units(1))
                j = nx.slot()
                v.tensor_tensor(wl[:, j, :], stage[:, j, :], wh[:, j, :].bitcast(F32), ALU.subtract).then_inc(s.w_lo, 1)

            def low(L, i):
                j, span = piece_span(L, i)
                if L < 4:
                    dve.wait_ge(s.xh_ready, pieces_before(L, i) + 1)
                    v.scalar_tensor_tensor(out=xl[:, j, span], in0=xT[:, j, span], scalar=gain(LAYER_GAIN[L], j),
                                           in1=xh[:, j, span].bitcast(F32), op0=ALU.mult, op1=ALU.subtract).then_inc(s.x_ready, 1)
                else:
                    dve.wait_ge(s.sq_ready, pieces_before(L, i) + 1)
                    v.tensor_scalar(xT[:, j, span], xT[:, j, span], gain(4, j), None, ALU.mult).then_inc(s.x_ready, 1)

            def mean_square(L):
                dve.wait_ge(s.st_full, L + 1)
                v.tensor_scalar(v9[:, 0:NC], pA[:, 0:NC], 1.0 / D, EPS, ALU.mult, ALU.add).then_inc(s.v9_ready, 1)
                v.tensor_scalar(v9[0:TS, NC:NT], pA[0:TS, NC:NT], 1.0 / D, EPS, ALU.mult, ALU.add).then_inc(s.v9_ready, 1)

            def rms_rows(L):
                for n, (bank, o, w) in enumerate(((pA, 0, 512), (pB, 512, 512), (pA, 1024, TS))):
                    dve.wait_ge(s.rb_full, 3 * L + n + 1)
                    v.tensor_copy(rb[:, o:o + w], bank[:, 0:w]).then_inc(s.rb_free, 1)
                dve.wait_ge(s.rb_free, 3 * L + 3)

            def bank(at, k):
                return acc[:, 3 * (at.t % 2) + k, 0:SL[k][1]]

            def sum_piece(L, i):
                _, span = piece_span(L, i)
                before = sums_before(L, i, True)
                dve.wait_ge(s.sq_ready, pieces_before(L, i) + 1)
                if L > 0:
                    dve.wait_ge(s.ssq_ready, sums_before(L, 4))
                if before > 0:
                    dve.wait_ge(s.ssqv_ready, before)
                v.tensor_tensor(ssq[:, span], ssq[:, span], square_at(L, i), ALU.add).then_inc(s.ssqv_ready, 1)

            def refresh(L, i):
                low(L, i)
                if L > 0 and by_vector(L, PIECES[L][i][1]):
                    sum_piece(L, i)

            def bank_in_turn(at, m):
                return acc[:, (3 * (at.t % 2) + m) % 6, :]

            def down(at, L=None, hook=None, first_hook=None):
                late = None
                for half in range(2):
                    u = at.after(half, 4 * half)
                    convert(u)
                    for m in range(12):
                        j, k = (4 * half + m % 4, m // 4) if by_slices(L, half) else (4 * half + m // 3, m % 3)
                        o, n = SL[k]
                        dve.wait_ge(s.acc_full, u.slices(m + 1))
                        v.tensor_tensor(xT[:, j, o:o + n], xT[:, j, o:o + n], bank_in_turn(u, m)[:, 0:n], ALU.add).then_inc(s.acc_free, 1)
                        if L is None or (not by_slices(L, half) and k < 2):
                            continue
                        if late is not None:
                            refresh(L, late)
                        late = half * (len(PIECES[L]) - 12) + (m if by_slices(L, half) else j)
                        if first_hook and not half and m == 3:
                            first_hook()
                        if hook and half and m % 4 == 3 and k < 2:
                            refresh(L, late)
                            late = None
                            if k == 1:
                                hook(0)
                if L is not None:
                    refresh(L, late)

            v.memset(stage[:, 0, :], 0.0).then_inc(s.gate_zero, 1)
            v.memset(cols[:], 0.0).then_inc(s.row_link, 1)

            def from_psum(k):
                for c in range(3 * k, 3 * k + 3):
                    dve.wait_ge(s.xt_full, c + 1)
                    b = X_PAIR[c]
                    src = acc[:, b:b + 2, :].rearrange("p a (k n) -> p (a k) n", n=P) if c < NC else \
                        pB[:, :].rearrange("p (k n) -> p k n", n=TS)
                    v.tensor_copy(xT[:, :, tok(c)], src).then_inc(s.xt_free, 1)

            from_psum(0)
            dve.wait_ge(s.vecT_full, 1)
            v.tensor_copy(vecs[:], pA[:, 0:NV * KD]).then_inc(s.vec_ready, 1)
            dve.wait_ge(s.w_hi, 1)
            v.tensor_tensor(wl[:, 0, :], stage[:, 0, :], wh[:, 0, :].bitcast(F32), ALU.subtract).then_inc(s.w_lo, 1)
            from_psum(1)
            for k in range(3):
                for i in range(KD * k, KD * (k + 1)):
                    low(0, i)
                if k == 0:
                    from_psum(2)
                    dve.wait_ge(s.nT_full, 1)
                    v.tensor_copy(nT_all[:, :, :, :].rearrange("p b h t -> p (b h t)"), pA[:, 0:64])
            convert(G_AT)
            for i in range(2 * KD + 1, 3 * KD):
                sum_piece(0, i)
            convert(M_AT)
            mean_square(0)
            rms_rows(0)
            for k, (o, n) in enumerate(SL):
                dve.wait_ge(s.acc_full, k + 1)
                v.tensor_tensor(rows[0:36, 0, o:o + n], bank(G_AT, k)[0:36, :], rb[0:36, o:o + n], ALU.mult).then_inc(s.acc_free, 1)

            R = lambda k, p=0: rows[p:p + H, k, :]
            done = [1]

            def link(ins):
                done[0] += 1
                ins.then_inc(s.row_link, 1)
                dve.wait_ge(s.row_link, done[0])

            def starts(r):
                return (r[:, 0:SEQ].rearrange("p (c l) -> p c l", l=P)[:, :, 0:1].rearrange("p c l -> p (c l)"),
                        r[:, SEQ:T].rearrange("p (c l) -> p c l", l=DS)[:, :, 0:1].rearrange("p c l -> p (c l)"))

            def ends(r):
                return (r[:, 0:SEQ].rearrange("p (c l) -> p c l", l=P)[:, :, P - 1:P].rearrange("p c l -> p (c l)"),
                        r[:, SEQ:T].rearrange("p (c l) -> p c l", l=DS)[:, :, DS - 1:DS].rearrange("p c l -> p (c l)"))

            def chunks(r):
                return (r[:, 0:SEQ].rearrange("p (c l) -> p c l", l=P), r[:, SEQ:T].rearrange("p (c l) -> p c l", l=DS))

            def spread(m):
                return (m[:, 0:NC].rearrange("p (c l) -> p c l", l=1).to_broadcast([H, NC, P]),
                        m[:, NC:2 * NC].rearrange("p (c l) -> p c l", l=1).to_broadcast([H, DB, DS]))

            halves = (slice(0, NC), slice(NC, 2 * NC))
            M_IN, B_L, U_MAX, BU, M_L, M_DIFF, A_, M_OUT = range(8)

            def rows_gates():
                dve.wait_ge(s.m_ld, 48)
                dve.wait_ge(s.acc_free, 3)
                link(v.tensor_scalar(R(1), R(0), bcol[0:H, :], None, ALU.add))
                link(v.tensor_scalar(R(2), R(0, 32), bcol[32:32 + H, :], None, ALU.add))
                v.scalar_tensor_tensor(out=R(3), in0=R(2), scalar=-1.0, in1=R(2), op0=ALU.mult, op1=ALU.max).then_inc(s.row_full, 1)

            def rows_cumsum():
                dve.wait_ge(s.row_act, 2)
                link(v.tensor_scalar(R(2), R(2), 0.0, None, ALU.min))
                link(v.tensor_tensor(R(4), R(2), R(3), ALU.subtract))
                link(v.memset(R(0), 1.0))
                for part in starts(R(0)):
                    link(v.memset(part, 0.0))
                link(v.tensor_tensor_scan(R(2), R(0), R(4), 0.0, ALU.mult, ALU.add))
                link(v.memset(rows[:, 7, :], 0.0))
                link(v.tensor_tensor(R(7), R(1), R(2), ALU.subtract))

            def rows_starts():
                for part, src in zip(halves, ends(R(2))):
                    link(v.tensor_copy(sm[:, B_L, part], src))
                link(v.tensor_reduce(sm[:, U_MAX, 0:NC], chunks(R(7))[0], AX.X, ALU.max))
                link(v.tensor_tensor(sm[:, BU, 0:NC], sm[:, B_L, 0:NC], sm[:, U_MAX, 0:NC], ALU.add))
                link(v.memset(sm[:, M_IN, 0:1], 0.0))
                link(v.tensor_tensor_scan(sm[:, M_IN, 1:NC], sm[:, B_L, 0:NC - 1], sm[:, BU, 0:NC - 1], 0.0, ALU.add, ALU.max))

            def rows_max():
                link(v.tensor_copy(R(3), R(7)))
                for part, at in zip(halves, starts(R(3))):
                    link(v.tensor_tensor(at, at, sm[:, M_IN, part], ALU.max))
                link(v.memset(R(0), BIG))
                for part in starts(R(0)):
                    link(v.memset(part, -BIG))
                link(v.tensor_tensor_scan(R(1), R(0), R(3), 0.0, ALU.min, ALU.max))

            def rows_scan():
                rows_starts()
                rows_max()

            def rows_args():
                parts = list(zip(spread(sm[:, M_IN, :]), chunks(R(1)), chunks(R(3))))
                link(v.tensor_tensor(parts[0][2], parts[0][0], parts[0][1], ALU.subtract))
                v.tensor_tensor(parts[1][2], parts[1][0], parts[1][1], ALU.subtract).then_inc(s.row_full, 1)
                v.tensor_tensor(R(0), R(2), R(1), ALU.add).then_inc(s.row_full, 1)
                for part, src in zip(halves, ends(R(1))):
                    link(v.tensor_copy(sm[:, M_L, part], src))
                link(v.tensor_tensor(sm[:, M_DIFF, :], sm[:, M_IN, :], sm[:, M_L, :], ALU.subtract))
                parts = list(zip(chunks(R(7)), spread(sm[:, M_L, :]), chunks(R(5))))
                link(v.tensor_tensor(parts[0][2], parts[0][0], parts[0][1], ALU.subtract))
                v.tensor_tensor(parts[1][2], parts[1][0], parts[1][1], ALU.subtract).then_inc(s.row_full, 1)
                link(v.tensor_scalar(R(4), R(1), -1.0, None, ALU.mult))
                v.tensor_tensor(sm[:, M_OUT, :], sm[:, B_L, :], sm[:, M_L, :], ALU.add).then_inc(s.row_ready, 1)

            def cols_first():
                for n, bk in enumerate((pA, pB)):
                    dve.wait_ge(s.rowT_full, n + 1)
                    for c in range(4):
                        src = bk[:, c * P:(c + 1) * P].rearrange("p (k h) -> p h k", h=32)[:, 0:H, :]
                        last = v.tensor_copy(cols[:, :, 4 * n + c, 0:4], src)
                    last.then_inc(s.cols_ready, 1)

            def cols_last():
                dve.wait_ge(s.rowT_full, 3)
                src = pA[0:TS, 0:P].rearrange("p (k h) -> p h k", h=32)[:, 0:H, :]
                v.tensor_copy(cols[0:TS, :, NC, 0:4], src)
                src = pA[:, P:P + 4 * NT].rearrange("p (c h) -> p h c", h=H)
                v.tensor_copy(cols[:, :, 0:NC, M_:M_ + 1].rearrange("p h c a -> p h (c a)"), src[:, :, 0:NC])
                v.tensor_copy(cols[0:TS, :, NC, M_:M_ + 1].rearrange("p h a -> p (h a)"), pA[0:TS, P + 4 * NC:P + 4 * NT])
                v.tensor_copy(abc[:, :, :].rearrange("p h c -> p (h c)"), pA[:, 256:256 + 2 * NC * H]).then_inc(s.cols_ready, 1)
                dve.wait_ge(s.m_st, 32)
                dve.wait_ge(s.cols_ready, 3)
                pick_head(0)

            def up_head(at, hooks, starts):
                for j in range(6):
                    u = at.after(j, j)
                    if j > 0 or at is not M_AT:
                        convert(u)
                    if j in starts:
                        starts[j]()
                    for k, (o, n) in enumerate(SL):
                        dve.wait_ge(s.acc_full, u.slices(k + 1))
                        if j < 2:
                            last = v.scalar_tensor_tensor(out=work[:, j, o:o + n], in0=bank(u, k), scalar=DK ** -0.5,
                                                          in1=rb[:, o:o + n], op0=ALU.mult, op1=ALU.mult)
                        else:
                            last = v.tensor_tensor(work[:, j, o:o + n], bank(u, k), rb[:, o:o + n], ALU.mult)
                        last.then_inc(s.acc_free, 1)
                    if j in hooks:
                        hooks[j]()

            def pick_head(h):
                hs = slice(h, h + 1) if isinstance(h, int) else bass.ds(h, 1)
                v.tensor_copy(cc[:], cols[:, hs].rearrange("p a c k -> p (a c) k"))
                v.tensor_copy(ca[:], abc[:, hs].rearrange("p a c -> p (a c)"))
                v.tensor_copy(cn[:], nT_all[:, :, hs, :].rearrange("p b a t -> p (a t) b"))
                v.tensor_copy(cg[:], vecs[:, bass.ds(h * 2 + 5 * KD, 2)])
                v.memset(kvc[:, 2 * DK:2 * DK + 1], 1.0)
                v.memset(kvs[:, 2 * DK:2 * DK + 1], 1.0)
                v.memset(CT[:], 0.0).then_inc(s.cur_ready, 1)

            def mix(at, h, before):
                st, hc = h * NT, h * NC

                def drain(c, p):
                    f = filler(at, before, c, p)
                    if f is None or f[4] == 0:
                        return
                    u, j, e, k, _ = f
                    o, n = SL[k]
                    dve.wait_ge(s.acc_full, u.slices(k + 1))
                    if j is not None:
                        v.tensor_tensor(xT[:, j, o:o + n], xT[:, j, o:o + n], acc[:, 2, 0:n], ALU.add).then_inc(s.acc_free, 1)
                    else:
                        v.tensor_tensor(work[:, 6 + e, o:o + n], acc[:, 2, 0:n], rb[:, o:o + n], ALU.mult).then_inc(s.acc_free, 1)

                hs = slice(h, h + 1) if isinstance(h, int) else bass.ds(h, 1)
                dve.wait_ge(s.cur_ready, h + 1)
                dve.wait_ge(s.kv_ready, st + 1)
                v.tensor_scalar(wgm[:], blocksel[:], cc[0:TS, NC, G_:G_ + 1], None, ALU.mult).then_inc(s.wgm_ready, 1)

                def scores(c):
                    n = ntok(c)
                    dve.wait_ge(s.qk_full, st + (c + 1))
                    dve.wait_ge(s.dx_ready, st + (c + 1))
                    v.tensor_tensor(dx[0:n, 0:n], acc[0:n, 3, P:P + n], dx[0:n, 0:n], ALU.mult).then_inc(s.sd_ready, 1)

                def weigh(c):
                    dve.wait_ge(s.kv_ready, st + (c + 2))
                    if c >= 1:
                        dve.wait_ge(s.up_full, hc + c)
                    v.tensor_scalar(wgv[:], kvc[:, DK:2 * DK + 1], cc[:, c, G_:G_ + 1], None, ALU.mult).then_inc(s.wgv_ready, 1)

                drain(0, 0)
                weigh(0)
                drain(0, 1)
                scores(0)
                for c in range(NT):
                    n = ntok(c)
                    if c < NC:
                        if c > 0:
                            drain(c, 0)
                        dve.wait_ge(s.up_full, hc + (c + 1))
                        for out, change in ((CT[:, 0, :], acc[:, 5, 0:DK + 1]), (CT[:, 1, 0:DK - 1], acc[:, 5, DK + 1:2 * DK]),
                                            (CT[:, 1, DK - 1:DK + 1], acc[:, 1, 300:302])):
                            last = v.scalar_tensor_tensor(out=out, in0=out, scalar=ca[:, c:c + 1], in1=change, op0=ALU.mult, op1=ALU.add)
                        last.then_inc(s.ct_ready, 1)
                        if c > 0:
                            drain(c, 1)
                    dve.wait_ge(s.ia_full, st + (c + 1))
                    dve.wait_ge(s.t1_ready, st + (c + 1))
                    if c == NC:
                        v.scalar_tensor_tensor(out=qd[:], in0=acc[0:TS, 1, 340:340 + DB], scalar=1.0, in1=blocksel[:],
                                               op0=ALU.mult, op1=ALU.mult, accum_out=sc[0:TS, 6:7]).then_inc(s.smp_link, 1)
                        dve.wait_ge(s.smp_link, h * 3 + 1)
                        v.tensor_tensor(t1[0:TS, DK:DK + 1], sc[0:TS, 6:7], cc[0:TS, NC, W_:W_ + 1], ALU.mult).then_inc(s.smp_link, 1)
                        v.tensor_tensor(nn[:], cn[:], ca[:, NC:2 * NC].rearrange("p (a b) -> p a b", a=1).to_broadcast([P, 2, DB]),
                                        ALU.mult).then_inc(s.smp_link, 1)
                        dve.wait_ge(s.smp_link, h * 3 + 3)
                        v.tensor_tensor(nT_all[:, :, hs, :].rearrange("p b a t -> p (a t) b"), nn[:],
                                        acc[:, 1, 320:336].rearrange("p (t b) -> p t b", t=2), ALU.add)
                    if c >= 1:
                        dve.wait_ge(s.ht_full, st + c)
                    v.tensor_tensor(num[0:n, :], acc[0:n, 1, 0:DK + 1], t1[0:n, :], ALU.add).then_inc(s.num_ready, 1)
                    if c < NC:
                        drain(c, 2)
                        if c + 1 < NC:
                            weigh(c + 1)
                        drain(c, 3)
                        scores(c + 1)
                        if filler_unit(at, before, c):
                            convert(filler_unit(at, before, c))
                        dve.wait_ge(s.upb_full, hc + (c + 1))
                        cr = cring[:, c % RING].rearrange("p t k -> p (t k)")
                        v.scalar_tensor_tensor(out=cr, in0=cr, scalar=ca[:, NC + c:NC + c + 1], in1=acc[:, 5, :],
                                               op0=ALU.mult, op1=ALU.add).then_inc(s.cb_ready, 1)
                        drain(c, 4)
                        dve.wait_ge(s.iv_full, hc + (c + 1))
                        v.tensor_copy(ivs[:, :, c * DS:(c + 1) * DS], pA[:, 0:2 * DS].rearrange("p (t s) -> p t s", t=2)).then_inc(s.iv_free, 1)
                        drain(c, 5)
                    dve.wait_ge(s.num_ready, st + (c + 1))
                    den = num[0:n, DK:DK + 1]
                    v.scalar_tensor_tensor(out=sc[0:n, 1:2], in0=den, scalar=-1.0, in1=den, op0=ALU.mult, op1=ALU.max).then_inc(s.den_link, 1)
                    dve.wait_ge(s.den_link, h * (4 * NT) + (4 * c + 1))
                    v.tensor_scalar(sc[0:n, 1:2], sc[0:n, 1:2], cc[0:n, c, T_:T_ + 1], None, ALU.max).then_inc(s.den_link, 1)
                    dve.wait_ge(s.den_link, h * (4 * NT) + (4 * c + 2))
                    v.reciprocal(sc[0:n, 2:3], sc[0:n, 1:2]).then_inc(s.den_link, 1)
                    dve.wait_ge(s.den_link, h * (4 * NT) + (4 * c + 3))
                    if c == NC:
                        gate(h, 0)
                    dve.wait_ge(s.ss_ready, st + (c + 1))
                    v.tensor_scalar(sc[0:n, 7:8], sc[0:n, 0:1], 1.0 / DK, sc[0:n, 2:3], ALU.mult, ALU.mult).then_inc(s.den_link, 1)
                    dve.wait_ge(s.den_link, h * (4 * NT) + (4 * c + 4))
                    v.tensor_scalar(sc[0:n, 3:4], sc[0:n, 7:8], sc[0:n, 2:3], EPS, ALU.mult, ALU.add).then_inc(s.ms_ready, 1)
                    if c >= 1:
                        tail(h, c - 1)
                    dve.wait_ge(s.rs0_ready, st + (c + 1))
                    v.tensor_tensor(sc[0:n, 5:6], sc[0:n, 4:5], sc[0:n, 2:3], ALU.mult).then_inc(s.rs_ready, 1)

            def tail(h, c):
                dve.wait_ge(s.ht_full, h * NT + (c + 1))
                v.tensor_copy(work[:, 0:2, tok(c)], pB[:, 0:2 * P].rearrange("p (e n) -> p e n", e=2)[:, :, 0:ntok(c)]).then_inc(s.ho_ready, 1)

            def gate(h, k):
                o, n = SL[k]
                dve.wait_ge(s.ho_ready, h * NT + 3 * (k + 1))
                dve.wait_ge(s.so_ready, h * 3 + (k + 1))
                for e in range(2):
                    last = v.scalar_tensor_tensor(out=work[:, e, o:o + n], in0=work[:, e, o:o + n], scalar=cg[:, e:e + 1],
                                                  in1=work[:, 6 + e, o:o + n], op0=ALU.mult, op1=ALU.mult)
                last.then_inc(s.hg_ready, 1)

            def gated_low(h, k):
                o, n = SL[k]
                dve.wait_ge(s.hhm_ready, h * 3 + (k + 1))
                v.tensor_tensor(hl0[:, :, o:o + n], work[:, 0:2, o:o + n], hh0[:, :, o:o + n].bitcast(F32), ALU.subtract).then_inc(s.hlm_ready, 1)

            def gate_start(h):
                gated_low(h, 0)
                gate(h, 1)
                gated_low(h, 1)

            def gate_end(h):
                tail(h, NT - 1)
                gate(h, 2)
                gated_low(h, 2)
                dve.wait_ge(s.hlm_ready, h * 3 + 3)
                dve.wait_ge(s.ot_full, h + 1)
                v.tensor_copy(ct0[:], pA[:, :].rearrange("p (a v) -> p a v", a=2)).then_inc(s.cp_ready, 1)
                hs = slice(h, h + 1) if isinstance(h, int) else bass.ds(h, 1)
                v.tensor_copy(ncol[:, hs, :].rearrange("p a t -> p (a t)"), CT[:, :, DK:DK + 1].rearrange("p t a -> p (t a)"))

            up_head(M_AT, {1: rows_cumsum, 2: rows_scan, 3: rows_args, 4: cols_first},
                    {0: rows_gates, 5: cols_last})
            mix(M_AT.after(6, 6), 0, False)
            with dve.Fori(0, H - 1) as h:
                at = At(M_AT.u + 8, M_AT.t + 8, h, HEAD_DU, HEAD_DT)
                up_head(at, {4: lambda: pick_head(h + 1)}, {0: lambda: (gate_start(h), gate_end(h))})
                mix(at.after(6, 6), h + 1, True)
            gate_start(H - 1)
            down(M_AT.after(38, 56), 1, first_hook=lambda: gate_end(H - 1))

            def norm(L, first):
                convert(first)
                mean_square(L)
                rms_rows(L)

            def up_ffn(at, i, q):
                for t in range(2):
                    u = at.after(2 * t, 2 * t)
                    if i > 0 or t > 0:
                        convert(u)
                    for k, (o, n) in enumerate(SL):
                        c0 = q + (3 * t + k + 1)
                        dve.wait_ge(s.acc_full, u.slices(k + 1))
                        v.tensor_tensor(work[:, 0, o:o + n], bank(u, k), rb[:, o:o + n], ALU.mult).then_inc(s.acc_free, 1)
                        dve.wait_ge(s.acc_free, u.slices(k + 1))
                        v.tensor_tensor(work[:, 2, o:o + n], work[:, 0, o:o + n], rb[:, o:o + n], ALU.mult).then_inc(s.g2_ready, 1)
                        dve.wait_ge(s.g2_ready, c0)
                        dve.wait_ge(s.sg_ready, c0)
                        v.tensor_tensor(work[:, 2, o:o + n], work[:, 2, o:o + n], work[:, 1, o:o + n], ALU.mult).then_inc(s.g3_ready, 1)
                    u = at.after(2 * t + 1, 2 * t + 1)
                    convert(u)
                    for k, (o, n) in enumerate(SL):
                        c0 = q + (3 * t + k + 1)
                        dve.wait_ge(s.acc_full, u.slices(k + 1))
                        dve.wait_ge(s.g3_ready, c0)
                        v.tensor_tensor(work[:, 3, o:o + n], bank(u, k), work[:, 2, o:o + n], ALU.mult).then_inc(s.acc_free, 1)
                        dve.wait_ge(s.acc_free, u.slices(k + 1))
                        dve.wait_ge(s.hh_ready, c0)
                        v.tensor_tensor(HL[i % 2][:, t, o:o + n], work[:, 3, o:o + n], HH[i % 2][:, t, o:o + n].bitcast(F32),
                                        ALU.subtract).then_inc(s.hl_ready, 1)

            def ffn(base, l, L, hook=None, last_hook=None):
                q = 6 * FB * l
                norm(L - 1, base)
                up_ffn(base, 0, q)
                if hook:
                    hook()
                with dve.Fori(0, ffn_turns // 2) as i:
                    at = At(base.u + 4, base.t + 4, i, FFN_DU, FFN_DT)
                    for e in range(2):
                        up_ffn(at.after(6 * e, 12 * e), 1 + e, i * 12 + (q + 6 + 6 * e))
                        down(at.after(6 * e + 4, 12 * e + 4))
                down(base.after(6 * FB - 2, 12 * FB - 8), L, last_hook)

            ffn(F0_AT, 0, 2)

            dve.wait_ge(s.cs_full, 1)
            v.tensor_copy(cstT.rearrange("p b r k -> p (b r k)"), pB[:, 0:P]).then_inc(s.cs_ready, 1)
            v.memset(ub[:, 0:2], 0.0)
            dve.wait_ge(s.cs_ready, 1)
            ncv = [0]

            def clink(ins):
                ncv[0] += 1
                ins.then_inc(s.cv_link, 1)
                dve.wait_ge(s.cv_link, ncv[0])

            def up_conv(at, i):
                for t in range(2):
                    ct = 2 * i + t
                    tap = lambda r: gain(6 + r, ct)
                    u = at.after(3 * t, 3 * t)
                    if i > 0 or t > 0:
                        convert(u)
                    for k, (o, n) in enumerate(SL):
                        dve.wait_ge(s.acc_full, u.slices(k + 1))
                        v.tensor_tensor(work[:, 0, o:o + n], bank(u, k), rb[:, o:o + n], ALU.mult).then_inc(s.acc_free, 1)
                        dve.wait_ge(s.acc_free, u.slices(k + 1))
                        clink(v.tensor_tensor(work[:, 0, o:o + n], work[:, 0, o:o + n], rb[:, o:o + n], ALU.mult))
                    u = at.after(3 * t + 1, 3 * t + 1)
                    convert(u)
                    clink(v.tensor_copy(us[:, :, 0:2], cstT[:, :, :, ct:ct + 1].rearrange("p b r a -> p b (r a)")))
                    for k, (o, n) in enumerate(SL):
                        dve.wait_ge(s.acc_full, u.slices(k + 1))
                        w = min(n, SEQ - o)
                        if w < n:
                            v.tensor_tensor(us[:, :, 2:2 + DS], bank(u, k)[:, w:n].rearrange("p (b s) -> p b s", b=DB),
                                            work[:, 0, SEQ:T].rearrange("p (b s) -> p b s", b=DB), ALU.mult)
                        v.tensor_tensor(ub[:, 2 + o:2 + o + w], bank(u, k)[:, 0:w], work[:, 0, o:o + w], ALU.mult).then_inc(s.acc_free, 1)
                    dve.wait_ge(s.acc_free, u.slices(3))
                    v.tensor_copy(cpo[:, :, ct:ct + 1].rearrange("p r a -> p (r a)"), ub[:, SEQ:SEQ + 2])
                    v.tensor_copy(cso[:, :, :, ct:ct + 1].rearrange("p b r a -> p b (r a)"), us[:, :, DS:DS + 2])
                    cv = work[:, 1, 0:SEQ]
                    cvs = work[:, 1, SEQ:T].rearrange("p (b s) -> p b s", b=DB)
                    v.tensor_scalar(cv, ub[:, 0:SEQ], tap(0), None, ALU.mult)
                    clink(v.tensor_scalar(cvs, us[:, :, 0:DS], tap(0), None, ALU.mult))
                    for r in (1, 2):
                        v.scalar_tensor_tensor(out=cv, in0=ub[:, r:r + SEQ], scalar=tap(r), in1=cv, op0=ALU.mult, op1=ALU.add)
                        clink(v.scalar_tensor_tensor(out=cvs, in0=us[:, :, r:r + DS], scalar=tap(r), in1=cvs, op0=ALU.mult, op1=ALU.add))
                    clink(v.tensor_tensor(work[:, 1, :], work[:, 1, :], rb[:], ALU.mult))
                    u = at.after(3 * t + 2, 3 * t + 2)
                    convert(u)
                    for k, (o, n) in enumerate(SL):
                        dve.wait_ge(s.acc_full, u.slices(k + 1))
                        v.tensor_tensor(work[:, 2, o:o + n], bank(u, k), work[:, 1, o:o + n], ALU.mult).then_inc(s.acc_free, 1)
                        dve.wait_ge(s.acc_free, u.slices(k + 1))
                        dve.wait_ge(s.chh_ready, 6 * i + 3 * t + k + 1)
                        v.tensor_tensor(HL[i % 2][:, t, o:o + n], work[:, 2, o:o + n], HH[i % 2][:, t, o:o + n].bitcast(F32),
                                        ALU.subtract).then_inc(s.chl_ready, 1)

            norm(2, C_AT)
            up_conv(C_AT, 0)
            for i in range(CB):
                if i + 1 < CB:
                    up_conv(C_AT.after(6 + 8 * i, 6 + 14 * i), i + 1)
                    down(C_AT.after(12 + 8 * i, 12 + 14 * i))
                else:
                    down(C_AT.after(8 * CB - 2, 14 * CB - 8), 3)

            def small_out():
                dve.wait_ge(s.so_full, 1)
                for n, p in enumerate((64, 8, P, 16)):
                    v.tensor_copy(outv[0:p, n, :], pA[0:p, n * P:(n + 1) * P]).then_inc(s.so_evict, 1)

            def last_mean_square(k):
                dve.wait_ge(s.st_full, 5 + k)
                whole = min(3 * k + 3, NC)
                v.tensor_scalar(v9[:, 3 * k:whole], pA[:, 3 * k:whole], 1.0 / D, EPS, ALU.mult, ALU.add).then_inc(s.v9_ready, 1)
                if whole < 3 * k + 3:
                    v.tensor_scalar(v9[0:TS, NC:NT], pA[0:TS, NC:NT], 1.0 / D, EPS, ALU.mult, ALU.add).then_inc(s.v9_ready, 1)

            ffn(F1_AT, 1, 4, small_out, last_mean_square)
            last_mean_square(1)
            dve.wait_ge(s.so_st, 64)
            for c in range(1, NT, 2):
                if c == 5:
                    last_mean_square(2)
                dve.wait_ge(s.rcol_ready, 5 + c // 3)
                dve.wait_ge(s.fin_full, c + 1)
                b = PAIR[c % 3]
                v.tensor_scalar(workf[:, c * D:(c + 1) * D].rearrange("p (a n) -> p a n", a=2), acc[:, b:b + 2, :],
                                rcol[:, c:c + 1], None, ALU.mult).then_inc(s.yd_ready, 1)

        @block.tensor
        def _(pe):
            mm = nc.tensor.matmul

            def flip(out, in_, n):
                k = in_.shape[0]
                if n == P:
                    return nc.tensor.transpose(out, in_, ident[0:k, 0:k])
                return mm(out, in_, ident[0:k, 0:k], start=True, stop=True)

            def three(out, ah, al, bh, bl, first, last):
                mm(out, ah, bh, start=first, stop=False)
                mm(out, ah, bl, start=False, stop=False)
                return mm(out, al, bh, start=False, stop=last)

            def bank(at, k):
                return acc[:, 3 * (at.t % 2) + k, 0:SL[k][1]]

            def free(at, k):
                if at.t >= 2:
                    pe.wait_ge(s.acc_free, at.slices(k - 5))

            def up(at, L=None, hooks={}):
                pe.wait_ge(s.w_lo, at.units(1))
                j = at.slot()
                for k, (o, n) in enumerate(SL):
                    free(at, k)
                    for kk in range(KD):
                        if L is not None:
                            pe.wait_ge(s.x_ready, piece_count(L, kk, k))
                        ws = slice(kk * P, (kk + 1) * P)
                        last = three(bank(at, k), wh[:, j, ws], wl[:, j, ws], xh[:, kk, o:o + n], xl[:, kk, o:o + n],
                                     kk == 0, kk == KD - 1)
                    last.then_inc(s.acc_full, 1)
                    if k in hooks:
                        hooks[k]()

            def down(at, hh, hl, L=None, wait_slice=None, hook=None, first_hook=None):
                for half in range(2):
                    u = at.after(half, 4 * half)
                    pe.wait_ge(s.w_lo, u.units(1))
                    j = u.slot()
                    for m in range(12):
                        jj, k = (m % 4, m // 4) if by_slices(L, half) else (m // 3, m % 3)
                        o, n = SL[k]
                        out = acc[:, (3 * (u.t % 2) + m) % 6, 0:n]
                        pe.wait_ge(s.acc_free, u.slices(m - 5))
                        if wait_slice and not half and jj == 0:
                            wait_slice(k)
                        for kk in range(2):
                            ws = slice(kk * 512 + jj * P, kk * 512 + (jj + 1) * P)
                            last = three(out, wh[:, j, ws], wl[:, j, ws], hh[:, kk, o:o + n], hl[:, kk, o:o + n], kk == 0, kk == 1)
                        last.then_inc(s.acc_full, 1)
                        if hook and half and jj == 3:
                            hook(k)
                        if first_hook and not half and m == 3:
                            first_hook()

            def square_sums(L):
                pe.wait_ge(s.ssq_ready, sums_before(L, len(PIECES[L])))
                if L == 0:
                    pe.wait_ge(s.ssqv_ready, KD - 1)
                if L == 2:
                    pe.wait_ge(s.cs_ready, 1)
                for c in range(NT):
                    last = mm(pA[0:ntok(c), c:c + 1], ssq[:, tok(c)], ones[:, 0:1], start=True, stop=True)
                last.then_inc(s.st_full, 1)

            def rms_rows(L):
                pe.wait_ge(s.rcol_ready, L + 1)
                for c in range(NT):
                    n = ntok(c)
                    if c == NC:
                        pe.wait_ge(s.rb_free, 3 * L + 1)
                    out = (pA, pB, pA)[c // 4][:, (c % 4) * P:(c % 4) * P + n]
                    last = mm(out, rcol[0:n, c:c + 1].to_broadcast([n, P]), ident[0:n, 0:n], start=True, stop=True)
                    if c % 4 == 3 or c == NC:
                        last.then_inc(s.rb_full, 1)

            pe.wait_ge(s.const_ready, 1)

            def x_transpose(k):
                for c in range(3 * k, 3 * k + 3):
                    pe.wait_ge(x_ld[c], 16)
                    n, b = ntok(c), X_PAIR[c]
                    if 3 <= c < NC:
                        pe.wait_ge(s.xt_free, c - 2 if c < 6 else c - 1)
                    for kk in range(KD):
                        out = acc[:, b + kk // 4, (kk % 4) * P:(kk % 4) * P + n] if c < NC else pB[:, kk * TS:(kk + 1) * TS]
                        last = nc.tensor.transpose(out, xin[c][:, kk * P:(kk + 1) * P], ident[0:n, 0:n])
                    last.then_inc(s.xt_full, 1)

            for k in range(3):
                x_transpose(k)
                if k == 0:
                    pe.wait_ge(s.vec_ld, 80)
                    nc.tensor.transpose(pA[:, 0:NV * KD], rows[0:NV * KD, 7, 0:P], ident[0:NV * KD, 0:NV * KD]).then_inc(s.vecT_full, 1)
            pe.wait_ge(s.n_ld, 16)
            pe.wait_ge(s.vec_ready, 1)
            nc.tensor.transpose(pA[:, 0:64], rows[0:64, 7, P:2 * P], ident[0:64, 0:64]).then_inc(s.nT_full, 1)
            up(G_AT, 0, {1: lambda: pe.wait_ge(s.xt_free, NT)})

            def rows_first():
                pe.wait_ge(s.row_act, 6)
                pe.wait_ge(s.row_ready, 1)
                for n, bk in enumerate((pA, pB)):
                    for c in range(4):
                        last = nc.tensor.transpose(bk[:, c * P:(c + 1) * P], rows[:, 7, tok(4 * n + c)], ident[:])
                    last.then_inc(s.rowT_full, 1)

            def rows_last():
                pe.wait_ge(s.cols_ready, 1)
                mm(pA[0:TS, 0:P], rows[:, 7, tok(NC)], ident[:], start=True, stop=True)
                for c in range(NT):
                    n = ntok(c)
                    mm(pA[0:n, P + 4 * c:P + 4 * c + 4], rows[0:H, 4, tok(c)], ident[0:H, 0:H], start=True, stop=True)
                for h in range(H):
                    last = mm(pA[:, 256 + 2 * NC * h:256 + 2 * NC * (h + 1)], ident[0:H, h:h + 1].to_broadcast([H, P]), sm[:, 6, :],
                              start=True, stop=True)
                last.then_inc(s.rowT_full, 1)

            def up_head(at, hooks={}, tails={}):
                for j in range(6):
                    up(at.after(j, j), None, {k: f for (unit, k), f in tails.items() if unit == j})
                    if j in hooks:
                        hooks[j]()

            def out_rows(h, c):
                n, st = ntok(c), h * NT
                pe.wait_ge(s.hn_ready, st + (c + 1))
                if c >= 1:
                    pe.wait_ge(s.ho_ready, st + c)
                for e in range(2):
                    if n == P:
                        last = nc.tensor.transpose(pB[:, e * P:e * P + n], num[:, e * P:(e + 1) * P], ident[:])
                    else:
                        last = mm(pB[:, e * P:e * P + n], num[0:n, e * P:(e + 1) * P], ident[0:n, 0:n], start=True, stop=True)
                last.then_inc(s.ht_full, 1)

            def mix(at, h, before):
                st, hc = h * NT, h * NC

                def fill(c, p):
                    f = filler(at, before, c, p)
                    if f is None:
                        return
                    u, tile, _, k, part = f
                    (o, n), j = SL[k], u.slot()
                    if k == 0 and (part == 0 if tile is None else tile % 4 == 0):
                        pe.wait_ge(s.w_lo, u.units(1))
                        if tile == 0:
                            pe.wait_ge(s.hlm_ready, h * 3)
                    if part != 1:
                        pe.wait_ge(s.acc_free, u.slices(k))
                    if tile is not None:
                        for kk in range(2):
                            ws = slice(kk * 512 + (tile % 4) * P, kk * 512 + (tile % 4 + 1) * P)
                            last = three(acc[:, 2, 0:n], wh[:, j, ws], wl[:, j, ws], hh0[:, kk, o:o + n], hl0[:, kk, o:o + n],
                                         kk == 0, kk == 1)
                    else:
                        for kk in range(4 * part, 4 * part + 4):
                            ws = slice(kk * P, (kk + 1) * P)
                            last = three(acc[:, 2, 0:n], wh[:, j, ws], wl[:, j, ws], xh[:, kk, o:o + n], xl[:, kk, o:o + n],
                                         kk == 0, kk == KD - 1)
                    if part != 0:
                        last.then_inc(s.acc_full, 1)

                pe.wait_ge(s.acc_free, at.slices(0))
                pe.wait_ge(s.cur_ready, h + 1)

                def key_value(c):
                    if c >= 0:
                        pe.wait_ge(s.kv_ready, st + (c + 1))
                    ts = tok(NC if c < 0 else c)
                    n = TS if c < 0 else P
                    for j in range(4):
                        last = flip(acc[0:n, 4, j * P:(j + 1) * P], work[:, 2 + j, ts], n)
                    last.then_inc(s.kvp_full, 1)

                def prepare(c, between=None):
                    n, ts = ntok(c), tok(c)
                    if c >= 1:
                        pe.wait_ge(s.sd_ready, st + c)
                    mm(acc[0:n, 3, 0:n], cc[:, c, M_:M_ + 1].to_broadcast([P, n]), ident[:, 0:n], start=True, stop=False)
                    mm(acc[0:n, 3, 0:n], identb[0:n, 0:n], causal[:] if c < NC else blockneg[:], start=False, stop=True).then_inc(s.db_full, 1)
                    if c < NC:
                        key_value(c)
                    if between:
                        between()
                    pe.wait_ge(s.dx_ready, st + (c + 1))
                    for e in range(2):
                        last = mm(acc[0:n, 3, P:P + n], work[:, 2 + e, ts], work[:, e, ts], start=e == 0, stop=e == 1)
                    last.then_inc(s.qk_full, 1)

                key_value(-1)
                fill(0, 0)
                prepare(0, lambda: fill(0, 1))
                for c in range(NC):
                    ts = tok(c)
                    if c >= 1:
                        pe.wait_ge(s.ct_ready, hc + c)
                        pe.wait_ge(s.t1_ready, st + c)
                    for e in range(2):
                        last = mm(acc[:, 0, 0:DK + 1], work[:, e, ts], CT[:, e, :], start=e == 0, stop=e == 1)
                    last.then_inc(s.in_full, 1)
                    if c > 0:
                        fill(c, 0)
                    pe.wait_ge(s.sd_ready, st + (c + 1))
                    pe.wait_ge(s.wgv_ready, hc + (c + 1))
                    if c >= 1:
                        pe.wait_ge(s.num_ready, st + c)
                    mm(acc[:, 1, 0:DK + 1], dx[:], kvc[:, DK:2 * DK + 1], start=True, stop=True)
                    last = mm(acc[:, 1, 300:302], kvc[:, P:2 * P], wgv[:, DK - 1:DK + 1], start=True, stop=True)
                    last.then_inc(s.ia_full, 1)
                    if c >= 1:
                        pe.wait_ge(s.cb_ready, hc + c)
                    mm(acc[:, 5, 0:DK + 1], kvc[:, 0:P], wgv[:, 0:DK + 1], start=True, stop=True)
                    last = mm(acc[:, 5, DK + 1:2 * DK], kvc[:, P:2 * P], wgv[:, 0:DK - 1], start=True, stop=True)
                    last.then_inc(s.up_full, 1)
                    if c > 0:
                        fill(c, 1)
                    if c >= 1:
                        out_rows(h, c - 1)
                    pe.wait_ge(c_ld[c % RING], h * (16 * TURNS) + 16 * (c // RING + 1))
                    if c >= 1:
                        pe.wait_ge(s.iv_free, hc + c)
                    for e in range(2):
                        for t in range(2):
                            last = nc.tensor.transpose(pA[:, e * DK + t * P:e * DK + (t + 1) * P], cring[:, c % RING, t, e * P:(e + 1) * P], ident[:])
                    last.then_inc(s.tr_full, 1)
                    fill(c, 2)
                    prepare(c + 1, lambda: fill(c, 3))
                    pe.wait_ge(s.wgvb_ready, hc + (c + 1))
                    pe.wait_ge(s.ct_ready, hc + (c + 1))
                    for t in range(2):
                        last = mm(acc[:, 5, t * DK:(t + 1) * DK], wgvb[:, t * P:(t + 1) * P], kvs[:, 0:DK], start=True, stop=True)
                    last.then_inc(s.upb_full, 1)
                    fill(c, 4)
                    pe.wait_ge(s.ct0_ready, hc + (c + 1))
                    for t in range(2):
                        for e in range(2):
                            last = mm(pA[:, t * DS:(t + 1) * DS], ct0[:, e, t * P:(t + 1) * P], work[:, e, SEQ + c * DS:SEQ + (c + 1) * DS],
                                      start=e == 0, stop=e == 1)
                    last.then_inc(s.iv_full, 1)
                    fill(c, 5)
                c = NC
                pe.wait_ge(s.iv_free, hc + NC)
                pe.wait_ge(s.t1_ready, st + c)
                for t in range(2):
                    last = flip(acc[0:TS, 0, t * P:(t + 1) * P], ivs[:, t, :], TS)
                last.then_inc(s.in_full, 1)
                pe.wait_ge(s.sd_ready, st + (c + 1))
                pe.wait_ge(s.wgm_ready, h + 1)
                pe.wait_ge(s.num_ready, st + c)
                for e in range(2):
                    mm(acc[:, 1, 320 + e * DB:320 + (e + 1) * DB], kvs[:, e * P:(e + 1) * P], wgm[:], start=True, stop=True)
                mm(acc[0:TS, 1, 0:DK + 1], dx[0:TS, 0:TS], kvs[:, DK:2 * DK + 1], start=True, stop=True)
                for e in range(2):
                    last = mm(acc[0:TS, 1, 340:340 + DB], work[:, e, SEQ:T], cn[:, e, :], start=e == 0, stop=e == 1)
                last.then_inc(s.ia_full, 1)
                pe.wait_ge(s.cb_ready, hc + NC)

            def mix_tail(h):
                out_rows(h, NT - 1)
                for t in range(2):
                    for e in range(2):
                        last = nc.tensor.transpose(pA[:, t * DK + e * P:t * DK + (e + 1) * P], CT[:, e, t * P:(t + 1) * P], ident[:])
                last.then_inc(s.ot_full, 1)

            up_head(M_AT, {4: rows_first}, {(0, 1): lambda: square_sums(0), (0, 2): lambda: rms_rows(0), (5, 0): rows_last})
            pe.wait_ge(s.cols_ready, 3)
            mix(M_AT.after(6, 6), 0, False)
            with pe.Fori(0, H - 1) as h:
                at = At(M_AT.u + 8, M_AT.t + 8, h, HEAD_DU, HEAD_DT)
                up_head(at, tails={(0, 0): lambda: out_rows(h, NC - 1), (0, 2): lambda: mix_tail(h)})
                mix(at.after(6, 6), h + 1, True)
            out_rows(H - 1, NC - 1)
            down(M_AT.after(38, 56), hh0, hl0, 1, lambda k: pe.wait_ge(s.hlm_ready, (H - 1) * 3 + k + 1),
                 first_hook=lambda: mix_tail(H - 1))

            def up_ffn(at, L=None):
                for j in range(4):
                    first = L is not None and j == 0
                    up(at.after(j, j), L if first else None,
                       {1: lambda: square_sums(L), 2: lambda: rms_rows(L)} if first else {})

            def ffn(base, l, L, hook=None, last_hook=None):
                q = 6 * FB * l
                up_ffn(base, L)
                if hook:
                    hook()
                with pe.Fori(0, ffn_turns // 2) as i:
                    at = At(base.u + 4, base.t + 4, i, FFN_DU, FFN_DT)
                    for e in range(2):
                        up_ffn(at.after(6 * e, 12 * e))
                        pe.wait_ge(s.hl_ready, i * 12 + (q + 6 + 6 * e))
                        down(at.after(6 * e + 4, 12 * e + 4), HH[e], HL[e])
                pe.wait_ge(s.hl_ready, q + 6 * FB)
                down(base.after(6 * FB - 2, 12 * FB - 8), HH[(FB - 1) % 2], HL[(FB - 1) % 2], L + 1, None, last_hook)

            ffn(F0_AT, 0, 1)
            pe.wait_ge(s.cs_ld, 16)
            nc.tensor.transpose(pB[:, 0:P], outv[:, 0, :], ident[:]).then_inc(s.cs_full, 1)

            def up_conv(at, L=None):
                for j in range(6):
                    first = L is not None and j == 0
                    up(at.after(j, j), L if first else None,
                       {1: lambda: square_sums(L), 2: lambda: rms_rows(L)} if first else {})

            up_conv(C_AT, 2)
            for i in range(CB):
                if i + 1 < CB:
                    up_conv(C_AT.after(6 + 8 * i, 6 + 14 * i))
                pe.wait_ge(s.chl_ready, 6 * (i + 1))
                at = C_AT.after(12 + 8 * i, 12 + 14 * i) if i + 1 < CB else C_AT.after(8 * CB - 2, 14 * CB - 8)
                down(at, HH[i % 2], HL[i % 2], 3 if i + 1 == CB else None)

            def small_out():
                pe.wait_ge(s.rb_free, 12)
                flip(pA[0:64, 0:P], nT_all[:, :, :, :].rearrange("p b h t -> p (b h t)"), 64)
                flip(pA[0:8, P:2 * P], ncol[:, :, :].rearrange("p h t -> p (h t)"), 8)
                flip(pA[:, 2 * P:3 * P], cso.rearrange("p b r k -> p (b r k)"), P)
                flip(pA[0:16, 3 * P:4 * P], cpo.rearrange("p r k -> p (r k)"), 16).then_inc(s.so_full, 1)

            def last_square_sums(k):
                pe.wait_ge(s.ssq_ready, sums_before(4, 4 + 4 * (k + 1)))
                if k == 2:
                    pe.wait_ge(s.ssqv_ready, KD - 1 + 4)
                if k > 0:
                    pe.wait_ge(s.v9_ready, 8 + k)
                for c in range(3 * k, 3 * k + 3):
                    last = mm(pA[0:ntok(c), c:c + 1], ssq[:, tok(c)], ones[:, 0:1], start=True, stop=True)
                last.then_inc(s.st_full, 1)

            ffn(F1_AT, 1, 3, small_out, lambda k: last_square_sums(k - 1) if k else None)
            for c in range(NT):
                n, b = ntok(c), PAIR[c % 3]
                if c == 3:
                    last_square_sums(2)
                if c < 3:
                    pe.wait_ge(s.acc_free, SLICES - (3, 1, 0)[c])
                pe.wait_ge(s.x_ready, piece_count(4, KD - 1, c // 3))
                if c >= 3:
                    pe.wait_ge(s.yd_ready if (c - 3) % 2 else s.ya_ready, (c - 3) // 2 + 1)
                for k in range(KD):
                    last = flip(acc[0:n, b + k // 4, (k % 4) * P:(k % 4 + 1) * P], xT[:, k, tok(c)], n)
                last.then_inc(s.fin_full, 1)


_IN = ["x_prompt", "x_sample", "state_mlstm_C", "state_mlstm_n", "state_mlstm_m", "state_conv", "norm_mix", "norm_ffn",
       "norm_final", "w_mlstm_in", "b_mlstm_gate", "mlstm_head_norm", "w_mlstm_out", "w_conv_in", "w_conv_taps",
       "w_conv_out", "w_ffn_gate_up", "w_ffn_down"]


def kernel(**inputs):
    import numpy as np
    import concourse.bacc as bacc
    from concourse.bass_utils import run_bass_kernel_spmd

    nc = bacc.Bacc("TRN2", target_bir_lowering=False, num_devices=1)
    arrays = {f"in_{n}": np.ascontiguousarray(inputs[n]) for n in _IN}
    args = [nc.dram_tensor(n, a.shape, mybir.dt.from_np(a.dtype), kind="ExternalInput").ap() for n, a in arrays.items()]
    shape = {n: a.shape for n, a in zip(_IN, arrays.values())}
    (B, S, D), (DB, DS, _) = shape["x_prompt"], shape["x_sample"]
    NM, _, H, DV, DK = shape["state_mlstm_C"]
    N2, _, R, _ = shape["state_conv"]
    outs = [(B, S, D), (DB, DS, D), (NM, B, H, DV, DK), (NM, B, H, DK), (NM, B, H), (N2, B, R, D),
            (NM, DB, H, DV, DK), (NM, DB, H, DK), (NM, DB, H), (N2, DB, R, D)]
    for i, o in enumerate(outs):
        args.append(nc.dram_tensor(f"out_{i}", o, F32, kind="ExternalOutput").ap())
    build(nc, *args)
    r = run_bass_kernel_spmd(nc, [arrays], core_ids=[0])
    return tuple(r.results[0][f"out_{i}"] for i in range(len(outs)))
```
